# Optimizing a Trainium2 kernel written in Bass

```python
import math, functools
import jax, jax.numpy as jnp
from jax import lax
import numpy as np

D_MODEL = 1024
BATCH = 1
SEQ = 1024
DEPTH = 1

CTX_LEN = 256
GRID_W = 64
D_MIX = D_MODEL
MLSTM_HEADS = 4
MLSTM_HEAD_DIM = D_MODEL // 8
D_MLSTM = MLSTM_HEADS * MLSTM_HEAD_DIM
FOURIER_GROUPS = 8
FOURIER_GROUP_DIM = (D_MIX - D_MLSTM) // FOURIER_GROUPS
D_FOURIER = FOURIER_GROUPS * FOURIER_GROUP_DIM
N_DIRS = 2
N_GATE_COLS = N_DIRS * 2 * MLSTM_HEADS
D_IN_PROJ = 4 * D_MLSTM + N_GATE_COLS + D_FOURIER
SPLITS = (2 * D_MLSTM, 3 * D_MLSTM, 4 * D_MLSTM, 4 * D_MLSTM + N_GATE_COLS)
CHUNK = 128
CONV_K = 3
N_EXPERTS = 64
TOP_K = 8
D_EXPERT = D_MODEL // 4
ROUTED_SCALE = 2.5
EXPERT_BLOCK = 128
DEEPNORM_ALPHA = (2.0 * DEPTH) ** 0.25
DEEPNORM_BETA = (8.0 * DEPTH) ** -0.25
LN_EPS = 1e-5

kernel_name = "hybrid_mlstm_fourier_moe_diffusion_block"

def layer_norm(x):
    xf = x.astype(jnp.float32)
    mu = xf.mean(-1, keepdims=True)
    var = jnp.mean(jnp.square(xf - mu), -1, keepdims=True)
    return ((xf - mu) * lax.rsqrt(var + LN_EPS)).astype(x.dtype)

def layer_norm_affine(x, gain, bias):
    return (layer_norm(x) * gain + bias).astype(x.dtype)

def modulate(u, shift, scale):
    return u * (1.0 + scale) + shift

def conv_grid(u, w, b, rows):
    bsz, n, ch = u.shape
    img = u.reshape(bsz, rows, GRID_W, ch)
    out = lax.conv_general_dilated(img, w[:, :, None, :], window_strides=(1, 1), padding="SAME",
                                   dimension_numbers=("NHWC", "HWIO", "NHWC"), feature_group_count=ch)
    return out.reshape(bsz, n, ch) + b

def conv_seq(u, w, b):
    ch = u.shape[-1]
    out = lax.conv_general_dilated(u, w[CONV_K // 2][:, None, :], window_strides=(1,), padding="SAME",
                                   dimension_numbers=("NWC", "WIO", "NWC"), feature_group_count=ch)
    return out + b

def split_heads(u):
    bsz, n, _ = u.shape
    return u.astype(jnp.float32).reshape(bsz, n, MLSTM_HEADS, MLSTM_HEAD_DIM).transpose(0, 2, 1, 3)

def zero_states(bsz):
    c0 = jnp.zeros((bsz, MLSTM_HEADS, MLSTM_HEAD_DIM, MLSTM_HEAD_DIM), jnp.float32)
    n0 = jnp.zeros((bsz, MLSTM_HEADS, MLSTM_HEAD_DIM), jnp.float32)
    m0 = jnp.zeros((bsz, MLSTM_HEADS), jnp.float32)
    return ((c0, n0, m0), (c0, n0, m0))

def mlstm_chunkwise(q, k, v, log_i, log_f, state):
    bsz, nh, n, dh = q.shape
    nc = n // CHUNK

    def to_chunks(t):
        return jnp.moveaxis(t.reshape(bsz, nh, nc, CHUNK, *t.shape[3:]), 2, 0)

    tri = jnp.tril(jnp.ones((CHUNK, CHUNK), dtype=bool))

    def step(carry, inp):
        c_prev, n_prev, m_prev = carry
        qc, kc, vc, li, lf = inp
        b = jnp.cumsum(lf, axis=-1)
        log_d = jnp.where(tri, b[..., :, None] - b[..., None, :] + li[..., None, :], -jnp.inf)
        m_t = jnp.maximum(b + m_prev[..., None], log_d.max(-1))
        d = jnp.exp(log_d - m_t[..., None])
        inter = jnp.exp(b + m_prev[..., None] - m_t)
        s = jnp.einsum("bhtd,bhsd->bhts", qc, kc) * d
        num = jnp.einsum("bhts,bhsd->bhtd", s, vc) + inter[..., None] * jnp.einsum("bhvd,bhtd->bhtv", c_prev, qc)
        den = s.sum(-1) + inter * jnp.einsum("bhd,bhtd->bht", n_prev, qc)
        h = num / jnp.maximum(jnp.abs(den), jnp.exp(-m_t))[..., None]
        b_last = b[..., -1]
        log_w = b_last[..., None] - b + li
        m_new = jnp.maximum(b_last + m_prev, log_w.max(-1))
        w = jnp.exp(log_w - m_new[..., None])
        decay = jnp.exp(b_last + m_prev - m_new)
        c_new = decay[..., None, None] * c_prev + jnp.einsum("bhs,bhsv,bhsd->bhvd", w, vc, kc)
        n_new = decay[..., None] * n_prev + jnp.einsum("bhs,bhsd->bhd", w, kc)
        return (c_new, n_new, m_new), h

    state, h = lax.scan(step, state, (to_chunks(q), to_chunks(k), to_chunks(v), to_chunks(log_i), to_chunks(log_f)))
    return jnp.moveaxis(h, 0, 2).reshape(bsz, nh, n, dh), state

def mixer_heads(stream, shift, scale, w_in, conv_fn, conv_w, conv_b, gate_b, states):
    proj = modulate(layer_norm(stream), shift, scale) @ w_in
    qk_pre, v, o_pre, g, f_in = jnp.split(proj, SPLITS, axis=-1)
    qk = jax.nn.silu(conv_fn(qk_pre, conv_w, conv_b))
    q, k = jnp.split(qk, 2, axis=-1)
    q = split_heads(q)
    k = split_heads(k) * MLSTM_HEAD_DIM ** -0.5
    v = split_heads(v)
    bsz, n, _ = g.shape
    pre = (g.reshape(bsz, n, N_DIRS, 2, MLSTM_HEADS) + gate_b).astype(jnp.float32)
    pre = jnp.transpose(pre, (2, 3, 0, 4, 1))
    log_i = pre[:, 0]
    log_f = jax.nn.log_sigmoid(pre[:, 1])
    h_fwd, st_fwd = mlstm_chunkwise(q, k, v, log_i[0], log_f[0], states[0])
    rev = lambda t: jnp.flip(t, axis=2)
    h_bwd, st_bwd = mlstm_chunkwise(rev(q), rev(k), rev(v), rev(log_i[1]), rev(log_f[1]), states[1])
    return h_fwd + rev(h_bwd), o_pre, f_in, (st_fwd, st_bwd)

def mlstm_readout(h, o_pre, head_g):
    bsz, nh, n, dh = h.shape
    hn = jnp.transpose(layer_norm(h), (0, 2, 1, 3)).reshape(bsz, n, nh * dh)
    return (hn * head_g * jax.nn.sigmoid(o_pre.astype(jnp.float32))).astype(o_pre.dtype)

def fourier_mix(u):
    bsz, n, _ = u.shape
    grp = u.astype(jnp.float32).reshape(bsz, n, FOURIER_GROUPS, FOURIER_GROUP_DIM)
    spec = jnp.fft.fft2(grp, axes=(1, 3), norm="ortho")
    return jnp.real(spec).reshape(bsz, n, D_FOURIER).astype(u.dtype)

def mixer_residual(stream, h_m, o_pre, f_in, gate, head_g, w_out, ln_g, ln_b):
    mix = jnp.concatenate([mlstm_readout(h_m, o_pre, head_g), fourier_mix(f_in)], axis=-1) @ w_out
    return layer_norm_affine(DEEPNORM_ALPHA * stream + gate * mix, ln_g, ln_b)

def moe_ffn(h, w_router, router_bias, w_expert_gu, w_expert_down, w_shared_gu, w_shared_down):
    bsz, n, d = h.shape
    t = h.reshape(bsz * n, d)
    n_tok = t.shape[0]
    n_assign = n_tok * TOP_K
    scores = jax.nn.sigmoid((t @ w_router).astype(jnp.float32))
    _, idx = lax.top_k(scores + router_bias.astype(jnp.float32), TOP_K)
    sel = jnp.take_along_axis(scores, idx, axis=-1)
    gate_w = ROUTED_SCALE * sel / sel.sum(-1, keepdims=True)
    flat_e = idx.reshape(-1)
    order = jnp.argsort(flat_e)
    sorted_e = flat_e[order]
    sizes = jnp.bincount(flat_e, length=N_EXPERTS)
    padded = (sizes + EXPERT_BLOCK - 1) // EXPERT_BLOCK * EXPERT_BLOCK
    start = jnp.cumsum(sizes) - sizes
    pad_end = jnp.cumsum(padded)
    pad_start = pad_end - padded
    dest = pad_start[sorted_e] + jnp.arange(n_assign) - start[sorted_e]
    n_rows = (n_assign + EXPERT_BLOCK - 1) // EXPERT_BLOCK * EXPERT_BLOCK + N_EXPERTS * EXPERT_BLOCK
    n_blocks = n_rows // EXPERT_BLOCK
    row_tok = jnp.zeros((n_rows,), jnp.int32).at[dest].set((order // TOP_K).astype(jnp.int32))
    row_w = jnp.zeros((n_rows,), jnp.float32).at[dest].set(gate_w.reshape(-1)[order])
    block_e = jnp.minimum(jnp.searchsorted(pad_end, jnp.arange(n_blocks) * EXPERT_BLOCK, side="right"), N_EXPERTS - 1)
    xb = t[row_tok].reshape(n_blocks, EXPERT_BLOCK, d)

    def expert_block(args):
        xblk, e = args
        g, u = jnp.split(xblk @ w_expert_gu[e], 2, axis=-1)
        return (jax.nn.silu(g) * u) @ w_expert_down[e]

    yb = lax.map(expert_block, (xb, block_e)).reshape(n_rows, d)
    routed = jax.ops.segment_sum(yb * row_w[:, None].astype(yb.dtype), row_tok, num_segments=n_tok)
    sg, su = jnp.split(t @ w_shared_gu, 2, axis=-1)
    shared = (jax.nn.silu(sg) * su) @ w_shared_down
    return (routed + shared).reshape(bsz, n, d)

def channel_residual(stream, shift, scale, gate, w_router, router_bias, w_expert_gu, w_expert_down,
                     w_shared_gu, w_shared_down, ln_g, ln_b):
    y = moe_ffn(modulate(layer_norm(stream), shift, scale), w_router, router_bias,
                w_expert_gu, w_expert_down, w_shared_gu, w_shared_down)
    return layer_norm_affine(DEEPNORM_ALPHA * stream + gate * y, ln_g, ln_b)

def setup_inputs(seed: int = 0) -> dict:
    key = jax.random.key(seed)
    ks = jax.random.split(key, 24)

    def nrm(k, shape, scale):
        return scale * jax.random.normal(k, shape, jnp.float32)

    f_bias = jnp.linspace(3.0, 6.0, MLSTM_HEADS, dtype=jnp.float32)
    gate_b = jnp.stack([nrm(ks[9], (DEPTH, N_DIRS, MLSTM_HEADS), 0.1),
                        f_bias + nrm(ks[10], (DEPTH, N_DIRS, MLSTM_HEADS), 0.1)], axis=2)
    return {
        "x": nrm(ks[0], (BATCH, SEQ, D_MODEL), 1.0),
        "c": nrm(ks[1], (BATCH, D_MODEL), 1.0),
        "ctx": nrm(ks[2], (BATCH, CTX_LEN, D_MODEL), 1.0),
        "c_ctx": nrm(ks[3], (D_MODEL,), 1.0),
        "w_ada": nrm(ks[4], (DEPTH, D_MODEL, 6 * D_MODEL), 0.5 * D_MODEL ** -0.5),
        "b_ada": nrm(ks[5], (DEPTH, 6 * D_MODEL), 0.02),
        "w_in": nrm(ks[6], (DEPTH, D_MODEL, D_IN_PROJ), D_MODEL ** -0.5),
        "conv_w": nrm(ks[7], (DEPTH, CONV_K, CONV_K, 2 * D_MLSTM), 1.0 / CONV_K),
        "conv_b": nrm(ks[8], (DEPTH, 2 * D_MLSTM), 0.02),
        "gate_b": gate_b,
        "head_g": 1.0 + nrm(ks[11], (DEPTH, D_MLSTM), 0.02),
        "w_out": nrm(ks[12], (DEPTH, D_MIX, D_MODEL), DEEPNORM_BETA * D_MIX ** -0.5),
        "ln1_g": 1.0 + nrm(ks[13], (DEPTH, D_MODEL), 0.02),
        "ln1_b": nrm(ks[14], (DEPTH, D_MODEL), 0.02),
        "w_router": nrm(ks[15], (DEPTH, D_MODEL, N_EXPERTS), D_MODEL ** -0.5),
        "router_bias": nrm(ks[16], (DEPTH, N_EXPERTS), 0.01),
        "w_expert_gu": nrm(ks[17], (DEPTH, N_EXPERTS, D_MODEL, 2 * D_EXPERT), D_MODEL ** -0.5),
        "w_expert_down": nrm(ks[18], (DEPTH, N_EXPERTS, D_EXPERT, D_MODEL), DEEPNORM_BETA * D_EXPERT ** -0.5),
        "w_shared_gu": nrm(ks[19], (DEPTH, D_MODEL, 2 * D_EXPERT), D_MODEL ** -0.5),
        "w_shared_down": nrm(ks[20], (DEPTH, D_EXPERT, D_MODEL), DEEPNORM_BETA * D_EXPERT ** -0.5),
        "ln2_g": 1.0 + nrm(ks[21], (DEPTH, D_MODEL), 0.02),
        "ln2_b": nrm(ks[22], (DEPTH, D_MODEL), 0.02),
    }

def reference(x, c, ctx, c_ctx, w_ada, b_ada, w_in, conv_w, conv_b, gate_b, head_g, w_out, ln1_g, ln1_b,
              w_router, router_bias, w_expert_gu, w_expert_down, w_shared_gu, w_shared_down, ln2_g, ln2_b):
    rows = x.shape[1] // GRID_W
    latent_conv = functools.partial(conv_grid, rows=rows)
    for l in range(DEPTH):
        mod_x = [m[:, None, :] for m in jnp.split(jax.nn.silu(c) @ w_ada[l] + b_ada[l], 6, axis=-1)]
        mod_c = jnp.split(jax.nn.silu(c_ctx) @ w_ada[l] + b_ada[l], 6, axis=-1)
        h_c, o_c, f_c, ctx_states = mixer_heads(ctx, mod_c[0], mod_c[1], w_in[l], conv_seq, conv_w[l], conv_b[l],
                                                gate_b[l], zero_states(ctx.shape[0]))
        h_x, o_x, f_x, _ = mixer_heads(x, mod_x[0], mod_x[1], w_in[l], latent_conv, conv_w[l], conv_b[l],
                                       gate_b[l], ctx_states)
        x = mixer_residual(x, h_x, o_x, f_x, mod_x[2], head_g[l], w_out[l], ln1_g[l], ln1_b[l])
        x = channel_residual(x, mod_x[3], mod_x[4], mod_x[5], w_router[l], router_bias[l], w_expert_gu[l],
                             w_expert_down[l], w_shared_gu[l], w_shared_down[l], ln2_g[l], ln2_b[l])
        if l + 1 < DEPTH:
            ctx = mixer_residual(ctx, h_c, o_c, f_c, mod_c[2], head_g[l], w_out[l], ln1_g[l], ln1_b[l])
            ctx = channel_residual(ctx, mod_c[3], mod_c[4], mod_c[5], w_router[l], router_bias[l], w_expert_gu[l],
                                   w_expert_down[l], w_shared_gu[l], w_shared_down[l], ln2_g[l], ln2_b[l])
    return x


_drawn_inputs = setup_inputs


def setup_inputs(seed=0):
    import zlib

    import numpy as np

    out = dict(_drawn_inputs(seed))
    spreads = {}
    factors = {'ctx': 7.257,
     'c_ctx': 5.605,
     'conv_b': 8.0,
     'head_g': 33.219,
     'ln2_g': 7.511,
     'ln2_b': 7.771}
    for name, (base, spread) in spreads.items():
        noise = np.random.default_rng([zlib.crc32(name.encode()), seed]).standard_normal(out[name].shape)
        drawn = base * np.exp(spread * noise) if base else spread * noise
        out[name] = __import__('jax').numpy.asarray(drawn.astype(out[name].dtype))
    for name, factor in factors.items():
        out[name] = (out[name] * factor).astype(out[name].dtype)
    return out
```

```python
from contextlib import ExitStack

import numpy as np

import concourse.bass as bass
from concourse import mybir

P = 128
D = 1024
KT = D // P
SEQ = 1024
CTX = 256
NTC = CTX // P
NTX = SEQ // P
NT = NTC + NTX
HEADS = 4
DH = 128
DM = HEADS * DH
DF = 512
VW = DH + 1
NE = 64
TOPK = 8
DE = 256
ROWS_OUT = SEQ + P
XW = D + NE
MAXB = P
NBUF = 4
WE = KT * 2 * DE + (DE // P) * D
ALPHA = 2.0 ** 0.25
EPS = 1e-5
KSCALE = DH ** -0.5
ROUTED = 2.5
BIG = 1e30
NEV = SEQ // 4 + 1
NOD = SEQ // 4
GW = 66
GH = 18

ALU = mybir.AluOpType
ACT = mybir.ActivationFunctionType
AX = mybir.AxisListType.X
F32 = mybir.dt.float32
I32 = mybir.dt.int32
U32 = mybir.dt.uint32

C_ID, C_REV, C_MF, C_MB, C_ONE, C_LT, C_IOTA, C_SEL = (i * P for i in range(8))
C_HALF = C_SEL + 8 * P
C_PADROW = C_HALF + 16
C_TOK = C_PADROW + 1
C_P = C_TOK + 8
C_CD = C_P + 7
C_END = C_CD + 256


def constant_tiles():
    p = np.arange(P)
    c = np.zeros((P, C_END), np.float32)
    c[p, C_ID + p] = 1
    c[p, C_REV + P - 1 - p] = 1
    c[:, C_MF:C_MF + P] = np.where(p[:, None] <= p[None, :], 0, -BIG)
    c[:, C_MB:C_MB + P] = np.where(p[:, None] >= p[None, :], 0, -BIG)
    c[:, C_ONE:C_ONE + P] = 1
    c[:, C_LT:C_LT + P] = p[:, None] < p[None, :]
    c[:, C_IOTA:C_IOTA + P] = p[None, :]
    for r in range(8):
        c[r, C_SEL + r * P:C_SEL + (r + 1) * P] = 1
    c[:, C_HALF:C_HALF + 16] = -0.5
    c[:, C_PADROW] = SEQ + p + 1
    c[:, C_TOK:C_TOK + 8] = p[:, None] + P * np.arange(8)[None, :] + 1
    c[:, C_P] = p
    g = 64
    m = np.arange(g)
    ang = 2 * np.pi * (np.outer(m, m) % g) / g
    scale = 1.0 / np.sqrt(SEQ * g)
    for b in range(2):
        s = slice(b * g, (b + 1) * g)
        c[s, C_CD + b * g:C_CD + (b + 1) * g] = np.cos(ang) * scale
        c[s, C_CD + P + b * g:C_CD + P + (b + 1) * g] = np.sin(ang) * scale
    n = np.arange(SEQ // 2)
    ev = 2 * np.pi * (np.outer(n, 2 * np.arange(NEV)) % SEQ) / SEQ
    od = 2 * np.pi * (np.outer(n, 2 * np.arange(NOD) + 1) % SEQ) / SEQ
    dft = np.concatenate([np.cos(ev), np.sin(ev), np.cos(od), np.sin(od)], axis=1).astype(np.float32)
    return c, np.ascontiguousarray(dft)


def build(nc, a, out):
    ctx = ExitStack()
    with ctx:
        def sb(name, cols, dt=F32, parts=P):
            return ctx.enter_context(nc.sbuf_tensor(name, [parts, cols], dt))

        sems = {}

        def sem(name):
            if name not in sems:
                sems[name] = ctx.enter_context(nc.semaphore(name))
            return sems[name]

        cst = sb("cst", C_END)
        arena = sb("arena", 48188)
        A0, B0, C0, D0 = 0, 10240, 19496, 39996

        def at(o, n):
            return arena[:, o:o + n]

        ident = cst[:, C_ID:C_ID + P]
        rev = cst[:, C_REV:C_REV + P]
        ones = cst[:, C_ONE:C_ONE + P]
        iota = cst[:, C_IOTA:C_IOTA + P]

        ccol = sb("ccol", 16)
        silc = sb("silc", 16)
        bada = sb("bada", 48)
        modc = sb("modc", 4 * 16)
        convw = sb("convw", 8 * 9)
        convb = sb("convb", 8)
        gateb = sb("gateb", 2)
        stats = sb("stats", 12)
        mv = sb("mv", 2 * NT)
        veps = sb("veps", NT)
        rstd = sb("rstd", NT)
        G = sb("G", NT * 32)
        mprev = sb("mprev", NT + 1)
        COL = sb("COL", NT * 48)
        dgl = sb("dgl", NT * 8)
        DEC = sb("DEC", NT * 8)
        den = sb("den", 4)
        rec = sb("rec", 4)
        rowt = sb("rowt", 512, parts=1)
        idxg = sb("idxg", 2, U32)
        idxs = sb("idxs", 2, U32)
        zrow = sb("zrow", P, parts=8)
        hst = sb("hst", 24)
        hmv = sb("hmv", 16)[:, :].rearrange("p (b h n) -> p b h n", b=2, h=4)
        hveps = sb("hveps", 8)[:, :].rearrange("p (b h) -> p b h", b=2)
        hrstd = sb("hrstd", 8)[:, :].rearrange("p (b h) -> p b h", b=2)
        mvj = sb("mvj", 4)[:, :].rearrange("p (b n) -> p b n", b=2)
        mvk = sb("mvk", 4)[:, :].rearrange("p (b n) -> p b n", b=2)

        psum = ctx.enter_context(nc.psum_tensor("psum", [P, 8 * 512], F32))
        psN = psum[:, 3 * 512:5 * 512]
        psY = psum[:, 5 * 512:7 * 512]

        def bank(i):
            return psum[:, 512 * i:512 * i + 512]

        ada = [at(C0, 8192).rearrange("p (k n) -> p k n", k=8), at(C0 + 8192, 8192).rearrange("p (k n) -> p k n", k=8)]
        piece = [at(D0, 4096).rearrange("p (k n) -> p k n", k=4), at(D0 + 4096, 4096).rearrange("p (k n) -> p k n", k=4)]
        xin = [at(B0 + 1024 * (t % 9), 1024) for t in range(NT)]
        uT = at(A0, 10240).rearrange("p (k n) -> p k n", k=8)
        wf = at(C0 + 16396, 4096).rearrange("p (k n) -> p k n", k=8)
        fT = at(C0, 4096).rearrange("p (c n) -> p c n", c=4)
        EO = at(C0 + 4096, 8192).rearrange("p (s c n) -> p s c n", s=8, c=4)
        CSW = 2 * NEV + 2 * NOD
        CS = at(C0 + 12288, 4 * CSW).rearrange("p (j n) -> p j n", j=4)
        qtmp = at(C0 + 16400, 2 * 260).rearrange("p (b n) -> p b n", b=2)
        mixT = at(D0, 8192).rearrange("p (k n) -> p k n", k=8)
        wqk = at(B0, 8192).rearrange("p (k n) -> p k n", k=8)
        cbuf = [at(D0 + 1188 * i, 1188).rearrange("p (r c) -> p r c", r=GH) for i in range(2)]
        cacc = at(D0 + 2376, 1024).rearrange("p (r c) -> p r c", r=16)
        cbufc = at(D0 + 3400, 258)
        caccc = at(D0 + 3658, 256)
        qkT = at(C0, 8192).rearrange("p (c n) -> p c n", c=8)
        kTc = at(C0 + 8192, 1024).rearrange("p (c n) -> p c n", c=4)
        wvog = at(C0 + 9216, 8320).rearrange("p (k n) -> p k n", k=8)
        V = at(B0, NT * 4 * VW).rearrange("p (t h n) -> p t h n", t=NT, h=4)
        O = at(B0 + NT * 4 * VW, 4096).rearrange("p (t n) -> p t n", t=NTX)
        NR = NT * P

        def row(o):
            return arena[0:8, o:o + NR]

        Ra, Rf, Rl = row(D0), row(D0 + NR), row(D0 + 2 * NR)
        Ri, Rw, Re = (row(C0 + 9216 + i * NR) for i in range(3))
        Rb, Rm = (row(C0 + 17536 + i * NR) for i in range(2))
        Rrev = [row(C0 + 9216 + (3 + i) * NR) for i in range(3)]
        kM = at(A0, 5120).rearrange("p (t n) -> p t n", t=NT)
        H = at(A0 + 5120, 4096).rearrange("p (t n) -> p t n", t=NTX)
        qI = at(A0 + 9216, 1024).rearrange("p (b n) -> p b n", b=2)
        HB = C0 + 9216 + 3 * NR
        Dt = at(HB, 1024).rearrange("p (b n) -> p b n", b=2)
        vw = at(HB + 1024, 1032).rearrange("p (b h n) -> p b h n", b=2, h=4)
        Cst = at(HB + 2056, 1032).rearrange("p (b h n) -> p b h n", b=2, h=4)
        htmp = at(HB + 3088, 512)
        hgB = at(HB, 512)
        og = at(HB + 512, 512)
        wout = at(C0, 8192).rearrange("p (k n) -> p k n", k=8)
        x1 = at(A0, 8192).rearrange("p (t n) -> p t n", t=NTX)
        g1B, lg1, lb1 = (at(B0 + i * 1024, 1024) for i in range(3))
        xres = at(B0 + 3072, 2048).rearrange("p (b n) -> p b n", b=2)
        ytmp = at(B0 + 5120, 2048).rearrange("p (b n) -> p b n", b=2)
        tT = at(C0 + 8192, 8192).rearrange("p (k n) -> p k n", k=8)
        lnt = at(C0 + 16384, 2 * 1024).rearrange("p (b n) -> p b n", b=2)
        wr = at(B0, 512).rearrange("p (k n) -> p k n", k=8)
        rbB = at(B0 + 512, 64)
        KB = B0 + 1024
        sc, bs, rp, mk, wt, sl, t512, t512b = (at(KB + i * 512, 512) for i in range(8))
        KC = KB + 8 * 512
        m8 = at(KC, 64)
        s8 = at(KC + 64, 64)
        ssum = at(KC + 128, 8)
        cnt, nbf, bend, bbase, zr, n2 = (at(KC + 136 + 64 * i, 64) for i in range(6))
        cnti = arena[:, KC + 520:KC + 584].bitcast(I32)
        p8 = at(KC + 584, 64)
        b8 = at(KC + 648, 64)
        s8i = arena[:, KC + 712:KC + 776].bitcast(I32)
        b8i = arena[:, KC + 776:KC + 840].bitcast(I32)
        ebc = at(KC + 840, 1)
        zpad = at(KC + 848, XW)
        oneP = at(C0 + 18432, 256).rearrange("p (b n) -> p b n", b=2)
        oneB = at(C0 + 18688, 256).rearrange("p (b n) -> p b n", b=2)
        Ttmp = at(C0 + 18944, 256).rearrange("p (b n) -> p b n", b=2)
        idxT = sb("idxT", P + 2, U32)
        tbl = sb("tbl", 3 * P, I32, parts=1)
        tblf = sb("tblf", P, parts=1)
        endi = sb("endi", NE, I32, parts=1)
        npair = sb("npair", 1, I32, parts=1)
        wsgu = at(D0, 4096).rearrange("p (k n) -> p k n", k=8)
        wsd = at(D0 + 4096, 2048).rearrange("p (k n) -> p k n", k=2)
        sg, hx, hTf = (at(A0 + 8192 + 512 * i, 512).rearrange("p (b n) -> p b n", b=2) for i in range(3))
        hT = at(A0 + 8192 + 1024, 512).rearrange("p (b k n) -> p b k n", b=2, k=2)
        W0 = A0 + 8192 + 1536
        MB = W0 + NBUF * WE
        xT = at(MB, 2048).rearrange("p (b k n) -> p b k n", b=2, k=8)
        xg = at(MB + 2048, 2 * XW).rearrange("p (b n) -> p b n", b=2)
        yB = at(D0 + 6144, 2048).rearrange("p (b n) -> p b n", b=2)
        assert MB + 2048 + 2 * XW <= D0
        g2B, lg2, lb2 = (at(W0 + i * 1024, 1024) for i in range(3))
        acc_in = [at(W0 + 3072 + 1024 * i, 1024) for i in range(8)]
        acc_tmp = at(W0 + 11264, 1024)

        t_dram = nc.dram_tensor("t_rows", [ROWS_OUT, XW], F32, kind="Internal").ap()
        acc = nc.dram_tensor("moe_sum", [ROWS_OUT, D], F32, kind="Internal").ap()
        grow = nc.dram_tensor("gate_rows", [2, D], F32, kind="Internal").ap()

        def drows(w, n0, n1):
            return w.rearrange("(p k) n -> p k n", k=8)[:, :, n0:n1]

        def tiles_of(s):
            return (s, NTC - 1 - s) if s < NTC else (s, NTC + NT - 1 - s)

        ABJOBS = [(i, j, cp) for i, j in enumerate((0, 4, 1, 5, 2, 6, 3, 7)) for cp in range(2)]
        QKJOBS = [(c, part) for c in range(8) for part in range(3 if c >= 4 else 2)]
        JOBS = [(s, d, tiles_of(s)[d]) for s in range(NT) for d in range(2)]
        NJ = len(JOBS)
        FIRSTX = 2 * NTC
        PIECES = [(3, 0), (3, 1), (4, 0), (4, 1), (2, 0), (2, 1), (5, 0), (5, 1)]
        XG = [0] * 2 + [1] * 4 + [2] * 4
        GROUPS = [(0, 2), (2, 4), (6, 4)]

        block = ctx.enter_context(nc.Block())
        S = sem

        @block.sync
        def _(sp):
            sp.dma_start(ccol[:, :], a["cc"]).then_inc(S("c_in"), 16)
            sp.dma_start(cst[:, :], a["const"]).then_inc(S("const_in"), 16)
            sp.dma_start(bada[:, :].rearrange("p (m k) -> p m k", m=6), a["b_ada"].rearrange("o (m p k) -> p (o m) k", m=6, k=8)).then_inc(S("const_in"), 16)
            for t in range(3):
                sp.dma_start(xin[t], a["toks"][P * t:P * t + P, :]).then_inc(S(f"x_in{XG[t]}"), 16)
            for m in range(2):
                sp.dma_start(ada[m], drows(a["w_ada"], m * D, (m + 1) * D)).then_inc(S(f"ada_in{m}"), 16)
            for t in range(3, 9):
                sp.dma_start(xin[t], a["toks"][P * t:P * t + P, :]).then_inc(S(f"x_in{XG[t]}"), 16)
            sp.dma_start(wf, drows(a["w_f"], 0, DF)).then_inc(S("wf_in"), 16)
            sp.wait_ge(S("tr_done"), 8)
            sp.dma_start(xin[9], a["toks"][P * 9:P * 10, :]).then_inc(S("x_in2"), 16)
            sp.dma_start(convw[:, :], a["conv_wt"]).then_inc(S("small_in"), 16)
            sp.dma_start(convb[:, :], a["conv_bt"]).then_inc(S("small_in"), 16)
            sp.dma_start(gateb[0:8, :], a["gate_bt"]).then_inc(S("small_in"), 16)
            for i, (m, h) in enumerate(PIECES):
                if i >= 2:
                    sp.wait_ge(S("piece_used"), i - 1)
                sp.dma_start(piece[i % 2], drows(a["w_ada"], m * D, (m + 1) * D)[:, 4 * h:4 * h + 4, :]).then_inc(S(f"piece_in{i % 2}"), 16)
                if i == 2:
                    sp.wait_ge(S("ada_done"), 2)
                    sp.dma_start(CS, a["dft"].rearrange("(j p) n -> p j n", p=P)).then_inc(S("cs_in"), 16)
                if i == 3:
                    sp.wait_ge(S("tr_done"), 24)
                    sp.dma_start(wqk, drows(a["w_qk"], 0, D)).then_inc(S("wqk_in"), 16)
            sp.wait_ge(S("fourier_mm"), 16)
            sp.wait_ge(S("qtmp_used"), 8)
            sp.dma_start(wvog, drows(a["w_vog"], 0, 1040)).then_inc(S("wvog_in"), 16)
            sp.wait_ge(S("N_done"), 16)
            sp.wait_ge(S("h_done"), 16)
            sp.dma_start(wout, a["w_out"].rearrange("(k p) n -> p k n", p=P)).then_inc(S("wout_in"), 16)
            sp.dma_start(hgB, a["head_g"].to_broadcast([P, DM])).then_inc(S("wout_in"), 16)
            sp.wait_ge(S("mix_ready"), NTX)
            sp.wait_ge(S("grow_out"), 64)
            sp.dma_start(g1B, grow[0:1, :].to_broadcast([P, D])).then_inc(S("rows1_in"), 16)
            sp.dma_start(lg1, a["ln1_g"].to_broadcast([P, D])).then_inc(S("rows1_in"), 16)
            sp.dma_start(lb1, a["ln1_b"].to_broadcast([P, D])).then_inc(S("rows1_in"), 16)
            sp.dma_start(ytmp[:, 0], a["b_ada"][0:1, 2 * D:3 * D].to_broadcast([P, D])).then_inc(S("rows1_in"), 16)
            for j in range(NTX):
                if j >= 2:
                    sp.wait_ge(S("res_used"), j - 1)
                sp.dma_start(xres[:, j % 2, :], a["toks"][P * (NTC + j):P * (NTC + j + 1), :]).then_inc(S(f"xres_in{j % 2}"), 16)
                if j >= 1:
                    sp.wait_ge(S("ln_ready"), j)
                    sp.dma_start(t_dram[P * (j - 1):P * j, 0:D], lnt[:, (j - 1) % 2, :]).then_inc(S(f"t_out{(j - 1) % 2}"), 16)
            sp.wait_ge(S("ln_ready"), NTX)
            sp.dma_start(t_dram[P * (NTX - 1):P * NTX, 0:D], lnt[:, (NTX - 1) % 2, :]).then_inc(S(f"t_out{(NTX - 1) % 2}"), 16)
            sp.wait_ge(S("proj_done"), NTX)
            sp.dma_start(wsgu, drows(a["w_shared_gu"], 0, 2 * DE)).then_inc(S(f"w_in{NBUF - 1}"), 16)
            sp.dma_start(wsd, a["w_shared_down"].rearrange("(p k) n -> p k n", k=2)).then_inc(S(f"w_in{NBUF - 1}"), 16)
            sp.dma_start(wr, drows(a["w_router"], 0, NE)).then_inc(S("wr_in"), 16)
            sp.dma_start(rbB, a["router_bias"].to_broadcast([P, NE])).then_inc(S("wr_in"), 16)
            sp.wait_ge(S("wt_ready"), 1)
            sp.dma_start(t_dram[0:SEQ, D:XW].rearrange("(t p) n -> p t n", p=P), wt.rearrange("p (t n) -> p t n", t=8)).then_inc(S("pad_out"), 16)
            sp.wait_ge(S("zpad_ready"), 1)
            sp.dma_start(t_dram[SEQ:ROWS_OUT, :], zpad).then_inc(S("pad_out"), 16)
            for j in range(NTX):
                sp.wait_ge(S("sy_act"), j + 1)
                sp.wait_ge(S("sy_dve"), j + 1)
                sp.dma_start(acc[P * j:P * j + P, :], yB[:, j % 2, :]).then_inc(S(f"acc_out{j % 2}"), 16)
            for i in range(2):
                sp.wait_ge(S(f"acc_out{i}"), 16 * 4)
            sp.wait_ge(S("pad_out"), 32)
            sp.wait_ge(S("scattered"), 16)
            sp.wait_ge(S("table_ready"), 1)
            with sp.Fori(0, NE // NBUF) as g:
                for i in range(NBUF):
                    lim = sp.value_load(endi[0:1, bass.ds(g * NBUF + i, 1)], min_val=1, max_val=P + 1)
                    sp.wait_ge(S("block_done"), lim)
                    w = at(W0 + i * WE, WE)
                    sp.dma_start(w[:, 0:4096], a["w_gu"][bass.ds(g * (NBUF * P) + i * P, P), :]).then_inc(S(f"w_in{i}"), 16)
                    sp.dma_start(w[:, 4096:WE], a["w_dn"][bass.ds(g * (NBUF * P) + i * P, P), :]).then_inc(S(f"w_in{i}"), 16)
                    sp.wait_ge(S(f"w_in{(i - 1) % NBUF}"), 32 * (g + 1))
                    sp.sem_inc(S("weights_ready"), 1)
            sp.wait_ge(S(f"w_in{NBUF - 1}"), 32 * (NE // NBUF) + 32)
            sp.sem_inc(S("weights_ready"), 1)
            sp.wait_ge(S("experts_done"), 1)
            sp.dma_start(g2B, grow[1:2, :].to_broadcast([P, D])).then_inc(S("rows2_in"), 16)
            sp.dma_start(lg2, a["ln2_g"].to_broadcast([P, D])).then_inc(S("rows2_in"), 16)
            sp.dma_start(lb2, a["ln2_b"].to_broadcast([P, D])).then_inc(S("rows2_in"), 16)
            sp.dma_start(acc_tmp, a["b_ada"][0:1, 5 * D:6 * D].to_broadcast([P, D])).then_inc(S("rows2_in"), 16)
            for j in range(NTX):
                sp.dma_start(acc_in[j], acc[P * j:P * j + P, :]).then_inc(S(f"accin{j // 2}"), 16)
            for j in range(NTX):
                sp.wait_ge(S("out_ready"), j + 1)
                sp.dma_start(out[P * j:P * j + P, :], acc_in[j]).then_inc(S("out_done"), 16)
            sp.wait_ge(S("out_done"), 16 * NTX)

        @block.gpsimd
        def _(pool):
            def rstd_of(var_ready, v, col, done):
                pool.wait_ge(*var_ready)
                pool.tensor_scalar(veps[:, col:col + 1], v, EPS, None, ALU.add).then_inc(S("pool_step"), 1)
                n["p"] += 1
                pool.wait_ge(S("pool_step"), n["p"])
                pool.tensor_tensor(rstd[:, col:col + 1], veps[:, col:col + 1], cst[:, C_HALF:C_HALF + 1], ALU.pow).then_inc(S(done), 1)

            n = {"p": 0}
            pool.wait_ge(S("const_in"), 32)
            for t in range(NT):
                rstd_of((S("mv_ready"), t + 1), mv[:, 2 * t + 1:2 * t + 2], t, "rstd_ready")
            pool.wait_ge(S("piece_used"), 8)
            pool.memset(at(D0, 2376), 0.0).then_inc(S("cbuf_zero"), 1)
            pool.memset(cbufc, 0.0).then_inc(S("cbuf_zero"), 1)
            pool.wait_ge(S("qk_done"), 20)
            pool.memset(V[:, :, :, DH:VW], 1.0).then_inc(S("v_ones"), 1)
            pool.wait_ge(S("v_evac"), NT)
            pool.wait_ge(S("v_ones"), 1)
            pool.wait_ge(S("cols_ready"), 1)
            for q, (s, d, t) in enumerate(JOBS):
                if q >= 2:
                    pool.wait_ge(S("U_half"), 2 * (q - 1))
                c0 = s * 48 + 16 + 12 * d
                pool.tensor_tensor(vw[:, q % 2], V[:, t], COL[:, c0:c0 + 4].unsqueeze(2).to_broadcast([P, 4, VW]), ALU.mult).then_inc(S("vw_ready"), 1)
            for j in range(NTX):
                pool.wait_ge(S("hmv_ready"), j + 1)
                if j >= 2:
                    pool.wait_ge(S("mix_ready"), j - 1)
                pool.tensor_scalar(hveps[:, j % 2], hmv[:, j % 2, :, 1], EPS, None, ALU.add).then_inc(S("pool_step"), 1)
                n["p"] += 1
                pool.wait_ge(S("pool_step"), n["p"])
                pool.tensor_tensor(hrstd[:, j % 2], hveps[:, j % 2], cst[:, C_HALF:C_HALF + 4], ALU.pow).then_inc(S("hrstd_ready"), 1)
            for j in range(NTX + 1):
                if j < NTX:
                    rstd_of((S("y_mv"), j + 1), mvj[:, j % 2, 1:2], j % 2, "y_rstd")
                    pool.wait_ge(S("y_norm"), j + 1)
                    pool.wait_ge(S("rows1_in"), 64)
                    pool.tensor_tensor(ytmp[:, j % 2], ytmp[:, j % 2], lg1, ALU.mult).then_inc(S("y_gain"), 1)
                if j >= 1:
                    rstd_of((S("x1_mv"), j), mvk[:, (j - 1) % 2, 1:2], 2 + (j - 1) % 2, "x1_rstd")
            pool.memset(zpad, 0.0).then_inc(S("zpad_ready"), 1)
            pool.wait_ge(S("zpad_ready"), 1)
            pool.dma_start(acc[SEQ:ROWS_OUT, :], zpad[:, 0:D]).then_inc(S("scattered"), 16)
            pool.wait_ge(S("idx_ready"), 1)
            pool.wait_ge(S("table_ready"), 1)
            for i in range(2):
                pool.wait_ge(S(f"t_out{i}"), 64)
                pool.wait_ge(S(f"acc_out{i}"), 64)
            pool.wait_ge(S("pad_out"), 32)
            pool.sem_inc(S("y_free"), 1)

            def gather(col, p, nth):
                pool.tensor_copy(idxg[:, p:p + 1], idxT[:, col]).then_inc(S("idx_copied"), 1)
                pool.wait_ge(S("idx_copied"), nth)
                pool.sem_inc(S("pool_pass"), 1)
                pool.indirect_dma_start(out=xg[:, p], out_offset=None, in_=t_dram[:, :],
                                        in_offset=bass.IndirectOffsetOnAxis(ap=idxg[:, p:p + 1], axis=0)).then_inc(S(f"gathered{p}"), 16)

            gather(slice(0, 1), 0, 1)
            gather(slice(1, 2), 1, 2)
            np_ = pool.value_load(npair[0:1, 0:1], min_val=1, max_val=MAXB // 2)
            with pool.Fori(0, np_) as i:
                for p in range(2):
                    pool.wait_ge(S("m_hx"), 2 * i + (p + 1))
                    pool.wait_ge(S("m_xt"), 2 * i + (p + 1))
                    gather(bass.ds(2 * i + (p + 2), 1), p, 4 * i + (2 * p + 3))
                    pool.wait_ge(S("scattered"), 32 * i + 16 * (p + 1))
                    pool.sem_inc(S("y_free"), 1)
                    pool.tensor_copy(idxs[:, p:p + 1], idxT[:, bass.ds(2 * i + p, 1)]).then_inc(S("idx_copied"), 1)
                    pool.wait_ge(S("idx_copied"), 4 * i + (2 * p + 4))
                    pool.wait_ge(S("m_ya"), 2 * i + (p + 2))
                    pool.wait_ge(S("m_yb"), 2 * i + (p + 2))
                    pool.sem_inc(S("pool_pass"), 1)
                    pool.indirect_dma_start(out=acc[:, :], out_offset=bass.IndirectOffsetOnAxis(ap=idxs[:, p:p + 1], axis=0),
                                            in_=yB[:, p], in_offset=None, compute_op=ALU.add).then_inc(S("scattered"), 16)
            pool.wait_ge(S("scattered"), 32 * np_ + 16)
            for p in range(2):
                pool.wait_ge(S(f"gathered{p}"), 16 * np_ + 16)
            pool.sem_inc(S("experts_done"), 1)
            for j in range(NTX):
                rstd_of((S("o_mv"), j + 1), mvj[:, j % 2, 1:2], j % 2, "o_rstd")
                pool.wait_ge(S("o_norm"), j + 1)
                pool.wait_ge(S("rows2_in"), 64)
                pool.tensor_tensor(acc_in[j], acc_in[j], lg2, ALU.mult).then_inc(S("o_gain"), 1)

        @block.scalar
        def _(act):
            def copy(o, i):
                return act.activation(o, i, ACT.Copy)

            act.wait_ge(S("c_in"), 16)
            act.activation(silc[:, :], ccol[:, :], ACT.Silu).then_inc(S("sil_ready"), 1)
            act.wait_ge(S("mod_ready"), 2)
            for g, (t0, nt) in enumerate(GROUPS):
                for k in range(0, 8, 2):
                    q = 8 * g + k
                    w = 0 if g else 1
                    act.wait_ge(S("tr_done"), q + 1)
                    act.activation(uT[:, k, P * t0:P * (t0 + nt)], bank(q % 4)[:, 0:P * nt], ACT.Identity,
                                   scale=modc[:, 16 + 2 * k + w:17 + 2 * k + w], bias=modc[:, 2 * k + w:2 * k + w + 1]).then_inc(S("uT_act"), 1)
            def grow_out(m):
                for h in range(2):
                    act.wait_ge(S("piece_used"), 6 + 2 * m)
                    if 2 * m + h >= 1:
                        act.wait_ge(S("grow_out"), 16 * (2 * m + h))
                    copy(rowt[:, :], bank(6 if h == 0 else 0)[0:1, :]).then_inc(S("grow_put"), 1)
                    act.wait_ge(S("grow_put"), 2 * m + h + 1)
                    act.dma_start(grow[m:m + 1, 512 * h:512 * h + 512], rowt[:, :]).then_inc(S("grow_out"), 16)
            for i in range(8):
                act.wait_ge(S("f_done"), i + 1)
                c, h = i // 2, i % 2
                copy(fT[:, c, 512 * h:512 * h + 512], bank(4 + i % 2)).then_inc(S("f_evac"), 1)
                if i == 5:
                    grow_out(0)
            grow_out(1)
            for q, (idx, j, cp) in enumerate(ABJOBS):
                if idx % 2 == 0:
                    act.wait_ge(S("ab_done"), q + 1)
                    copy(EO[:, j, 2 * cp:2 * cp + 2, :], bank(1 + q % 3).rearrange("p (c n) -> p c n", c=2)).then_inc(S("ab_act"), 1)
            for c in range(4):
                for g, w in ((0, NEV), (1, NOD)):
                    act.wait_ge(S("fourier_mm"), 4 * c + 2 * g + 2)
                    if c:
                        act.wait_ge(S("qtmp_used"), 2 * (c - 1) + g + 1)
                    copy(qtmp[:, g, 0:w], bank((0 if c % 2 else 4) + 2 * g + 1)[:, 0:w]).then_inc(S("qtmp_ready"), 1)
            act.wait_ge(S("cbuf_zero"), 2)
            act.wait_ge(S("small_in"), 48)
            for c in range(9):
                if c < 8:
                    for q, (cc, part) in enumerate(QKJOBS):
                        if cc != c:
                            continue
                        act.wait_ge(S("qk_done"), q + 1)
                        if part == 0 and c >= 2:
                            act.wait_ge(S("conv_done"), c - 1)
                        if part == 2 and c >= 5:
                            act.wait_ge(S("conv_done"), c)
                        if part < 2:
                            copy(cbuf[c % 2][:, 1 + 8 * part:9 + 8 * part, 1:65], bank(q % 4).rearrange("p (r c) -> p r c", r=8)).then_inc(S("cv_evac"), 1)
                        else:
                            copy(cbufc[:, 1:257], bank(q % 4)[:, 0:256]).then_inc(S("cv_evac"), 1)
                if c >= 1:
                    act.wait_ge(S("conv_done"), c)
                    x = c - 1
                    act.activation(qkT[:, x, :], cacc.rearrange("p r c -> p (r c)"), ACT.Silu, bias=convb[:, x:x + 1]).then_inc(S("silu_done"), 1)
                    if x >= 4:
                        act.activation(kTc[:, x - 4, :], caccc, ACT.Silu, bias=convb[:, x:x + 1]).then_inc(S("siluc_done"), 1)
            act.wait_ge(S("rows_evac"), 6)
            act.activation(Rl, Rf, ACT.Abs).then_inc(S("rl_step"), 1)
            act.wait_ge(S("rl_step"), 1)
            act.activation(Rl, Rl, ACT.Exp, scale=-1.0).then_inc(S("rl_step"), 1)
            act.wait_ge(S("rl_step"), 2)
            act.activation(Rl, Rl, ACT.Ln, bias=1.0).then_inc(S("rl_step"), 1)
            for t in range(NT):
                act.wait_ge(S("v_done"), t + 1)
                copy(V[:, t, :, 0:DH], bank(4 + t % 2).rearrange("p (h n) -> p h n", h=4)).then_inc(S("v_evac"), 1)
                if t >= NTC:
                    act.wait_ge(S("o_done"), t - NTC + 1)
                    act.activation(O[:, t - NTC], bank(6), ACT.Tanh, scale=0.5).then_inc(S("o_evac"), 1)
            act.wait_ge(S("wargs_ready"), 3)
            for i, r in enumerate((Rw, Re, Ri)):
                act.activation(r, r, ACT.Exp).then_inc(S("rows_exp"), 1)
            act.wait_ge(S("rows_exp"), 3)
            for r, o in zip((Ra, Rw, Re), Rrev):
                copy(o.rearrange("p (s n) -> p s n", s=NT), r.rearrange("p (s n) -> p s n", s=NT)[:, :, ::-1]).then_inc(S("rows_rev"), 1)
            for t in range(NT):
                act.wait_ge(S("kM_done"), t + 1)
                act.mul(kM[:, t], bank(t % 2), KSCALE).then_inc(S("kM_evac"), 1)
            act.wait_ge(S("cols_ready"), 1)
            for x in range(16):
                s, d, t = JOBS[x + FIRSTX]
                act.wait_ge(S("SD_done"), x + 1)
                if x >= 2:
                    act.wait_ge(S("N_done"), x - 1)
                for h in range(4):
                    c0 = s * 48 + 12 * d + h
                    ins = act.activation(Dt[:, x % 2, P * h:P * h + P], bank(2 if x % 2 == 0 else 5)[:, P * h:P * h + P], ACT.Exp, bias=COL[:, c0:c0 + 1])
                ins.then_inc(S("D_ready"), 1)
            for j in range(NTX):
                act.wait_ge(S("mixt_done"), j + 1)
                copy(mixT[:, 0:4, P * j:P * j + P], bank(j % 2).rearrange("p (h n) -> p h n", h=4)).then_inc(S("mixt_evac"), 1)
            for j in range(NTX):
                act.wait_ge(S("tt_done"), j + 1)
                for k in range(8):
                    ins = act.activation(tT[:, k, P * j:P * j + P], bank(k // 4)[:, P * (k % 4):P * (k % 4) + P], ACT.Identity,
                                         scale=modc[:, 48 + 2 * k:49 + 2 * k], bias=modc[:, 32 + 2 * k:33 + 2 * k])
                ins.then_inc(S("tT_evac"), 1)
            act.wait_ge(S("router_done"), 1)
            act.activation(sc, bank(2), ACT.Sigmoid).then_inc(S("sc_ready"), 1)
            for j in range(NTX):
                act.wait_ge(S("sgu_done"), j + 1)
                act.activation(sg[:, j % 2], bank(3 + j % 2)[:, 0:DE], ACT.Silu).then_inc(S("s_sg"), 1)
                act.wait_ge(S("sht_done"), j + 1)
                copy(hT[:, j % 2], bank(7)[:, 0:2 * P].rearrange("p (k n) -> p k n", k=2)).then_inc(S("s_hT"), 1)
                act.wait_ge(S("sdown_done"), j + 1)
                if j >= 2:
                    act.wait_ge(S(f"acc_out{j % 2}"), 16 * (j // 2))
                copy(yB[:, j % 2, 0:512], bank(5)).then_inc(S("sy_act"), 1)
            def x_evac(p):
                for k in range(4):
                    ins = act.activation(xT[:, p, k], bank(0)[:, P * k:P * k + P], ACT.Identity,
                                         scale=modc[:, 48 + 2 * k:49 + 2 * k], bias=modc[:, 32 + 2 * k:33 + 2 * k])
                ins.then_inc(S("m_xa"), 1)

            act.wait_ge(S("m_xt"), 1)
            x_evac(0)
            act.wait_ge(S("table_ready"), 1)
            act.sem_inc(S("m_ya"), 1)
            np_ = act.value_load(npair[0:1, 0:1], min_val=1, max_val=MAXB // 2)
            with act.Fori(0, np_) as i:
                for p in range(2):
                    b1 = 2 * i + (p + 1)
                    act.wait_ge(S("m_gu"), b1)
                    act.activation(sg[:, p], bank(3 + p)[:, 0:DE], ACT.Silu).then_inc(S("m_sg"), 1)
                    act.wait_ge(S("m_ht"), b1)
                    copy(hT[:, p], bank(7)[:, 0:2 * P].rearrange("p (k n) -> p k n", k=2)).then_inc(S("m_hT"), 1)
                    act.wait_ge(S("m_xt"), 2 * i + (p + 2))
                    x_evac(1 - p)
                    act.wait_ge(S("block_done"), 2 * i + (p + 2))
                    act.wait_ge(S("y_free"), 2 * i + (p + 1))
                    copy(yB[:, p, 0:512], bank(5)).then_inc(S("m_ya"), 1)

        @block.tensor
        def _(pe):
            mm = pe.matmul

            def ada_cols(w, kc, k, rhs, base, start):
                return mm(bank(7)[:, base + 2 * k:base + 2 * k + 2], w[:, kc % w.shape[1], k::8], rhs, start=start, stop=False, skip_group_check=True)

            pe.wait_ge(S("sil_ready"), 1)
            for m in range(2):
                pe.wait_ge(S(f"ada_in{m}"), 16)
                for kc in range(8):
                    for k in range(8):
                        ins = ada_cols(ada[m], kc, k, silc[:, 2 * kc:2 * kc + 2], 16 * m, m == 0 and kc == 0 and k == 0)
                ins.then_inc(S("ada_done"), 1)
            pe.wait_ge(S("const_in"), 32)
            for g, (t0, nt) in enumerate(GROUPS):
                pe.wait_ge(S("xn_ready"), t0 + nt)
                for k in range(8):
                    q = 8 * g + k
                    if q >= 4:
                        pe.wait_ge(S("uT_act") if q % 2 == 0 else S("uT_dve"), (q - 4) // 2 + 1)
                    for i in range(nt):
                        ins = pe.transpose(bank(q % 4)[:, P * i:P * i + P], xin[t0 + i][:, k::8], ident)
                    ins.then_inc(S("tr_done"), 1)
            pe.wait_ge(S("uT_act"), 12)
            pe.wait_ge(S("uT_dve"), 12)
            pe.wait_ge(S("wf_in"), 16)
            pe.wait_ge(S("mod_ready"), 2)
            for i in range(8):
                c, h = i // 2, i % 2
                if i >= 2:
                    pe.wait_ge(S("f_evac"), i - 1)
                for k in range(8):
                    ins = mm(bank(4 + i % 2), wf[:, k, P * c:P * c + P], uT[:, k, CTX + 512 * h:CTX + 512 * h + 512], start=(k == 0), stop=(k == 7))
                ins.then_inc(S("f_done"), 1)
                m, ph = PIECES[i]
                pe.wait_ge(S(f"piece_in{i % 2}"), 16 * (i // 2 + 1))
                if m in (3, 4):
                    for kc in range(4 * ph, 4 * ph + 4):
                        for k in range(8):
                            ins = ada_cols(piece[i % 2], kc, k, silc[:, 2 * kc:2 * kc + 2], 16 * (m - 1), m == 3 and kc == 0 and k == 0)
                    ins.then_inc(S("piece_used"), 1)
                else:
                    if (m, ph) == (5, 0):
                        pe.wait_ge(S("grow_put"), 2)
                    for kc in range(4 * ph, 4 * ph + 4):
                        for h2 in range(2):
                            ins = mm(bank(6 if h2 == 0 else 0)[0:1, :], silc[:, 2 * kc:2 * kc + 1], piece[i % 2][:, kc % 4, 512 * h2:512 * h2 + 512],
                                     start=(kc == 0), stop=(kc == 7))
                    ins.then_inc(S("piece_used"), 1)
            pe.wait_ge(S("f_evac"), 8)
            for q, (idx, j, cp) in enumerate(ABJOBS):
                if q >= 3:
                    i3, _, c3 = ABJOBS[q - 3]
                    pe.wait_ge(S("ab_act") if i3 % 2 == 0 else S("ab_dve"), 2 * (i3 // 2) + c3 + 1)
                for c in range(2):
                    ins = mm(bank(1 + q % 3)[:, 256 * c:256 * c + 256], fT[:, 2 * cp + c, P * j:P * j + P], cst[:, C_CD:C_CD + 256], start=True, stop=True)
                ins.then_inc(S("ab_done"), 1)
            pe.wait_ge(S("ab_act"), 8)
            pe.wait_ge(S("ab_dve"), 8)
            pe.wait_ge(S("cs_in"), 16)
            pe.wait_ge(S("grow_put"), 4)
            pe.wait_ge(S("mod_ready"), 4)
            for c in range(4):
                if c >= 2:
                    pe.wait_ge(S("qtmp_used"), 2 * (c - 1))
                for g in range(4):
                    odd, sin = g // 2, g % 2
                    w = NOD if odd else NEV
                    o = (2 * NEV if odd else 0) + sin * w
                    for j in range(4):
                        ins = mm(bank((0 if c % 2 else 4) + g)[:, 0:w], EO[:, j if odd else 4 + j, c, P * sin:P * sin + P], CS[:, j, o:o + w], start=(j == 0), stop=(j == 3))
                    ins.then_inc(S("fourier_mm"), 1)
            pe.wait_ge(S("qtmp_used"), 8)
            pe.wait_ge(S("wqk_in"), 16)
            for q, (c, part) in enumerate(QKJOBS):
                if q >= 4:
                    pe.wait_ge(S("cv_evac"), q - 3)
                n, o = (512, CTX + 512 * part) if part < 2 else (CTX, 0)
                for k in range(8):
                    ins = mm(bank(q % 4)[:, 0:n], wqk[:, k, P * c:P * c + P], uT[:, k, o:o + n], start=(k == 0), stop=(k == 7))
                ins.then_inc(S("qk_done"), 1)
            pe.wait_ge(S("wvog_in"), 16)
            for t in range(NT):
                if t >= 2:
                    pe.wait_ge(S("g_evac"), t - 1)
                for k in range(8):
                    ins = mm(bank(6 + t % 2)[:, 0:16], uT[:, k, P * t:P * t + P], wvog[:, k, 1024:1040], start=(k == 0), stop=(k == 7))
                ins.then_inc(S("g_done"), 1)
            pe.wait_ge(S("g_evac"), NT)
            pe.wait_ge(S("cv_evac"), 20)
            for r, (s0, ns) in enumerate(((0, 4), (4, 4), (8, 2))):
                for gate in range(2):
                    q = 2 * r + gate
                    if q >= 4:
                        pe.wait_ge(S("rows_evac"), q - 3)
                    for i in range(ns):
                        tf, tb = tiles_of(s0 + i)
                        o = bank(q % 4)[0:8, P * i:P * i + P]
                        mm(o, G[:, 32 * tf + 8 * gate:32 * tf + 8 * gate + 8], ident, start=True, stop=False)
                        ins = mm(o, G[:, 32 * tb + 16 + 8 * gate:32 * tb + 24 + 8 * gate], rev, start=False, stop=True)
                    ins.then_inc(S("rows_mm"), 1)
            for t in range(NT):
                if t >= 2:
                    pe.wait_ge(S("v_evac"), t - 1)
                for k in range(8):
                    ins = mm(bank(4 + t % 2), uT[:, k, P * t:P * t + P], wvog[:, k, 0:512], start=(k == 0), stop=(k == 7))
                ins.then_inc(S("v_done"), 1)
                if t >= NTC:
                    if t > NTC:
                        pe.wait_ge(S("o_evac"), t - NTC)
                    for k in range(8):
                        ins = mm(bank(6), uT[:, k, P * t:P * t + P], wvog[:, k, 512:1024], start=(k == 0), stop=(k == 7))
                    ins.then_inc(S("o_done"), 1)
            pe.wait_ge(S("silu_done"), 8)
            pe.wait_ge(S("siluc_done"), 4)
            pe.wait_ge(S("rows_evac"), 6)
            for t in range(NT):
                if t >= 2:
                    pe.wait_ge(S("kM_evac"), t - 1)
                for h in range(4):
                    src = kTc[:, h, P * t:P * t + P] if t < NTC else qkT[:, 4 + h, P * (t - NTC):P * (t - NTC) + P]
                    ins = pe.transpose(bank(t % 2)[:, P * h:P * h + P], src, ident)
                ins.then_inc(S("kM_done"), 1)
            pe.wait_ge(S("rows_exp"), 3)
            pe.wait_ge(S("rows_rev"), 4)
            first = True
            for s in range(NT):
                for v, r in enumerate((Ra, Rw, Re)):
                    for d in range(2):
                        src = (Rrev[v] if d else r)[:, P * s:P * s + P]
                        o = s * 48 + 16 * v + 8 * d
                        ins = mm(bank(2)[:, o:o + 8], src, cst[0:8, C_ID:C_ID + 8], start=first, stop=False, skip_group_check=True)
                        first = False
            mm(bank(3)[:, 0:NT * 8], cst[0:8, C_ONE:C_ONE + P], dgl[0:8, :], start=True, stop=True).then_inc(S("cols_mm"), 1)
            pe.wait_ge(S("cols_ready"), 1)
            pe.wait_ge(S("kM_evac"), NT)
            pe.wait_ge(S("v_evac"), NT)
            pe.wait_ge(S("v_ones"), 1)

            def rows_of(r, s, d, n=P):
                src = r[:, P * s:P * s + P]
                return src[:, ::-1] if d else src

            def scores(x):
                s, d, t = JOBS[x + FIRSTX]
                c = t - NTC
                if x >= 2:
                    pe.wait_ge(S("P_ready"), x - 1)
                for h in range(4):
                    mm(bank(x % 2)[:, P * h:P * h + P], qkT[:, 4 + h, P * c:P * c + P], qkT[:, h, P * c:P * c + P], start=True, stop=True)
                db = bank(2 if x % 2 == 0 else 5)
                mk_ = C_MB if d else C_MF
                for h in range(4):
                    mm(db[:, P * h:P * h + P], ident, cst[:, mk_:mk_ + P], start=True, stop=False)
                    r = 4 * d + h
                    ins = mm(db[:, P * h:P * h + P], cst[0:8, C_SEL + P * r:C_SEL + P * r + P], rows_of(Rm, s, d), start=False, stop=True)
                ins.then_inc(S("SD_done"), 1)

            def update(q, half, b):
                s, d, t = JOBS[q]
                for i in range(2):
                    h = 2 * half + i
                    ins = mm(bank(b)[:, 256 * i:256 * i + VW], kM[:, t, P * h:P * h + P], vw[:, q % 2, h], start=True, stop=True)
                ins.then_inc(S("U_half"), 1)
                return ins

            for q, (s, d, t) in enumerate(JOBS):
                x = q - FIRSTX
                if x == 0:
                    scores(0)
                if q >= 1:
                    pe.wait_ge(S("C_half"), 2 * q)
                if x >= 0:
                    for h in range(4):
                        r = 4 * d + h
                        ins = mm(bank(6)[:, P * h:P * h + P], cst[0:8, C_SEL + P * r:C_SEL + P * r + P], rows_of(Ri, s, d), start=True, stop=True)
                    ins.then_inc(S("I_done"), 1)
                    if x + 1 < 16:
                        scores(x + 1)
                pe.wait_ge(S("vw_ready"), q + 1)
                update(q, 0, 7)
                if x >= 0:
                    pe.wait_ge(S("qI_ready"), x + 1)
                update(q, 1, 6)
                if x >= 0:
                    pe.wait_ge(S("P_ready"), x + 1)
                    if x >= 1:
                        pe.wait_ge(S("h_read"), x)
                    for h in range(4):
                        o = psN[:, 512 * (h // 2) + 256 * (h % 2):512 * (h // 2) + 256 * (h % 2) + VW]
                        mm(o, Dt[:, x % 2, P * h:P * h + P], V[:, t, h], start=True, stop=False)
                        ins = mm(o, qI[:, x % 2, P * h:P * h + P], Cst[:, d, h], start=False, stop=True)
                    ins.then_inc(S("N_done"), 1)
            for j in range(NTX):
                pe.wait_ge(S("mix_ready"), j + 1)
                if j >= 2:
                    pe.wait_ge(S("mixt_evac"), j - 1)
                for h in range(4):
                    ins = pe.transpose(bank(j % 2)[:, P * h:P * h + P], H[:, j, P * h:P * h + P], ident)
                ins.then_inc(S("mixt_done"), 1)
            pe.wait_ge(S("mixt_evac"), NTX)
            pe.wait_ge(S("wout_in"), 32)
            for j in range(NTX + 2):
                if j < NTX:
                    if j >= 2:
                        pe.wait_ge(S("y_read"), j - 1)
                    for h in range(2):
                        o = (psN if j % 2 == 0 else psY)[:, 512 * h:512 * h + 512]
                        for k in range(8):
                            ins = mm(o, mixT[:, k, P * j:P * j + P], wout[:, k, 512 * h:512 * h + 512], start=(k == 0), stop=(k == 7))
                    ins.then_inc(S("proj_done"), 1)
                if j >= 2:
                    i = j - 2
                    pe.wait_ge(S("ln_ready"), i + 1)
                    if i >= 1:
                        pe.wait_ge(S("tT_evac"), i)
                    for k in range(8):
                        ins = pe.transpose(bank(k // 4)[:, P * (k % 4):P * (k % 4) + P], lnt[:, i % 2, k::8], ident)
                    ins.then_inc(S("tt_done"), 1)
            pe.wait_ge(S("tT_evac"), NTX)
            pe.wait_ge(S("wr_in"), 32)
            for j in range(NTX):
                for k in range(8):
                    ins = mm(bank(2)[:, NE * j:NE * j + NE], tT[:, k, P * j:P * j + P], wr[:, k, :], start=(k == 0), stop=(k == 7))
            ins.then_inc(S("router_done"), 1)
            pe.wait_ge(S(f"w_in{NBUF - 1}"), 32)

            def shared(j):
                for k in range(8):
                    ins = mm(bank(3 + j % 2), tT[:, k, P * j:P * j + P], wsgu[:, k, :], start=(k == 0), stop=(k == 7))
                ins.then_inc(S("sgu_done"), 1)
                pe.wait_ge(S("s_hx"), j + 1)
                for k in range(2):
                    ins = pe.transpose(bank(7)[:, P * k:P * k + P], hx[:, j % 2, k::2], ident)
                ins.then_inc(S("sht_done"), 1)
                pe.wait_ge(S("s_hT"), j + 1)
                if j >= 1:
                    pe.wait_ge(S("sy_act"), j)
                    pe.wait_ge(S("sy_dve"), j)
                for h in range(2):
                    for k in range(2):
                        ins = mm(bank(5 + h), hT[:, j % 2, k], wsd[:, k, 512 * h:512 * h + 512], start=(k == 0), stop=(k == 1))
                ins.then_inc(S("sdown_done"), 1)

            shared(0)
            pe.wait_ge(S("mask_ready"), 1)
            mkv = mk.rearrange("p (j e) -> p j e", j=8)
            for j in range(NTX):
                for i in range(j + 1):
                    mm(bank(0)[:, NE * j:NE * j + NE], cst[:, C_LT:C_LT + P] if i == j else ones, mkv[:, i, :], start=(i == 0), stop=(i == j))
            for i in range(NTX):
                ins = mm(bank(1)[:, 0:NE], ones, mkv[:, i, :], start=(i == 0), stop=(i == NTX - 1))
            ins.then_inc(S("pos_done"), 1)
            shared(1)
            shared(2)
            pe.wait_ge(S("eb_ready"), 1)
            mm(bank(1)[0:1, 0:P], ebc, ident, start=True, stop=True).then_inc(S("eb_mm"), 1)
            for q in range(64):
                pe.wait_ge(S("onehot_ready"), q + 1)
                mm(bank(2)[:, 0:P], oneP[:, q % 2], oneB[:, q % 2], start=(q == 0), stop=(q == 63)).then_inc(S("onehot_used"), 1)
            for j in range(3, NTX):
                shared(j)
            def x_transposes(p, landed):
                pe.wait_ge(S(f"gathered{p}"), landed)
                for k in range(8):
                    ins = pe.transpose(bank(k // 4)[:, P * (k % 4):P * (k % 4) + P], xg[:, p, 0:D][:, k::8], ident)
                ins.then_inc(S("m_xt"), 1)

            pe.wait_ge(S("table_ready"), 1)
            pe.wait_ge(S("sy_act"), NTX)
            pe.wait_ge(S("sy_dve"), NTX)
            x_transposes(0, 16)
            pe.sem_inc(S("block_done"), 1)
            np_ = pe.value_load(npair[0:1, 0:1], min_val=1, max_val=MAXB // 2)
            with pe.Fori(0, np_) as i:
                for p in range(2):
                    b = 2 * i + p
                    e = pe.value_load(tbl[0:1, bass.ds(b, 1)], min_val=0, max_val=NE - 1)
                    off = pe.value_load(tbl[0:1, bass.ds(b + 2 * P, 1)], min_val=W0, max_val=W0 + (NBUF - 1) * WE)
                    pe.wait_ge(S("weights_ready"), e + 2)
                    pe.wait_ge(S("m_xa"), b + 1)
                    pe.wait_ge(S("m_xb"), b + 1)
                    for k in range(8):
                        ins = mm(bank(3 + p), xT[:, p, k], arena[:, bass.ds(off + 512 * k, 512)], start=(k == 0), stop=(k == 7))
                    ins.then_inc(S("m_gu"), 1)
                    x_transposes(1 - p, 16 * i + 16 * (p + 1))
                    pe.wait_ge(S("m_hx"), b + 1)
                    for k in range(2):
                        ins = pe.transpose(bank(7)[:, P * k:P * k + P], hx[:, p, k::2], ident)
                    ins.then_inc(S("m_ht"), 1)
                    pe.wait_ge(S("m_hT"), b + 1)
                    pe.wait_ge(S("m_ya"), b + 1)
                    pe.wait_ge(S("m_yb"), b + 1)
                    for h in range(2):
                        for k in range(2):
                            ins = mm(bank(5 + h), hT[:, p, k], arena[:, bass.ds(off + (4096 + 1024 * k + 512 * h), 512)], start=(k == 0), stop=(k == 1))
                    ins.then_inc(S("block_done"), 1)

        @block.vector
        def _(dve):
            n = {"c": 0}

            def link(ins):
                n["c"] += 1
                ins.then_inc(S("dve_step"), 1)
                dve.wait_ge(S("dve_step"), n["c"])

            tt, ts, stt = dve.tensor_tensor, dve.tensor_scalar, dve.scalar_tensor_tensor

            def moments(x, o, done):
                dve.bn_stats(stats[:, 0:6], x[:, 0:512])
                link(dve.bn_stats(stats[:, 6:12], x[:, 512:1024]))
                dve.bn_aggr(o, stats[:, :]).then_inc(S(done), 1)

            def norm(t):
                dve.wait_ge(S(f"x_in{XG[t]}"), 16 * XG.count(XG[t]))
                moments(xin[t], mv[:, 2 * t:2 * t + 2], "mv_ready")
                dve.wait_ge(S("rstd_ready"), t + 1)
                ts(xin[t], xin[t], mv[:, 2 * t:2 * t + 1], rstd[:, t:t + 1], ALU.subtract, ALU.mult).then_inc(S("xn_ready"), 1)

            def modulation(i, m):
                dve.wait_ge(S("ada_done" if i < 2 else "piece_used"), 2 if i < 2 else 4)
                o = modc[:, 16 * i:16 * i + 16].rearrange("p (k w) -> p k w", k=8)
                link(tt(o, bank(7)[:, 16 * i:16 * i + 16].rearrange("p (k w) -> p k w", k=8),
                        bada[:, 8 * m:8 * m + 8].unsqueeze(2).to_broadcast([P, 8, 2]), ALU.add))
                if i % 2:
                    o = modc[:, 16 * i:16 * i + 16]
                    link(ts(o, o, 1.0, None, ALU.add))
                dve.sem_inc(S("mod_ready"), 1)

            def u_evac(g):
                t0, nt = GROUPS[g]
                w = 0 if g else 1
                for k in range(1, 8, 2):
                    dve.wait_ge(S("tr_done"), 8 * g + k + 1)
                    ts(uT[:, k, P * t0:P * (t0 + nt)], bank((8 * g + k) % 4)[:, 0:P * nt], modc[:, 16 + 2 * k + w:17 + 2 * k + w],
                       modc[:, 2 * k + w:2 * k + w + 1], ALU.mult, ALU.add).then_inc(S("uT_dve"), 1)

            norm(0)
            norm(1)
            dve.wait_ge(S("const_in"), 32)
            modulation(0, 0)
            modulation(1, 1)
            u_evac(0)
            for t in range(2, NT):
                norm(t)
            u_evac(1)
            u_evac(2)
            modulation(2, 3)
            modulation(3, 4)
            for q, (idx, j, cp) in enumerate(ABJOBS):
                if idx % 2 == 1:
                    dve.wait_ge(S("ab_done"), q + 1)
                    dve.wait_ge(S("ab_act"), 2 * (idx // 2) + cp + 1)
                    lo, hi = EO[:, j - 4, 2 * cp:2 * cp + 2, :], EO[:, j, 2 * cp:2 * cp + 2, :]
                    pp = bank(1 + q % 3).rearrange("p (c n) -> p c n", c=2)
                    tt(hi, lo, pp, ALU.add)
                    tt(lo, lo, pp, ALU.subtract).then_inc(S("ab_dve"), 1)
            for c in range(4):
                bk = 0 if c % 2 else 4
                m = mixT[:, 4 + c, :]
                dve.wait_ge(S("qtmp_ready"), 2 * c + 1)
                tt(m[:, 0:513:2], bank(bk)[:, 0:NEV], qtmp[:, 0, 0:NEV], ALU.subtract)
                tt(m[:, 1022:512:-2], bank(bk)[:, 1:NEV - 1], qtmp[:, 0, 1:NEV - 1], ALU.add).then_inc(S("qtmp_used"), 1)
                dve.wait_ge(S("qtmp_ready"), 2 * c + 2)
                tt(m[:, 1:512:2], bank(bk + 2)[:, 0:NOD], qtmp[:, 1, 0:NOD], ALU.subtract)
                tt(m[:, 1023:512:-2], bank(bk + 2)[:, 0:NOD], qtmp[:, 1, 0:NOD], ALU.add).then_inc(S("qtmp_used"), 1)
            nq = 0
            for c in range(8):
                nq += 2 + (c >= 4)
                dve.wait_ge(S("cv_evac"), nq)
                if c >= 1:
                    dve.wait_ge(S("silu_done"), c)
                for tap in range(9):
                    src = cbuf[c % 2][:, tap // 3:tap // 3 + 16, tap % 3:tap % 3 + 64]
                    w = convw[:, 9 * c + tap:9 * c + tap + 1]
                    ins = ts(cacc, src, w, None, ALU.mult) if tap == 0 else stt(cacc, src, w, cacc, ALU.mult, ALU.add)
                    if tap < 8 or c >= 4:
                        link(ins)
                if c >= 4:
                    if c >= 5:
                        dve.wait_ge(S("siluc_done"), c - 4)
                    for tap in range(3):
                        src = cbufc[:, tap:tap + 256]
                        w = convw[:, 9 * c + 3 + tap:9 * c + 4 + tap]
                        ins = ts(caccc, src, w, None, ALU.mult) if tap == 0 else stt(caccc, src, w, caccc, ALU.mult, ALU.add)
                        if tap < 2:
                            link(ins)
                ins.then_inc(S("conv_done"), 1)
            link(dve.memset(G[:, :], 0.0))
            for t in range(NT):
                dve.wait_ge(S("g_done"), t + 1)
                src = bank(6 + t % 2)[:, 0:16].rearrange("p (d g h) -> p d g h", d=2, g=2)
                for d in range(2):
                    o = G[:, 32 * t + 16 * d:32 * t + 16 * d + 16].rearrange("p (g x) -> p g x", g=2)[:, :, 4 * d:4 * d + 4]
                    ins = dve.tensor_copy(o, src[:, d])
                ins.then_inc(S("g_evac"), 1)
            dve.wait_ge(S("silu_done"), 8)
            dve.wait_ge(S("siluc_done"), 4)
            for r, (s0, ns) in enumerate(((0, 4), (4, 4), (8, 2))):
                for gate in range(2):
                    q = 2 * r + gate
                    dve.wait_ge(S("rows_mm"), q + 1)
                    ts((Rf if gate else Ra)[:, P * s0:P * (s0 + ns)], bank(q % 4)[0:8, 0:P * ns], gateb[0:8, gate:gate + 1], None, ALU.add).then_inc(S("rows_evac"), 1)
            dve.wait_ge(S("rows_evac"), 6)
            link(dve.memset(mprev[0:8, 0:1], 0.0))
            link(dve.memset(zrow[0:8, :], 0.0))
            dve.wait_ge(S("rl_step"), 3)
            link(stt(Rl, Rf, 0.0, Rl, ALU.min, ALU.subtract))
            for s in range(NT):
                ins = dve.tensor_tensor_scan(Rb[:, P * s:P * s + P], Rl[:, P * s:P * s + P], zrow[0:8, :], 0.0, ALU.add, ALU.add)
            link(ins)
            link(tt(Ra, Ra, Rb, ALU.subtract))
            for s in range(NT):
                sl_ = slice(P * s, P * s + P)
                link(dve.tensor_tensor_scan(Rm[:, sl_], Ra[:, sl_], Ra[:, sl_], mprev[0:8, s:s + 1], ALU.max, ALU.max))
                link(tt(mprev[0:8, s + 1:s + 2], Rb[:, P * s + P - 1:P * s + P], Rm[:, P * s + P - 1:P * s + P], ALU.add))

            def v3(r):
                return r.rearrange("p (s n) -> p s n", s=NT)

            dve.wait_ge(S("v_done"), NT)
            dve.wait_ge(S("o_done"), NTX)
            tt(v3(Rw), v3(Ra), v3(Rm)[:, :, P - 1:P].to_broadcast([8, NT, P]), ALU.subtract).then_inc(S("wargs_ready"), 1)
            stt(Re, Rb, -1.0, Rm, ALU.mult, ALU.subtract).then_inc(S("wargs_ready"), 1)
            tt(v3(Ri), mprev[0:8, 0:NT].unsqueeze(2).to_broadcast([8, NT, P]), v3(Rm), ALU.subtract).then_inc(S("wargs_ready"), 1)
            dve.wait_ge(S("wargs_ready"), 3)
            link(ts(Rm, Rm, -1.0, None, ALU.mult))
            dve.wait_ge(S("rows_exp"), 3)
            tt(dgl[0:8, :].rearrange("p (s r) -> p s r", s=NT), cst[0:8, C_ID:C_ID + 8].unsqueeze(1).to_broadcast([8, NT, 8]),
               v3(Ri)[:, :, P - 1:P].to_broadcast([8, NT, 8]), ALU.mult).then_inc(S("rows_rev"), 1)
            dve.wait_ge(S("cols_mm"), 1)
            link(dve.tensor_copy(COL[:, :], bank(2)[:, 0:NT * 48]))
            link(dve.memset(Cst.rearrange("p b h n -> p (b h n)"), 0.0))
            dve.tensor_copy(DEC[:, :], bank(3)[:, 0:NT * 8]).then_inc(S("cols_ready"), 1)
            dve.wait_ge(S("cols_ready"), 1)
            for q, (s, d, t) in enumerate(JOBS):
                x = q - FIRSTX
                if x >= 0:
                    c = t - NTC
                    dve.wait_ge(S("I_done"), x + 1)
                    if x >= 2:
                        dve.wait_ge(S("N_done"), x - 1)
                    tt(qI[:, x % 2].rearrange("p (h n) -> p h n", h=4), qkT[:, 0:4, P * c:P * c + P],
                       bank(6).rearrange("p (h n) -> p h n", h=4), ALU.mult).then_inc(S("qI_ready"), 1)
                    dve.wait_ge(S("D_ready"), x + 1)
                    stt(Dt[:, x % 2], bank(x % 2), KSCALE, Dt[:, x % 2], ALU.mult, ALU.mult).then_inc(S("P_ready"), 1)
                    dve.wait_ge(S("N_done"), x + 1)
                    num = psN.rearrange("p (b i n) -> p b i n", b=2, i=2)
                    den4 = den[:, :].rearrange("p (b i) -> p b i", b=2)
                    c0 = s * 48 + 32 + 12 * d
                    e4 = COL[:, c0:c0 + 4].rearrange("p (b i) -> p b i", b=2)
                    link(stt(den4, num[:, :, :, DH], -1.0, e4, ALU.mult, ALU.max))
                    link(tt(den4, num[:, :, :, DH], den4, ALU.max))
                    link(dve.reciprocal(rec[:, :], den[:, :]))
                    r4 = rec[:, :].rearrange("p (b i) -> p b i", b=2).unsqueeze(3).to_broadcast([P, 2, 2, DH])
                    tgt = H[:, c] if s - NTC < 4 else htmp
                    ins = tt(tgt.rearrange("p (b i n) -> p b i n", b=2, i=2), num[:, :, :, 0:DH], r4, ALU.mult)
                    ins.then_inc(S("h_read"), 1)
                    if s - NTC >= 4:
                        dve.wait_ge(S("h_read"), x + 1)
                        link(tt(H[:, c], H[:, c], htmp, ALU.add))
                for half in range(2):
                    dve.wait_ge(S("U_half"), 2 * q + half + 1)
                    for i in range(2):
                        h = 2 * half + i
                        dc = DEC[:, 8 * s + 4 * d + h:8 * s + 4 * d + h + 1]
                        ins = stt(Cst[:, d, h], Cst[:, d, h], dc, bank(6 if half else 7)[:, 256 * i:256 * i + VW], ALU.mult, ALU.add)
                    ins.then_inc(S("C_half"), 1)
            dve.wait_ge(S("C_half"), 2 * NJ)
            dve.sem_inc(S("h_done"), 16)
            dve.wait_ge(S("wout_in"), 32)
            link(ts(hgB, hgB, 0.5, None, ALU.mult))
            for j in range(NTX):
                for h in range(4):
                    ins = dve.bn_stats(hst[:, 6 * h:6 * h + 6], H[:, j, P * h:P * h + P])
                link(ins)
                for h in range(4):
                    ins = dve.bn_aggr(hmv[:, j % 2, h], hst[:, 6 * h:6 * h + 6])
                ins.then_inc(S("hmv_ready"), 1)
                link(stt(og, O[:, j], 1.0, hgB, ALU.add, ALU.mult))
                dve.wait_ge(S("hrstd_ready"), j + 1)
                for h in range(4):
                    hh = H[:, j, P * h:P * h + P]
                    ins = ts(hh, hh, hmv[:, j % 2, h, 0:1], hrstd[:, j % 2, h:h + 1], ALU.subtract, ALU.mult)
                link(ins)
                tt(H[:, j], H[:, j], og, ALU.mult).then_inc(S("mix_ready"), 1)
            dve.wait_ge(S("rows1_in"), 64)
            dve.wait_ge(S("mixt_done"), NTX)
            link(tt(g1B, g1B, ytmp[:, 0], ALU.add))
            for j in range(NTX + 1):
                if j < NTX:
                    y = ytmp[:, j % 2]
                    dve.wait_ge(S("proj_done"), j + 1)
                    tt(y, psN if j % 2 == 0 else psY, g1B, ALU.mult).then_inc(S("y_read"), 1)
                    dve.wait_ge(S("y_read"), j + 1)
                    dve.wait_ge(S(f"xres_in{j % 2}"), 16 * (j // 2 + 1))
                    stt(y, xres[:, j % 2], ALPHA, y, ALU.mult, ALU.add).then_inc(S("res_used"), 1)
                    dve.wait_ge(S("res_used"), j + 1)
                    moments(y, mvj[:, j % 2], "y_mv")
                    dve.wait_ge(S("y_rstd"), j + 1)
                    ts(y, y, mvj[:, j % 2, 0:1], rstd[:, j % 2:j % 2 + 1], ALU.subtract, ALU.mult).then_inc(S("y_norm"), 1)
                if j >= 1:
                    i = j - 1
                    dve.wait_ge(S("y_gain"), i + 1)
                    link(tt(x1[:, i], ytmp[:, i % 2], lb1, ALU.add))
                    moments(x1[:, i], mvk[:, i % 2], "x1_mv")
                    dve.wait_ge(S("x1_rstd"), i + 1)
                    if i >= 2:
                        dve.wait_ge(S(f"t_out{i % 2}"), 16 * (i // 2))
                        dve.wait_ge(S("tt_done"), i - 1)
                    ts(lnt[:, i % 2], x1[:, i], mvk[:, i % 2, 0:1], rstd[:, 2 + i % 2:3 + i % 2], ALU.subtract, ALU.mult).then_inc(S("ln_ready"), 1)
            def t3(x):
                return x.rearrange("p (j e) -> p j e", j=8)

            def shared(j):
                dve.wait_ge(S("s_sg"), j + 1)
                tt(hx[:, j % 2], sg[:, j % 2], bank(3 + j % 2)[:, DE:2 * DE], ALU.mult).then_inc(S("s_hx"), 1)

            def shared_y(j):
                dve.wait_ge(S("sdown_done"), j + 1)
                if j >= 2:
                    dve.wait_ge(S(f"acc_out{j % 2}"), 16 * (j // 2))
                dve.tensor_copy(yB[:, j % 2, 512:1024], bank(6)).then_inc(S("sy_dve"), 1)

            dve.wait_ge(S("sc_ready"), 1)
            dve.wait_ge(S("wr_in"), 32)
            link(dve.memset(zr, 0.0))
            link(tt(t3(bs), t3(sc), rbB.unsqueeze(1).to_broadcast([P, 8, NE]), ALU.add))
            for j in range(8):
                link(dve.max(m8[:, 8 * j:8 * j + 8], bs[:, NE * j:NE * j + NE]))
                link(dve.match_replace(rp[:, NE * j:NE * j + NE], m8[:, 8 * j:8 * j + 8], bs[:, NE * j:NE * j + NE], -BIG))
            ts(mk, rp, -BIG, None, ALU.is_equal).then_inc(S("mask_ready"), 1)
            dve.wait_ge(S("mask_ready"), 1)
            shared(0)
            link(tt(wt, sc, mk, ALU.mult))
            link(dve.tensor_reduce(ssum, t3(wt), AX, ALU.add))
            link(dve.reciprocal(ssum, ssum))
            link(ts(ssum, ssum, ROUTED, None, ALU.mult))
            tt(t3(wt), t3(wt), ssum.unsqueeze(2).to_broadcast([P, 8, NE]), ALU.mult).then_inc(S("wt_ready"), 1)
            shared_y(0)
            dve.wait_ge(S("pos_done"), 1)
            link(ts(cnti, bank(1)[:, 0:NE], float(P - 1), None, ALU.add))
            link(ts(cnti, cnti, 7, None, ALU.arith_shift_right))
            link(dve.tensor_copy(nbf, cnti))
            link(dve.tensor_tensor_scan(bend, nbf, zr, 0.0, ALU.add, ALU.add))
            link(tt(bbase, bend, nbf, ALU.subtract))
            link(ts(bbase, bbase, float(P), 1.0, ALU.mult, ALU.add))
            link(ts(n2, bend, cst[:, C_P:C_P + 1], None, ALU.is_le))
            link(dve.tensor_reduce(ebc, n2, AX, ALU.add))
            ts(ebc, ebc, float(NE - 1), None, ALU.min).then_inc(S("eb_ready"), 1)
            link(tt(t3(sl), t3(bank(0)), bbase.unsqueeze(1).to_broadcast([P, 8, NE]), ALU.add))
            link(tt(sl, sl, mk, ALU.mult))
            shared(1)
            for j in range(8):
                ins = dve.max(m8[:, 8 * j:8 * j + 8], sl[:, NE * j:NE * j + NE])
            link(ins)
            link(ts(s8i, m8, -1.0, None, ALU.add))
            link(ts(b8i, s8i, 7, None, ALU.arith_shift_right))
            link(ts(s8i, s8i, P - 1, None, ALU.bitwise_and))
            link(dve.tensor_copy(p8, s8i))
            link(dve.tensor_copy(b8, b8i))
            shared_y(1)
            shared(2)
            shared_y(2)
            link(dve.memset(endi[:, 0:NBUF], 1))
            link(ts(endi[:, NBUF:NE], bend[0:1, 0:NE - NBUF], 1.0, None, ALU.add))
            link(ts(npair[:, :], bend[0:1, NE - 1:NE], 1.0, None, ALU.add))
            link(ts(npair[:, :], npair[:, :], 1, None, ALU.arith_shift_right))
            dve.wait_ge(S("eb_mm"), 1)
            link(dve.tensor_copy(tbl[:, 0:P], bank(1)[0:1, 0:P]))
            link(ts(tbl[:, P:2 * P], tbl[:, 0:P], NBUF - 1, None, ALU.bitwise_and))
            link(ts(tbl[:, 2 * P:3 * P], tbl[:, P:2 * P], float(WE), float(W0), ALU.mult, ALU.add))
            for q in range(64):
                j, k = q // 8, q % 8
                if q >= 2:
                    dve.wait_ge(S("onehot_used"), q - 1)
                ts(oneP[:, q % 2], iota, p8[:, q:q + 1], None, ALU.is_equal)
                ts(oneB[:, q % 2], iota, b8[:, q:q + 1], cst[:, C_TOK + j:C_TOK + j + 1], ALU.is_equal, ALU.mult).then_inc(S("onehot_ready"), 1)
            dve.wait_ge(S("onehot_used"), 64)
            pad = cst[:, C_PADROW:C_PADROW + 1]
            link(ts(Ttmp[:, 0], bank(2)[:, 0:P], 0.0, pad, ALU.is_equal, ALU.mult))
            link(tt(Ttmp[:, 1], bank(2)[:, 0:P], Ttmp[:, 0], ALU.add))
            link(ts(idxT[:, 0:P], Ttmp[:, 1], -1.0, None, ALU.add))
            ts(idxT[:, P:P + 2], cst[:, C_PADROW:C_PADROW + 1].to_broadcast([P, 2]), -1.0, None, ALU.add).then_inc(S("idx_ready"), 1)
            dve.wait_ge(S("idx_ready"), 1)
            dve.sem_inc(S("table_ready"), 1)
            for j in range(3, NTX):
                shared(j)
                shared_y(j)
            def x_evac(p):
                for k in range(4, 8):
                    ins = ts(xT[:, p, k], bank(1)[:, P * (k - 4):P * (k - 4) + P], modc[:, 48 + 2 * k:49 + 2 * k], modc[:, 32 + 2 * k:33 + 2 * k], ALU.mult, ALU.add)
                ins.then_inc(S("m_xb"), 1)

            dve.wait_ge(S("m_xt"), 1)
            x_evac(0)
            dve.sem_inc(S("m_yb"), 1)
            np_ = dve.value_load(npair[0:1, 0:1], min_val=1, max_val=MAXB // 2)
            with dve.Fori(0, np_) as i:
                for p in range(2):
                    b1 = 2 * i + (p + 1)
                    e = dve.value_load(tbl[0:1, bass.ds(2 * i + p, 1)], min_val=0, max_val=NE - 1)
                    dve.wait_ge(S("m_sg"), b1)
                    stt(hx[:, p], bank(3 + p)[:, DE:2 * DE], xg[:, p, D:XW][:, bass.ds(e, 1)], sg[:, p], ALU.mult, ALU.mult).then_inc(S("m_hx"), 1)
                    dve.wait_ge(S("m_xt"), 2 * i + (p + 2))
                    x_evac(1 - p)
                    dve.wait_ge(S("block_done"), 2 * i + (p + 2))
                    dve.wait_ge(S("y_free"), 2 * i + (p + 1))
                    dve.tensor_copy(yB[:, p, 512:1024], bank(6)).then_inc(S("m_yb"), 1)
            dve.wait_ge(S("rows2_in"), 64)
            link(tt(g2B, g2B, acc_tmp, ALU.add))
            for j in range(NTX + 1):
                if j < NTX:
                    y = acc_in[j]
                    dve.wait_ge(S(f"accin{j // 2}"), 32)
                    link(tt(y, y, g2B, ALU.mult))
                    link(stt(y, x1[:, j], ALPHA, y, ALU.mult, ALU.add))
                    moments(y, mvj[:, j % 2], "o_mv")
                    dve.wait_ge(S("o_rstd"), j + 1)
                    ts(y, y, mvj[:, j % 2, 0:1], rstd[:, j % 2:j % 2 + 1], ALU.subtract, ALU.mult).then_inc(S("o_norm"), 1)
                if j >= 1:
                    dve.wait_ge(S("o_gain"), j)
                    tt(acc_in[j - 1], acc_in[j - 1], lb2, ALU.add).then_inc(S("out_ready"), 1)


def kernel(**inputs):
    import concourse.bacc as bacc
    from concourse.bass_utils import run_bass_kernel_spmd

    def flat(name):
        return np.asarray(inputs[name])

    const, dft = constant_tiles()
    w_in = flat("w_in")[0]
    cc = np.stack([flat("c")[0], flat("c_ctx")], axis=-1).reshape(P, 16)
    gate_b = flat("gate_b")[0]
    arrays = {
        "toks": np.concatenate([flat("ctx")[0], flat("x")[0]], axis=0),
        "cc": cc,
        "const": const,
        "dft": dft,
        "w_ada": flat("w_ada")[0],
        "b_ada": flat("b_ada"),
        "w_qk": w_in[:, 0:2 * DM],
        "w_vog": w_in[:, 2 * DM:4 * DM + 16],
        "w_f": w_in[:, 4 * DM + 16:],
        "conv_wt": flat("conv_w")[0].reshape(9, 8, P).transpose(2, 1, 0).reshape(P, 72),
        "conv_bt": flat("conv_b")[0].reshape(8, P).T,
        "gate_bt": gate_b.transpose(0, 2, 1).reshape(8, 2),
        "head_g": flat("head_g"),
        "w_out": flat("w_out")[0],
        "ln1_g": flat("ln1_g"), "ln1_b": flat("ln1_b"), "ln2_g": flat("ln2_g"), "ln2_b": flat("ln2_b"),
        "w_router": flat("w_router")[0],
        "router_bias": flat("router_bias"),
        "w_gu": flat("w_expert_gu")[0].reshape(NE * P, 8 * 2 * DE),
        "w_dn": flat("w_expert_down")[0].reshape(NE * P, 2 * D),
        "w_shared_gu": flat("w_shared_gu")[0],
        "w_shared_down": flat("w_shared_down")[0],
    }
    nc = bacc.Bacc("TRN2", target_bir_lowering=False, num_devices=1)
    feed, aps = {}, {}
    for name, v in arrays.items():
        v = np.ascontiguousarray(v)
        feed[f"in_{name}"] = v
        aps[name] = nc.dram_tensor(f"in_{name}", v.shape, F32, kind="ExternalInput").ap()
    out = nc.dram_tensor("out_0", (SEQ, D), F32, kind="ExternalOutput").ap()
    build(nc, aps, out)
    r = run_bass_kernel_spmd(nc, [feed], core_ids=[0])
    return r.results[0]["out_0"].reshape(1, SEQ, D)
```

```python
from contextlib import ExitStack

import numpy as np

import concourse.bass as bass
from concourse import mybir

P = 128
D = 1024
KT = D // P
SEQ = 1024
CTX = 256
NTC = CTX // P
NTX = SEQ // P
NT = NTC + NTX
HEADS = 4
DH = 128
DM = HEADS * DH
DF = 512
VW = DH + 1
NE = 64
TOPK = 8
DE = 256
ROWS_OUT = SEQ + P
XW = D + NE
MAXB = P
NBUF = 2
WE = KT * 2 * DE + (DE // P) * D
ALPHA = 2.0 ** 0.25
EPS = 1e-5
KSCALE = DH ** -0.5
ROUTED = 2.5
BIG = 1e30
NEV = SEQ // 4 + 1
NOD = SEQ // 4
GW = 66
GH = 18

ALU = mybir.AluOpType
ACT = mybir.ActivationFunctionType
AX = mybir.AxisListType.X
F32 = mybir.dt.float32
I32 = mybir.dt.int32
U32 = mybir.dt.uint32
F32R = mybir.dt.float32r

C_ID, C_REV, C_MF, C_MB, C_ONE, C_LT, C_IOTA, C_SEL = (i * P for i in range(8))
C_HALF = C_SEL + 8 * P
C_PADROW = C_HALF + 16
C_TOK = C_PADROW + 1
C_P = C_TOK + 8
C_CD = C_P + 7
C_END = C_CD + 256
ARENA = 48188


def constant_tiles():
    p = np.arange(P)
    c = np.zeros((P, C_END), np.float32)
    c[p, C_ID + p] = 1
    c[p, C_REV + P - 1 - p] = 1
    c[:, C_MF:C_MF + P] = np.where(p[:, None] <= p[None, :], 0, -BIG)
    c[:, C_MB:C_MB + P] = np.where(p[:, None] >= p[None, :], 0, -BIG)
    c[:, C_ONE:C_ONE + P] = 1
    c[:, C_LT:C_LT + P] = p[:, None] < p[None, :]
    c[:, C_IOTA:C_IOTA + P] = p[None, :]
    for r in range(8):
        c[r, C_SEL + r * P:C_SEL + (r + 1) * P] = 1
    c[:, C_HALF:C_HALF + 16] = -0.5
    c[:, C_PADROW] = SEQ + p + 1
    c[:, C_TOK:C_TOK + 8] = p[:, None] + P * np.arange(8)[None, :] + 1
    c[:, C_P] = p
    g = 64
    m = np.arange(g)
    ang = 2 * np.pi * (np.outer(m, m) % g) / g
    scale = 1.0 / np.sqrt(SEQ * g)
    for b in range(2):
        s = slice(b * g, (b + 1) * g)
        c[s, C_CD + b * g:C_CD + (b + 1) * g] = np.cos(ang) * scale
        c[s, C_CD + P + b * g:C_CD + P + (b + 1) * g] = np.sin(ang) * scale
    n = np.arange(SEQ // 2)
    ev = 2 * np.pi * (np.outer(n, 2 * np.arange(NEV)) % SEQ) / SEQ
    od = 2 * np.pi * (np.outer(n, 2 * np.arange(NOD) + 1) % SEQ) / SEQ
    dft = np.concatenate([np.cos(ev), np.sin(ev), np.cos(od), np.sin(od)], axis=1).astype(np.float32)
    return c, np.ascontiguousarray(dft)


def build(nc, a, out):
    ctx = ExitStack()
    with ctx:
        def sb(name, cols, dt=F32, parts=P):
            return ctx.enter_context(nc.sbuf_tensor(name, [parts, cols], dt))

        sems = {}

        def sem(name):
            if name not in sems:
                sems[name] = ctx.enter_context(nc.semaphore(name))
            return sems[name]

        cst = sb("cst", C_END)
        A0, B0, C0, D0 = 0, 10240, 19496, 39996
        arena_base = (nc.sbuf_base + 31) // 32 * 32
        arena = sb("arena", ARENA)

        def at(o, n):
            return arena[:, o:o + n]

        ident = cst[:, C_ID:C_ID + P]
        rev = cst[:, C_REV:C_REV + P]
        ones = cst[:, C_ONE:C_ONE + P]
        iota = cst[:, C_IOTA:C_IOTA + P]

        ccol = sb("ccol", 16)
        silc = sb("silc", 16)
        bada = sb("bada", 48)
        modc = sb("modc", 4 * 16)
        convw = sb("convw", 8 * 9)
        convb = sb("convb", 8)
        gateb = sb("gateb", 2)
        stats = sb("stats", 12)
        mv = sb("mv", 2 * NT)
        veps = sb("veps", NT)
        rstd = sb("rstd", NT)
        G = sb("G", NT * 32)
        mprev = sb("mprev", NT + 1)
        COL = sb("COL", NT * 48)
        dgl = sb("dgl", NT * 8)
        DEC = sb("DEC", NT * 8)
        den = sb("den", 4)
        rec = sb("rec", 4)
        rowt = sb("rowt", 512, parts=1)
        idxg = sb("idxg", 2, U32)
        idxs = sb("idxs", 2, U32)
        zrow = sb("zrow", P, parts=8)
        hst = sb("hst", 24)
        hmv = sb("hmv", 16)[:, :].rearrange("p (b h n) -> p b h n", b=2, h=4)
        hveps = sb("hveps", 8)[:, :].rearrange("p (b h) -> p b h", b=2)
        hrstd = sb("hrstd", 8)[:, :].rearrange("p (b h) -> p b h", b=2)
        mvj = sb("mvj", 4)[:, :].rearrange("p (b n) -> p b n", b=2)
        mvk = sb("mvk", 4)[:, :].rearrange("p (b n) -> p b n", b=2)

        def overlay(name, o, cols, dt):
            return nc.alloc_sbuf_tensor_at(name, [P, cols], dt, offset=arena_base + 4 * o)

        psum = ctx.enter_context(nc.psum_tensor("psum", [P, 8 * 512], F32))
        psN = psum[:, 3 * 512:5 * 512]
        psY = psum[:, 5 * 512:7 * 512]

        def bank(i):
            return psum[:, 512 * i:512 * i + 512]

        ada = [at(C0, 8192).rearrange("p (k n) -> p k n", k=8), at(C0 + 8192, 8192).rearrange("p (k n) -> p k n", k=8)]
        piece = [at(D0, 4096).rearrange("p (k n) -> p k n", k=4), at(D0 + 4096, 4096).rearrange("p (k n) -> p k n", k=4)]
        xin = [at(B0 + 1024 * (t % 9), 1024) for t in range(NT)]
        uT = at(A0, 10240).rearrange("p (k n) -> p k n", k=8)
        wf = at(C0 + 16396, 4096).rearrange("p (k n) -> p k n", k=8)
        fT = at(C0, 4096).rearrange("p (c n) -> p c n", c=4)
        EO = at(C0 + 4096, 8192).rearrange("p (s c n) -> p s c n", s=8, c=4)
        CSW = 2 * NEV + 2 * NOD
        CS = at(C0 + 12288, 4 * CSW).rearrange("p (j n) -> p j n", j=4)
        qtmp = at(C0 + 16400, 2 * 260).rearrange("p (b n) -> p b n", b=2)
        mixT = at(D0, 8192).rearrange("p (k n) -> p k n", k=8)
        wqk = at(B0, 8192).rearrange("p (k n) -> p k n", k=8)
        cbuf = [at(D0 + 1188 * i, 1188).rearrange("p (r c) -> p r c", r=GH) for i in range(2)]
        cacc = at(D0 + 2376, 1024).rearrange("p (r c) -> p r c", r=16)
        cbufc = at(D0 + 3400, 258)
        caccc = at(D0 + 3658, 256)
        qkT = at(C0, 8192).rearrange("p (c n) -> p c n", c=8)
        kTc = at(C0 + 8192, 1024).rearrange("p (c n) -> p c n", c=4)
        wvog = at(C0 + 9216, 8320).rearrange("p (k n) -> p k n", k=8)
        V = at(B0, NT * 4 * VW).rearrange("p (t h n) -> p t h n", t=NT, h=4)
        O = at(B0 + NT * 4 * VW, 4096).rearrange("p (t n) -> p t n", t=NTX)
        NR = NT * P

        def row(o):
            return arena[0:8, o:o + NR]

        Ra, Rf, Rl = row(D0), row(D0 + NR), row(D0 + 2 * NR)
        Ri, Rw, Re = (row(C0 + 9216 + i * NR) for i in range(3))
        Rb, Rm = (row(C0 + 17536 + i * NR) for i in range(2))
        Rrev = [row(C0 + 9216 + (3 + i) * NR) for i in range(3)]
        kM = at(A0, 5120).rearrange("p (t n) -> p t n", t=NT)
        H = at(A0 + 5120, 4096).rearrange("p (t n) -> p t n", t=NTX)
        qI = at(A0 + 9216, 1024).rearrange("p (b n) -> p b n", b=2)
        HB = C0 + 9216 + 3 * NR
        Dt = at(HB, 1024).rearrange("p (b n) -> p b n", b=2)
        vw = at(HB + 1024, 1032).rearrange("p (b h n) -> p b h n", b=2, h=4)
        Cst = at(HB + 2056, 1032).rearrange("p (b h n) -> p b h n", b=2, h=4)
        htmp = at(HB + 3088, 512)
        hgB = at(HB, 512)
        og = at(HB + 512, 512)
        wout = at(C0, 8192).rearrange("p (k n) -> p k n", k=8)
        x1 = at(A0, 8192).rearrange("p (t n) -> p t n", t=NTX)
        g1B, lg1, lb1 = (at(B0 + i * 1024, 1024) for i in range(3))
        sc2B, sh2B = (at(B0 + 7168 + i * 1024, 1024) for i in range(2))
        diag = at(C0 + 16384, 2048).rearrange("p (v k n) -> p v k n", v=2, k=8)
        xres = at(B0 + 3072, 2048).rearrange("p (b n) -> p b n", b=2)
        ytmp = at(B0 + 5120, 2048).rearrange("p (b n) -> p b n", b=2)
        tT = at(C0 + 8192, 8192).rearrange("p (k n) -> p k n", k=8)
        lnt = at(C0 + 16384, 2 * 1024).rearrange("p (b n) -> p b n", b=2)
        wr = at(2 * WE, 512).rearrange("p (k n) -> p k n", k=8)
        rbB = at(2 * WE + 512, 64)
        KB = 2 * WE + 1024
        sc, bs, rp, mk, wt, sl, t512, t512b = (at(KB + i * 512, 512) for i in range(8))
        KC = KB + 8 * 512
        m8 = at(KC, 64)
        s8 = at(KC + 64, 64)
        ssum = at(KC + 128, 8)
        cnt, nbf, bend, bbase, zr, n2 = (at(KC + 136 + 64 * i, 64) for i in range(6))
        cnti = arena[:, KC + 520:KC + 584].bitcast(I32)
        p8 = at(KC + 584, 64)
        b8 = at(KC + 648, 64)
        s8i = arena[:, KC + 712:KC + 776].bitcast(I32)
        b8i = arena[:, KC + 776:KC + 840].bitcast(I32)
        ebc = at(KC + 840, 1)
        zpad = at(KC + 848, XW)
        oneP = at(C0 + 18432, 256).rearrange("p (b n) -> p b n", b=2)
        oneB = at(C0 + 18688, 256).rearrange("p (b n) -> p b n", b=2)
        Ttmp = at(C0 + 18944, 256).rearrange("p (b n) -> p b n", b=2)
        idxT = sb("idxT", P + 2, U32)
        tbl = sb("tbl", 3 * P + 2, I32, parts=1)
        T_WORD, T_E, T_NEW = 0, P + 2, 2 * P + 2
        tblf = sb("tblf", P, parts=1)
        pairs_rest = sb("pairs_rest", 1, I32, parts=1)
        sgL, hxL, hTL = (at(A0 + 8192 + 512 * i, 512).rearrange("p (b n) -> p b n", b=2) for i in range(3))
        hTL = hTL.rearrange("p b (k n) -> p b k n", k=2)
        wsgu = at(D0, 4096).rearrange("p (k n) -> p k n", k=8)
        wsd = at(D0 + 4096, 2048).rearrange("p (k n) -> p k n", k=2)
        sg, hx = (at(C0 + 4 * WE + 512 * i, 512).rearrange("p (b n) -> p b n", b=2) for i in range(2))
        raw = overlay("raw_weights", A0, 2 * WE, F32)
        wsplit = overlay("split_weights", C0, 4 * WE, F32R)
        xh = overlay("split_rows", 2 * WE, 4 * 1024 + 4 * P, F32R)
        xTh = [xh[:, 2048 * i:2048 * i + 1024] for i in range(2)]
        xTl = [xh[:, 2048 * i + 1024:2048 * i + 2048] for i in range(2)]
        hTh, hTl = xh[:, 4096:4096 + 2 * P], xh[:, 4096 + 2 * P:4096 + 4 * P]
        xg = at(2 * WE + 4096 + 4 * P, 2 * XW).rearrange("p (b n) -> p b n", b=2)
        assert 2 * WE + 4096 + 4 * P + 2 * XW <= C0 and C0 + 4 * WE + 1024 <= D0 + 6144
        yB = at(D0 + 6144, 2048).rearrange("p (b n) -> p b n", b=2)
        gcol = sb("gcol", 2)
        g2B, lg2, lb2, acc_tmp = (at(A0 + i * 1024, 1024) for i in range(4))
        acc_in = [at(C0 + 1024 * i, 1024) for i in range(8)]
        x1_in = [at(A0 + 4096 + 1024 * i, 1024) for i in range(8)]

        x1_dram = nc.dram_tensor("x1_rows", [SEQ, D], F32, kind="Internal").ap()
        t_dram = nc.dram_tensor("t_rows", [ROWS_OUT, XW], F32, kind="Internal").ap()
        acc = nc.dram_tensor("moe_sum", [ROWS_OUT, D], F32, kind="Internal").ap()
        grow = nc.dram_tensor("gate_rows", [2, D], F32, kind="Internal").ap()

        def cols(t, o, n):
            return t[:, o:o + n] if isinstance(o, int) else t[:, bass.ds(o, n)]

        def word_of(engine, b):
            return engine.value_load(cols(tbl, b, 1), min_val=0, max_val=127)

        def drows(w, n0, n1):
            return w.rearrange("(p k) n -> p k n", k=8)[:, :, n0:n1]

        def tiles_of(s):
            return (s, NTC - 1 - s) if s < NTC else (s, NTC + NT - 1 - s)

        ABJOBS = [(i, j, cp) for i, j in enumerate((0, 4, 1, 5, 2, 6, 3, 7)) for cp in range(2)]
        QKJOBS = [(c, part) for c in range(8) for part in range(3 if c >= 4 else 2)]
        JOBS = [(s, d, tiles_of(s)[d]) for s in range(NT) for d in range(2)]
        NJ = len(JOBS)
        FIRSTX = 2 * NTC
        PIECES = [(3, 0), (3, 1), (4, 0), (4, 1), (2, 0), (2, 1), (5, 0), (5, 1)]
        XG = [0] * 2 + [1] * 4 + [2] * 4
        GROUPS = [(0, 2), (2, 4), (6, 4)]

        block = ctx.enter_context(nc.Block())
        S = sem

        @block.sync
        def _(sp):
            sp.dma_start(ccol[:, :], a["cc"]).then_inc(S("c_in"), 16)
            sp.dma_start(cst[:, :], a["const"]).then_inc(S("const_in"), 16)
            sp.dma_start(bada[:, :].rearrange("p (m k) -> p m k", m=6), a["b_ada"].rearrange("o (m p k) -> p (o m) k", m=6, k=8)).then_inc(S("const_in"), 16)
            for t in range(3):
                sp.dma_start(xin[t], a["toks"][P * t:P * t + P, :]).then_inc(S(f"x_in{XG[t]}"), 16)
            for m in range(2):
                sp.dma_start(ada[m], drows(a["w_ada"], m * D, (m + 1) * D)).then_inc(S(f"ada_in{m}"), 16)
            for t in range(3, 9):
                sp.dma_start(xin[t], a["toks"][P * t:P * t + P, :]).then_inc(S(f"x_in{XG[t]}"), 16)
            sp.dma_start(wf, drows(a["w_f"], 0, DF)).then_inc(S("wf_in"), 16)
            sp.wait_ge(S("tr_done"), 8)
            sp.dma_start(xin[9], a["toks"][P * 9:P * 10, :]).then_inc(S("x_in2"), 16)
            sp.dma_start(convw[:, :], a["conv_wt"]).then_inc(S("small_in"), 16)
            sp.dma_start(convb[:, :], a["conv_bt"]).then_inc(S("small_in"), 16)
            sp.dma_start(gateb[0:8, :], a["gate_bt"]).then_inc(S("small_in"), 16)
            for i, (m, h) in enumerate(PIECES):
                if i >= 2:
                    sp.wait_ge(S("piece_used"), i - 1)
                sp.dma_start(piece[i % 2], drows(a["w_ada"], m * D, (m + 1) * D)[:, 4 * h:4 * h + 4, :]).then_inc(S(f"piece_in{i % 2}"), 16)
                if i == 2:
                    sp.wait_ge(S("ada_done"), 2)
                    sp.dma_start(CS, a["dft"].rearrange("(j p) n -> p j n", p=P)).then_inc(S("cs_in"), 16)
                if i == 3:
                    sp.wait_ge(S("tr_done"), 24)
                    sp.dma_start(wqk, drows(a["w_qk"], 0, D)).then_inc(S("wqk_in"), 16)
            sp.wait_ge(S("fourier_mm"), 16)
            sp.wait_ge(S("qtmp_used"), 8)
            sp.dma_start(wvog, drows(a["w_vog"], 0, 1040)).then_inc(S("wvog_in"), 16)
            sp.wait_ge(S("N_done"), 16)
            sp.wait_ge(S("h_done"), 16)
            sp.dma_start(wout, a["w_out"].rearrange("(k p) n -> p k n", p=P)).then_inc(S("wout_in"), 16)
            sp.dma_start(hgB, a["head_g"].to_broadcast([P, DM])).then_inc(S("wout_in"), 16)
            sp.wait_ge(S("mix_ready"), NTX)
            sp.wait_ge(S("grow_out"), 64)
            sp.dma_start(g1B, grow[0:1, :].to_broadcast([P, D])).then_inc(S("rows1_in"), 16)
            sp.dma_start(lg1, a["ln1_g"].to_broadcast([P, D])).then_inc(S("rows1_in"), 16)
            sp.dma_start(lb1, a["ln1_b"].to_broadcast([P, D])).then_inc(S("rows1_in"), 16)
            sp.dma_start(ytmp[:, 0], a["b_ada"][0:1, 2 * D:3 * D].to_broadcast([P, D])).then_inc(S("rows1_in"), 16)
            for j in range(NTX):
                if j >= 2:
                    sp.wait_ge(S("res_used"), j - 1)
                sp.dma_start(xres[:, j % 2, :], a["toks"][P * (NTC + j):P * (NTC + j + 1), :]).then_inc(S(f"xres_in{j % 2}"), 16)
                if j >= 1:
                    sp.wait_ge(S("ln_ready"), j)
                    sp.dma_start(t_dram[P * (j - 1):P * j, 0:D], lnt[:, (j - 1) % 2, :]).then_inc(S(f"t_out{(j - 1) % 2}"), 16)
                    sp.dma_start(x1_dram[P * (j - 1):P * j, :], x1[:, j - 1]).then_inc(S("x1_out"), 16)
            sp.wait_ge(S("ln_ready"), NTX)
            sp.dma_start(t_dram[P * (NTX - 1):P * NTX, 0:D], lnt[:, (NTX - 1) % 2, :]).then_inc(S(f"t_out{(NTX - 1) % 2}"), 16)
            sp.dma_start(x1_dram[P * (NTX - 1):P * NTX, :], x1[:, NTX - 1]).then_inc(S("x1_out"), 16)
            sp.wait_ge(S("proj_done"), NTX)
            sp.dma_start(wsgu, drows(a["w_shared_gu"], 0, 2 * DE)).then_inc(S("ws_in"), 16)
            sp.dma_start(wsd, a["w_shared_down"].rearrange("(p k) n -> p k n", k=2)).then_inc(S("ws_in"), 16)
            sp.dma_start(wr, drows(a["w_router"], 0, NE)).then_inc(S("wr_in"), 16)
            sp.dma_start(rbB, a["router_bias"].to_broadcast([P, NE])).then_inc(S("wr_in"), 16)

            def load_expert(e, i):
                w = raw[:, WE * i:WE * i + WE]
                rows = slice(e * P, e * P + P) if isinstance(e, int) else bass.ds(e * P, P)
                if not isinstance(e, int):
                    sp.wait_ge(S("lo_split"), 6 * e - 8)
                sp.dma_start(w[:, 0:4096], a["w_gu"][rows, :]).then_inc(S(f"w_in{i}"), 16)
                if not isinstance(e, int):
                    sp.wait_ge(S("lo_split"), 6 * e - 6)
                sp.dma_start(w[:, 4096:WE], a["w_dn"][rows, :]).then_inc(S(f"w_in{i}"), 16)

            sp.wait_ge(S("x1_out"), 16 * NTX)
            load_expert(0, 0)
            sp.wait_ge(S("wt_ready"), 1)
            sp.dma_start(t_dram[0:SEQ, D:XW].rearrange("(t p) n -> p t n", p=P), wt.rearrange("p (t n) -> p t n", t=8)).then_inc(S("pad_out"), 16)
            sp.wait_ge(S("zpad_ready"), 1)
            sp.dma_start(t_dram[SEQ:ROWS_OUT, :], zpad).then_inc(S("pad_out"), 16)
            for j in range(NTX):
                sp.wait_ge(S("sy_act"), j + 1)
                sp.wait_ge(S("sy_dve"), j + 1)
                sp.dma_start(acc[P * j:P * j + P, :], yB[:, j % 2, :]).then_inc(S(f"acc_out{j % 2}"), 16)
            for i in range(2):
                sp.wait_ge(S(f"acc_out{i}"), 16 * 4)
            sp.wait_ge(S("pad_out"), 32)
            sp.wait_ge(S("scattered"), 16)
            load_expert(1, 1)
            sp.wait_ge(S("w_in0"), 32)
            sp.sem_inc(S("weights_ready"), 1)
            with sp.Fori(1, NE // NBUF) as g:
                for i in range(NBUF):
                    load_expert(g * NBUF + i, i)
                    sp.wait_ge(S(f"w_in{1 - i}"), 32 * (g + i))
                    sp.sem_inc(S("weights_ready"), 1)
            sp.wait_ge(S("w_in1"), 32 * (NE // NBUF))
            sp.sem_inc(S("weights_ready"), 1)
            sp.wait_ge(S("lo_split"), 6 * NE)
            sp.dma_start(g2B, grow[1:2, :].to_broadcast([P, D])).then_inc(S("rows2_in"), 16)
            sp.dma_start(lg2, a["ln2_g"].to_broadcast([P, D])).then_inc(S("rows2_in"), 16)
            sp.dma_start(lb2, a["ln2_b"].to_broadcast([P, D])).then_inc(S("rows2_in"), 16)
            sp.dma_start(acc_tmp, a["b_ada"][0:1, 5 * D:6 * D].to_broadcast([P, D])).then_inc(S("rows2_in"), 16)
            for j in range(NTX):
                sp.dma_start(x1_in[j], x1_dram[P * j:P * j + P, :]).then_inc(S("rows2_in"), 16)
            sp.wait_ge(S("experts_done"), 1)
            for j in range(NTX):
                sp.dma_start(acc_in[j], acc[P * j:P * j + P, :]).then_inc(S(f"accin{j // 4}"), 16)
            for j in range(NTX):
                sp.wait_ge(S("out_ready"), j + 1)
                sp.dma_start(out[P * j:P * j + P, :], acc_in[j]).then_inc(S("out_done"), 16)
            sp.wait_ge(S("out_done"), 16 * NTX)

        @block.gpsimd
        def _(pool):
            def rstd_of(var_ready, v, col, done):
                pool.wait_ge(*var_ready)
                pool.tensor_scalar(veps[:, col:col + 1], v, EPS, None, ALU.add).then_inc(S("pool_step"), 1)
                n["p"] += 1
                pool.wait_ge(S("pool_step"), n["p"])
                pool.tensor_tensor(rstd[:, col:col + 1], veps[:, col:col + 1], cst[:, C_HALF:C_HALF + 1], ALU.pow).then_inc(S(done), 1)

            n = {"p": 0}
            pool.wait_ge(S("const_in"), 32)
            for t in range(NT):
                rstd_of((S("mv_ready"), t + 1), mv[:, 2 * t + 1:2 * t + 2], t, "rstd_ready")
            pool.wait_ge(S("piece_used"), 8)
            pool.memset(at(D0, 2376), 0.0).then_inc(S("cbuf_zero"), 1)
            pool.memset(cbufc, 0.0).then_inc(S("cbuf_zero"), 1)
            pool.wait_ge(S("qk_done"), 20)
            pool.memset(V[:, :, :, DH:VW], 1.0).then_inc(S("v_ones"), 1)
            pool.wait_ge(S("v_evac"), NT)
            pool.wait_ge(S("v_ones"), 1)
            pool.wait_ge(S("cols_ready"), 1)
            for q, (s, d, t) in enumerate(JOBS):
                if q >= 2:
                    pool.wait_ge(S("U_half"), 2 * (q - 1))
                c0 = s * 48 + 16 + 12 * d
                pool.tensor_tensor(vw[:, q % 2], V[:, t], COL[:, c0:c0 + 4].unsqueeze(2).to_broadcast([P, 4, VW]), ALU.mult).then_inc(S("vw_ready"), 1)
            for j in range(NTX):
                pool.wait_ge(S("hmv_ready"), j + 1)
                if j >= 2:
                    pool.wait_ge(S("mix_ready"), j - 1)
                pool.tensor_scalar(hveps[:, j % 2], hmv[:, j % 2, :, 1], EPS, None, ALU.add).then_inc(S("pool_step"), 1)
                n["p"] += 1
                pool.wait_ge(S("pool_step"), n["p"])
                pool.tensor_tensor(hrstd[:, j % 2], hveps[:, j % 2], cst[:, C_HALF:C_HALF + 4], ALU.pow).then_inc(S("hrstd_ready"), 1)
            for j in range(NTX + 1):
                if j < NTX:
                    rstd_of((S("y_mv"), j + 1), mvj[:, j % 2, 1:2], j % 2, "y_rstd")
                    pool.wait_ge(S("y_norm"), j + 1)
                    pool.wait_ge(S("rows1_in"), 64)
                    pool.tensor_tensor(ytmp[:, j % 2], ytmp[:, j % 2], lg1, ALU.mult).then_inc(S("y_gain"), 1)
                if j >= 1:
                    rstd_of((S("x1_mv"), j), mvk[:, (j - 1) % 2, 1:2], 2 + (j - 1) % 2, "x1_rstd")
            pool.wait_ge(S("ln_ready"), NTX)
            pool.memset(zpad, 0.0).then_inc(S("zpad_ready"), 1)
            pool.wait_ge(S("zpad_ready"), 1)
            pool.dma_start(acc[SEQ:ROWS_OUT, :], zpad[:, 0:D]).then_inc(S("scattered"), 16)
            pool.wait_ge(S("idx_ready"), 1)
            pool.wait_ge(S("table_ready"), 1)
            for i in range(2):
                pool.wait_ge(S(f"t_out{i}"), 64)
                pool.wait_ge(S(f"acc_out{i}"), 64)
            pool.wait_ge(S("pad_out"), 32)
            pool.sem_inc(S("y_free"), 1)

            def gather(col, p, nth):
                pool.tensor_copy(idxg[:, p:p + 1], idxT[:, col]).then_inc(S("idx_copied"), 1)
                pool.wait_ge(S("idx_copied"), nth)
                pool.sem_inc(S("pool_pass"), 1)
                pool.indirect_dma_start(out=xg[:, p], out_offset=None, in_=t_dram[:, :],
                                        in_offset=bass.IndirectOffsetOnAxis(ap=idxg[:, p:p + 1], axis=0)).then_inc(S(f"gathered{p}"), 16)

            def scatter(b, p, nth):
                pool.wait_ge(S("scattered"), 16 * b + 16)
                pool.sem_inc(S("y_free"), 1)
                pool.tensor_copy(idxs[:, p:p + 1], idxT[:, b:b + 1] if isinstance(b, int) else idxT[:, bass.ds(b, 1)]).then_inc(S("idx_copied"), 1)
                pool.wait_ge(S("idx_copied"), nth)
                pool.wait_ge(S("m_y"), b + 2)
                pool.sem_inc(S("pool_pass"), 1)
                pool.indirect_dma_start(out=acc[:, :], out_offset=bass.IndirectOffsetOnAxis(ap=idxs[:, p:p + 1], axis=0),
                                        in_=yB[:, p], in_offset=None, compute_op=ALU.add).then_inc(S("scattered"), 16)

            gather(slice(0, 1), 0, 1)
            gather(slice(1, 2), 1, 2)
            pool.wait_ge(S("m_xb"), 1)
            gather(slice(2, 3), 0, 3)
            pool.wait_ge(S("m_xb"), 2)
            gather(slice(3, 4), 1, 4)
            rest = pool.value_load(pairs_rest[0:1, 0:1], min_val=NE // 2 - 1, max_val=MAXB // 2 - 1)
            with pool.Fori(0, rest) as i:
                for p in range(2):
                    pool.wait_ge(S("m_xb"), 2 * i + (p + 3))
                    gather(bass.ds(2 * i + (p + 4), 1), p, 4 * i + (2 * p + 5))
                    scatter(2 * i + p, p, 4 * i + (2 * p + 6))
            scatter(2 * rest, 0, 4 * rest + 5)
            scatter(2 * rest + 1, 1, 4 * rest + 6)
            pool.wait_ge(S("scattered"), 32 * rest + 48)
            for p in range(2):
                pool.wait_ge(S(f"gathered{p}"), 16 * rest + 32)
            pool.sem_inc(S("experts_done"), 1)
            for j in range(NTX):
                rstd_of((S("y_mv"), NTX + j + 1), mvj[:, j % 2, 1:2], j % 2, "y_rstd")
                pool.wait_ge(S("y_norm"), NTX + j + 1)
                pool.wait_ge(S("rows2_in"), 64 + 16 * NTX)
                pool.tensor_tensor(acc_in[j], acc_in[j], lg2, ALU.mult).then_inc(S("y_gain"), 1)

        @block.scalar
        def _(act):
            def copy(o, i):
                return act.activation(o, i, ACT.Copy)

            act.wait_ge(S("c_in"), 16)
            act.activation(silc[:, :], ccol[:, :], ACT.Silu).then_inc(S("sil_ready"), 1)
            act.wait_ge(S("mod_ready"), 2)
            for g, (t0, nt) in enumerate(GROUPS):
                for k in range(0, 8, 2):
                    q = 8 * g + k
                    w = 0 if g else 1
                    act.wait_ge(S("tr_done"), q + 1)
                    act.activation(uT[:, k, P * t0:P * (t0 + nt)], bank(q % 4)[:, 0:P * nt], ACT.Identity,
                                   scale=modc[:, 16 + 2 * k + w:17 + 2 * k + w], bias=modc[:, 2 * k + w:2 * k + w + 1]).then_inc(S("uT_act"), 1)
            def grow_out(m):
                for h in range(2):
                    act.wait_ge(S("piece_used"), 6 + 2 * m)
                    if 2 * m + h >= 1:
                        act.wait_ge(S("grow_out"), 16 * (2 * m + h))
                    copy(rowt[:, :], bank(6 if h == 0 else 0)[0:1, :]).then_inc(S("grow_put"), 1)
                    act.wait_ge(S("grow_put"), 2 * m + h + 1)
                    act.dma_start(grow[m:m + 1, 512 * h:512 * h + 512], rowt[:, :]).then_inc(S("grow_out"), 16)
            for i in range(8):
                act.wait_ge(S("f_done"), i + 1)
                c, h = i // 2, i % 2
                copy(fT[:, c, 512 * h:512 * h + 512], bank(4 + i % 2)).then_inc(S("f_evac"), 1)
                if i == 5:
                    grow_out(0)
            grow_out(1)
            for q, (idx, j, cp) in enumerate(ABJOBS):
                if idx % 2 == 0:
                    act.wait_ge(S("ab_done"), q + 1)
                    copy(EO[:, j, 2 * cp:2 * cp + 2, :], bank(1 + q % 3).rearrange("p (c n) -> p c n", c=2)).then_inc(S("ab_act"), 1)
            for c in range(4):
                for g, w in ((0, NEV), (1, NOD)):
                    act.wait_ge(S("fourier_mm"), 4 * c + 2 * g + 2)
                    if c:
                        act.wait_ge(S("qtmp_used"), 2 * (c - 1) + g + 1)
                    copy(qtmp[:, g, 0:w], bank((0 if c % 2 else 4) + 2 * g + 1)[:, 0:w]).then_inc(S("qtmp_ready"), 1)
            act.wait_ge(S("cbuf_zero"), 2)
            act.wait_ge(S("small_in"), 48)
            for c in range(9):
                if c < 8:
                    for q, (cc, part) in enumerate(QKJOBS):
                        if cc != c:
                            continue
                        act.wait_ge(S("qk_done"), q + 1)
                        if part == 0 and c >= 2:
                            act.wait_ge(S("conv_done"), c - 1)
                        if part == 2 and c >= 5:
                            act.wait_ge(S("conv_done"), c)
                        if part < 2:
                            copy(cbuf[c % 2][:, 1 + 8 * part:9 + 8 * part, 1:65], bank(q % 4).rearrange("p (r c) -> p r c", r=8)).then_inc(S("cv_evac"), 1)
                        else:
                            copy(cbufc[:, 1:257], bank(q % 4)[:, 0:256]).then_inc(S("cv_evac"), 1)
                if c >= 1:
                    act.wait_ge(S("conv_done"), c)
                    x = c - 1
                    act.activation(qkT[:, x, :], cacc.rearrange("p r c -> p (r c)"), ACT.Silu, bias=convb[:, x:x + 1]).then_inc(S("silu_done"), 1)
                    if x >= 4:
                        act.activation(kTc[:, x - 4, :], caccc, ACT.Silu, bias=convb[:, x:x + 1]).then_inc(S("siluc_done"), 1)
            act.wait_ge(S("rows_evac"), 6)
            act.activation(Rl, Rf, ACT.Abs).then_inc(S("rl_step"), 1)
            act.wait_ge(S("rl_step"), 1)
            act.activation(Rl, Rl, ACT.Exp, scale=-1.0).then_inc(S("rl_step"), 1)
            act.wait_ge(S("rl_step"), 2)
            act.activation(Rl, Rl, ACT.Ln, bias=1.0).then_inc(S("rl_step"), 1)
            for t in range(NT):
                act.wait_ge(S("v_done"), t + 1)
                copy(V[:, t, :, 0:DH], bank(4 + t % 2).rearrange("p (h n) -> p h n", h=4)).then_inc(S("v_evac"), 1)
                if t >= NTC:
                    act.wait_ge(S("o_done"), t - NTC + 1)
                    act.activation(O[:, t - NTC], bank(6), ACT.Tanh, scale=0.5).then_inc(S("o_evac"), 1)
            act.wait_ge(S("wargs_ready"), 3)
            for i, r in enumerate((Rw, Re, Ri)):
                act.activation(r, r, ACT.Exp).then_inc(S("rows_exp"), 1)
            act.wait_ge(S("rows_exp"), 3)
            for r, o in zip((Ra, Rw, Re), Rrev):
                copy(o.rearrange("p (s n) -> p s n", s=NT), r.rearrange("p (s n) -> p s n", s=NT)[:, :, ::-1]).then_inc(S("rows_rev"), 1)
            for t in range(NT):
                act.wait_ge(S("kM_done"), t + 1)
                act.mul(kM[:, t], bank(t % 2), KSCALE).then_inc(S("kM_evac"), 1)
            act.wait_ge(S("cols_ready"), 1)
            for x in range(16):
                s, d, t = JOBS[x + FIRSTX]
                act.wait_ge(S("SD_done"), x + 1)
                if x >= 2:
                    act.wait_ge(S("N_done"), x - 1)
                for h in range(4):
                    c0 = s * 48 + 12 * d + h
                    ins = act.activation(Dt[:, x % 2, P * h:P * h + P], bank(2 if x % 2 == 0 else 5)[:, P * h:P * h + P], ACT.Exp, bias=COL[:, c0:c0 + 1])
                ins.then_inc(S("D_ready"), 1)
            act.wait_ge(S("h_done"), 16)
            act.wait_ge(S("N_done"), 16)
            for v, c0 in enumerate((48, 32)):
                for k in range(8):
                    ins = act.activation(diag[:, v, k], ident, ACT.Copy, scale=modc[:, c0 + 2 * k:c0 + 2 * k + 1])
            ins.then_inc(S("diag_ready"), 1)
            for j in range(NTX):
                act.wait_ge(S("mixt_done"), j + 1)
                copy(mixT[:, 0:4, P * j:P * j + P], bank(j % 2).rearrange("p (h n) -> p h n", h=4)).then_inc(S("mixt_evac"), 1)
            act.wait_ge(S("mix_ready"), NTX)
            act.wait_ge(S("mod_rows"), 1)
            for v, (dst, banks) in enumerate(((sc2B, (2, 7)), (sh2B, (5, 6)))):
                for h in range(2):
                    ins = copy(dst.rearrange("p (q k) -> p k q", k=8)[:, 4 * h:4 * h + 4, :], bank(banks[h]).rearrange("p (k q) -> p k q", k=4))
            ins.then_inc(S("rows_evac2"), 1)
            for j in range(NTX):
                act.wait_ge(S("tt_done"), j + 1)
                for h in range(2):
                    ins = copy(tT[:, 4 * h:4 * h + 4, P * j:P * j + P], bank(h).rearrange("p (k n) -> p k n", k=4))
                ins.then_inc(S("tT_evac"), 1)
            act.wait_ge(S("router_done"), 1)
            act.activation(sc, bank(2), ACT.Sigmoid).then_inc(S("sc_ready"), 1)
            for j in range(NTX):
                act.wait_ge(S("sgu_done"), j + 1)
                act.activation(sgL[:, j % 2], bank(3 + j % 2)[:, 0:DE], ACT.Silu).then_inc(S("s_sg"), 1)
                act.wait_ge(S("sht_done"), j + 1)
                copy(hTL[:, j % 2], bank(7)[:, 0:2 * P].rearrange("p (k n) -> p k n", k=2)).then_inc(S("s_hT"), 1)
                act.wait_ge(S("sdown_done"), j + 1)
                if j >= 2:
                    act.wait_ge(S(f"acc_out{j % 2}"), 16 * (j // 2))
                copy(yB[:, j % 2, 0:512], bank(5)).then_inc(S("sy_act"), 1)
            def x_high(b, p):
                act.wait_ge(S("m_xt"), b + 1)
                copy(xTh[p], psum[:, 0:1024]).then_inc(S("m_xh"), 1)

            def h_high(b):
                act.wait_ge(S("m_ht"), b + 1)
                copy(hTh, bank(7)[:, 0:2 * P]).then_inc(S("m_hh"), 1)

            def w_high(par, chunks):
                for c in chunks:
                    copy(cols(wsplit, par * (2 * WE) + 1024 * c, 1024), cols(raw, par * WE + 1024 * c, 1024)).then_inc(S("hi_split"), 1)

            def y_evac(b, p):
                act.wait_ge(S("block_done"), b + 2)
                act.wait_ge(S("y_free"), b + 1)
                copy(yB[:, p], psY).then_inc(S("m_y"), 1)

            def silu(b, p):
                act.wait_ge(S("m_gu"), b + 1)
                act.activation(sg[:, p], bank(3 + p)[:, 0:DE], ACT.Silu).then_inc(S("m_sg"), 1)

            act.wait_ge(S("table_ready"), 1)
            act.sem_inc(S("m_y"), 1)
            act.wait_ge(S("weights_ready"), 1)
            w_high(0, range(6))
            x_high(0, 0)
            x_high(1, 1)
            act.wait_ge(S("weights_ready"), 2)
            w_high(1, range(4))
            silu(0, 0)

            def step(b, p, w0, w1):
                h_high(b - 1)
                if w0 is not None:
                    y_evac(b - 2, p)
                x_high(b + 1, 1 - p)
                if w0 is None:
                    w_high(1, range(4, 6))
                else:
                    with act.If_ne(act.to_reg((w0 >> 6) & 1), 0):
                        w_high(1 - (w0 & 1), range(4, 6))
                first, par1 = (w1 >> 6) & 1, 1 - (w1 & 1)
                with act.If_ne(act.to_reg(first), 0):
                    act.wait_ge(S("weights_ready"), (w1 & 63) + 2)
                    act.sem_inc(S("act_pass"), 1)
                    w_high(par1, range(2))
                silu(b, p)
                with act.If_ne(act.to_reg(first), 0):
                    w_high(par1, range(2, 4))

            def word(b):
                return word_of(act, b)

            step(1, 1, None, word(1))
            rest = act.value_load(pairs_rest[0:1, 0:1], min_val=NE // 2 - 1, max_val=MAXB // 2 - 1)
            with act.Fori(0, rest) as i:
                w0, w1 = word(2 * i + 1), word(2 * i + 2)
                step(2 * i + 2, 0, w0, w1)
                w2 = word(2 * i + 3)
                step(2 * i + 3, 1, w1, w2)
            h_high(2 * rest + 1)
            y_evac(2 * rest, 0)
            y_evac(2 * rest + 1, 1)

        @block.tensor
        def _(pe):
            mm = pe.matmul

            def ada_cols(w, kc, k, rhs, base, start):
                return mm(bank(7)[:, base + 2 * k:base + 2 * k + 2], w[:, kc % w.shape[1], k::8], rhs, start=start, stop=False, skip_group_check=True)

            pe.wait_ge(S("sil_ready"), 1)
            for m in range(2):
                pe.wait_ge(S(f"ada_in{m}"), 16)
                for kc in range(8):
                    for k in range(8):
                        ins = ada_cols(ada[m], kc, k, silc[:, 2 * kc:2 * kc + 2], 16 * m, m == 0 and kc == 0 and k == 0)
                ins.then_inc(S("ada_done"), 1)
            pe.wait_ge(S("const_in"), 32)
            for g, (t0, nt) in enumerate(GROUPS):
                pe.wait_ge(S("xn_ready"), t0 + nt)
                for k in range(8):
                    q = 8 * g + k
                    if q >= 4:
                        pe.wait_ge(S("uT_act") if q % 2 == 0 else S("uT_dve"), (q - 4) // 2 + 1)
                    for i in range(nt):
                        ins = pe.transpose(bank(q % 4)[:, P * i:P * i + P], xin[t0 + i][:, k::8], ident)
                    ins.then_inc(S("tr_done"), 1)
            pe.wait_ge(S("uT_act"), 12)
            pe.wait_ge(S("uT_dve"), 12)
            pe.wait_ge(S("wf_in"), 16)
            pe.wait_ge(S("mod_ready"), 2)
            for i in range(8):
                c, h = i // 2, i % 2
                if i >= 2:
                    pe.wait_ge(S("f_evac"), i - 1)
                for k in range(8):
                    ins = mm(bank(4 + i % 2), wf[:, k, P * c:P * c + P], uT[:, k, CTX + 512 * h:CTX + 512 * h + 512], start=(k == 0), stop=(k == 7))
                ins.then_inc(S("f_done"), 1)
                m, ph = PIECES[i]
                pe.wait_ge(S(f"piece_in{i % 2}"), 16 * (i // 2 + 1))
                if m in (3, 4):
                    for kc in range(4 * ph, 4 * ph + 4):
                        for k in range(8):
                            ins = ada_cols(piece[i % 2], kc, k, silc[:, 2 * kc:2 * kc + 2], 16 * (m - 1), m == 3 and kc == 0 and k == 0)
                    ins.then_inc(S("piece_used"), 1)
                else:
                    if (m, ph) == (5, 0):
                        pe.wait_ge(S("grow_put"), 2)
                    for kc in range(4 * ph, 4 * ph + 4):
                        for h2 in range(2):
                            ins = mm(bank(6 if h2 == 0 else 0)[0:1, :], silc[:, 2 * kc:2 * kc + 1], piece[i % 2][:, kc % 4, 512 * h2:512 * h2 + 512],
                                     start=(kc == 0), stop=(kc == 7))
                    ins.then_inc(S("piece_used"), 1)
            pe.wait_ge(S("f_evac"), 8)
            for q, (idx, j, cp) in enumerate(ABJOBS):
                if q >= 3:
                    i3, _, c3 = ABJOBS[q - 3]
                    pe.wait_ge(S("ab_act") if i3 % 2 == 0 else S("ab_dve"), 2 * (i3 // 2) + c3 + 1)
                for c in range(2):
                    ins = mm(bank(1 + q % 3)[:, 256 * c:256 * c + 256], fT[:, 2 * cp + c, P * j:P * j + P], cst[:, C_CD:C_CD + 256], start=True, stop=True)
                ins.then_inc(S("ab_done"), 1)
            pe.wait_ge(S("ab_act"), 8)
            pe.wait_ge(S("ab_dve"), 8)
            pe.wait_ge(S("cs_in"), 16)
            pe.wait_ge(S("grow_put"), 4)
            pe.wait_ge(S("mod_ready"), 4)
            for c in range(4):
                if c >= 2:
                    pe.wait_ge(S("qtmp_used"), 2 * (c - 1))
                for g in range(4):
                    odd, sin = g // 2, g % 2
                    w = NOD if odd else NEV
                    o = (2 * NEV if odd else 0) + sin * w
                    for j in range(4):
                        ins = mm(bank((0 if c % 2 else 4) + g)[:, 0:w], EO[:, j if odd else 4 + j, c, P * sin:P * sin + P], CS[:, j, o:o + w], start=(j == 0), stop=(j == 3))
                    ins.then_inc(S("fourier_mm"), 1)
            pe.wait_ge(S("qtmp_used"), 8)
            pe.wait_ge(S("wqk_in"), 16)
            for q, (c, part) in enumerate(QKJOBS):
                if q >= 4:
                    pe.wait_ge(S("cv_evac"), q - 3)
                n, o = (512, CTX + 512 * part) if part < 2 else (CTX, 0)
                for k in range(8):
                    ins = mm(bank(q % 4)[:, 0:n], wqk[:, k, P * c:P * c + P], uT[:, k, o:o + n], start=(k == 0), stop=(k == 7))
                ins.then_inc(S("qk_done"), 1)
            pe.wait_ge(S("wvog_in"), 16)
            for t in range(NT):
                if t >= 2:
                    pe.wait_ge(S("g_evac"), t - 1)
                for k in range(8):
                    ins = mm(bank(6 + t % 2)[:, 0:16], uT[:, k, P * t:P * t + P], wvog[:, k, 1024:1040], start=(k == 0), stop=(k == 7))
                ins.then_inc(S("g_done"), 1)
            pe.wait_ge(S("g_evac"), NT)
            pe.wait_ge(S("cv_evac"), 20)
            for r, (s0, ns) in enumerate(((0, 4), (4, 4), (8, 2))):
                for gate in range(2):
                    q = 2 * r + gate
                    if q >= 4:
                        pe.wait_ge(S("rows_evac"), q - 3)
                    for i in range(ns):
                        tf, tb = tiles_of(s0 + i)
                        o = bank(q % 4)[0:8, P * i:P * i + P]
                        mm(o, G[:, 32 * tf + 8 * gate:32 * tf + 8 * gate + 8], ident, start=True, stop=False)
                        ins = mm(o, G[:, 32 * tb + 16 + 8 * gate:32 * tb + 24 + 8 * gate], rev, start=False, stop=True)
                    ins.then_inc(S("rows_mm"), 1)
            for t in range(NT):
                if t >= 2:
                    pe.wait_ge(S("v_evac"), t - 1)
                for k in range(8):
                    ins = mm(bank(4 + t % 2), uT[:, k, P * t:P * t + P], wvog[:, k, 0:512], start=(k == 0), stop=(k == 7))
                ins.then_inc(S("v_done"), 1)
                if t >= NTC:
                    if t > NTC:
                        pe.wait_ge(S("o_evac"), t - NTC)
                    for k in range(8):
                        ins = mm(bank(6), uT[:, k, P * t:P * t + P], wvog[:, k, 512:1024], start=(k == 0), stop=(k == 7))
                    ins.then_inc(S("o_done"), 1)
            pe.wait_ge(S("silu_done"), 8)
            pe.wait_ge(S("siluc_done"), 4)
            pe.wait_ge(S("rows_evac"), 6)
            for t in range(NT):
                if t >= 2:
                    pe.wait_ge(S("kM_evac"), t - 1)
                for h in range(4):
                    src = kTc[:, h, P * t:P * t + P] if t < NTC else qkT[:, 4 + h, P * (t - NTC):P * (t - NTC) + P]
                    ins = pe.transpose(bank(t % 2)[:, P * h:P * h + P], src, ident)
                ins.then_inc(S("kM_done"), 1)
            pe.wait_ge(S("rows_exp"), 3)
            pe.wait_ge(S("rows_rev"), 4)
            first = True
            for s in range(NT):
                for v, r in enumerate((Ra, Rw, Re)):
                    for d in range(2):
                        src = (Rrev[v] if d else r)[:, P * s:P * s + P]
                        o = s * 48 + 16 * v + 8 * d
                        ins = mm(bank(2)[:, o:o + 8], src, cst[0:8, C_ID:C_ID + 8], start=first, stop=False, skip_group_check=True)
                        first = False
            mm(bank(3)[:, 0:NT * 8], cst[0:8, C_ONE:C_ONE + P], dgl[0:8, :], start=True, stop=True).then_inc(S("cols_mm"), 1)
            pe.wait_ge(S("cols_ready"), 1)
            pe.wait_ge(S("kM_evac"), NT)
            pe.wait_ge(S("v_evac"), NT)
            pe.wait_ge(S("v_ones"), 1)

            def rows_of(r, s, d, n=P):
                src = r[:, P * s:P * s + P]
                return src[:, ::-1] if d else src

            def scores(x):
                s, d, t = JOBS[x + FIRSTX]
                c = t - NTC
                if x >= 2:
                    pe.wait_ge(S("P_ready"), x - 1)
                for h in range(4):
                    mm(bank(x % 2)[:, P * h:P * h + P], qkT[:, 4 + h, P * c:P * c + P], qkT[:, h, P * c:P * c + P], start=True, stop=True)
                db = bank(2 if x % 2 == 0 else 5)
                mk_ = C_MB if d else C_MF
                for h in range(4):
                    mm(db[:, P * h:P * h + P], ident, cst[:, mk_:mk_ + P], start=True, stop=False)
                    r = 4 * d + h
                    ins = mm(db[:, P * h:P * h + P], cst[0:8, C_SEL + P * r:C_SEL + P * r + P], rows_of(Rm, s, d), start=False, stop=True)
                ins.then_inc(S("SD_done"), 1)

            def update(q, half, b):
                s, d, t = JOBS[q]
                for i in range(2):
                    h = 2 * half + i
                    ins = mm(bank(b)[:, 256 * i:256 * i + VW], kM[:, t, P * h:P * h + P], vw[:, q % 2, h], start=True, stop=True)
                ins.then_inc(S("U_half"), 1)
                return ins

            for q, (s, d, t) in enumerate(JOBS):
                x = q - FIRSTX
                if x == 0:
                    scores(0)
                if q >= 1:
                    pe.wait_ge(S("C_half"), 2 * q)
                if x >= 0:
                    for h in range(4):
                        r = 4 * d + h
                        ins = mm(bank(6)[:, P * h:P * h + P], cst[0:8, C_SEL + P * r:C_SEL + P * r + P], rows_of(Ri, s, d), start=True, stop=True)
                    ins.then_inc(S("I_done"), 1)
                    if x + 1 < 16:
                        scores(x + 1)
                pe.wait_ge(S("vw_ready"), q + 1)
                update(q, 0, 7)
                if x >= 0:
                    pe.wait_ge(S("qI_ready"), x + 1)
                update(q, 1, 6)
                if x >= 0:
                    pe.wait_ge(S("P_ready"), x + 1)
                    if x >= 1:
                        pe.wait_ge(S("h_read"), x)
                    for h in range(4):
                        o = psN[:, 512 * (h // 2) + 256 * (h % 2):512 * (h // 2) + 256 * (h % 2) + VW]
                        mm(o, Dt[:, x % 2, P * h:P * h + P], V[:, t, h], start=True, stop=False)
                        ins = mm(o, qI[:, x % 2, P * h:P * h + P], Cst[:, d, h], start=False, stop=True)
                    ins.then_inc(S("N_done"), 1)
            pe.wait_ge(S("diag_ready"), 1)
            pe.wait_ge(S("C_half"), 2 * NJ)
            for v, banks in enumerate(((2, 7), (5, 6))):
                for k in range(8):
                    ins = mm(bank(banks[k // 4])[:, P * (k % 4):P * (k % 4) + P], ones, diag[:, v, k], start=True, stop=True)
            ins.then_inc(S("mod_rows"), 1)
            for j in range(NTX):
                pe.wait_ge(S("mix_ready"), j + 1)
                if j >= 2:
                    pe.wait_ge(S("mixt_evac"), j - 1)
                for h in range(4):
                    ins = pe.transpose(bank(j % 2)[:, P * h:P * h + P], H[:, j, P * h:P * h + P], ident)
                ins.then_inc(S("mixt_done"), 1)
            pe.wait_ge(S("mixt_evac"), NTX)
            pe.wait_ge(S("wout_in"), 32)
            for j in range(NTX + 2):
                if j < NTX:
                    if j == 1:
                        pe.wait_ge(S("rows_evac2"), 1)
                    if j >= 2:
                        pe.wait_ge(S("y_read"), j - 1)
                    for h in range(2):
                        o = (psN if j % 2 == 0 else psY)[:, 512 * h:512 * h + 512]
                        for k in range(8):
                            ins = mm(o, mixT[:, k, P * j:P * j + P], wout[:, k, 512 * h:512 * h + 512], start=(k == 0), stop=(k == 7))
                    ins.then_inc(S("proj_done"), 1)
                if j >= 2:
                    i = j - 2
                    pe.wait_ge(S("ln_ready"), i + 1)
                    if i >= 1:
                        pe.wait_ge(S("tT_evac"), i)
                    for k in range(8):
                        ins = pe.transpose(bank(k // 4)[:, P * (k % 4):P * (k % 4) + P], lnt[:, i % 2, k::8], ident)
                    ins.then_inc(S("tt_done"), 1)
            pe.wait_ge(S("tT_evac"), NTX)
            pe.wait_ge(S("wr_in"), 32)
            for j in range(NTX):
                for k in range(8):
                    ins = mm(bank(2)[:, NE * j:NE * j + NE], tT[:, k, P * j:P * j + P], wr[:, k, :], start=(k == 0), stop=(k == 7))
            ins.then_inc(S("router_done"), 1)
            pe.wait_ge(S("ws_in"), 32)

            def shared(j):
                for k in range(8):
                    ins = mm(bank(3 + j % 2), tT[:, k, P * j:P * j + P], wsgu[:, k, :], start=(k == 0), stop=(k == 7))
                ins.then_inc(S("sgu_done"), 1)
                pe.wait_ge(S("s_hx"), j + 1)
                for k in range(2):
                    ins = pe.transpose(bank(7)[:, P * k:P * k + P], hxL[:, j % 2, k::2], ident)
                ins.then_inc(S("sht_done"), 1)
                pe.wait_ge(S("s_hT"), j + 1)
                if j >= 1:
                    pe.wait_ge(S("sy_act"), j)
                    pe.wait_ge(S("sy_dve"), j)
                for h in range(2):
                    for k in range(2):
                        ins = mm(bank(5 + h), hTL[:, j % 2, k], wsd[:, k, 512 * h:512 * h + 512], start=(k == 0), stop=(k == 1))
                ins.then_inc(S("sdown_done"), 1)

            shared(0)
            pe.wait_ge(S("mask_ready"), 1)
            mkv = mk.rearrange("p (j e) -> p j e", j=8)
            for j in range(NTX):
                for i in range(j + 1):
                    mm(bank(0)[:, NE * j:NE * j + NE], cst[:, C_LT:C_LT + P] if i == j else ones, mkv[:, i, :], start=(i == 0), stop=(i == j))
            for i in range(NTX):
                ins = mm(bank(1)[:, 0:NE], ones, mkv[:, i, :], start=(i == 0), stop=(i == NTX - 1))
            ins.then_inc(S("pos_done"), 1)
            shared(1)
            shared(2)
            pe.wait_ge(S("eb_ready"), 1)
            mm(bank(1)[0:1, 0:P], ebc, ident, start=True, stop=True).then_inc(S("eb_mm"), 1)
            for q in range(64):
                pe.wait_ge(S("onehot_ready"), q + 1)
                mm(bank(2)[:, 0:P], oneP[:, q % 2], oneB[:, q % 2], start=(q == 0), stop=(q == 63)).then_inc(S("onehot_used"), 1)
            for j in range(3, NTX):
                shared(j)
            def x_transposes(b, p, landed):
                pe.wait_ge(S(f"gathered{p}"), landed)
                if not isinstance(b, int) or b > 0:
                    pe.wait_ge(S("m_xb"), b)
                for k in range(8):
                    ins = pe.transpose(bank(k // 4)[:, P * (k % 4):P * (k % 4) + P], xg[:, p, 0:D][:, k::8], ident)
                ins.then_inc(S("m_xt"), 1)

            def part(par, low, o):
                return cols(wsplit, par * (2 * WE) + (WE * low + o), 512)

            def gate_up(b, p, par, e):
                pe.wait_ge(S("m_xb"), b + 1)
                for k in range(8):
                    if k % 2 == 0:
                        pe.wait_ge(S("lo_split"), 6 * e + (k // 2 + 1))
                    xk, xl = (x[:, P * k:P * k + P] for x in (xTh[p], xTl[p]))
                    mm(bank(3 + p), xk, part(par, 0, 512 * k), start=(k == 0), stop=False)
                    mm(bank(3 + p), xk, part(par, 1, 512 * k), start=False, stop=False)
                    ins = mm(bank(3 + p), xl, part(par, 0, 512 * k), start=False, stop=(k == 7))
                ins.then_inc(S("m_gu"), 1)

            def h_transposes(b, p):
                pe.wait_ge(S("m_hx"), b + 1)
                for k in range(2):
                    ins = pe.transpose(bank(7)[:, P * k:P * k + P], hx[:, p, k::2], ident)
                ins.then_inc(S("m_ht"), 1)

            def down(b, par, e):
                pe.wait_ge(S("m_hT"), b + 1)
                pe.wait_ge(S("m_y"), b + 1)
                pe.wait_ge(S("lo_split"), 6 * e + 6)
                for h in range(2):
                    for k in range(2):
                        hk, hl = (x[:, P * k:P * k + P] for x in (hTh, hTl))
                        o = 4096 + 1024 * k + 512 * h
                        mm(bank(5 + h), hk, part(par, 0, o), start=(k == 0), stop=False)
                        mm(bank(5 + h), hk, part(par, 1, o), start=False, stop=False)
                        ins = mm(bank(5 + h), hl, part(par, 0, o), start=False, stop=(k == 1))
                ins.then_inc(S("block_done"), 1)

            def word(b):
                return word_of(pe, b)

            pe.wait_ge(S("table_ready"), 1)
            pe.wait_ge(S("sy_act"), NTX)
            pe.wait_ge(S("sy_dve"), NTX)
            pe.sem_inc(S("block_done"), 1)
            x_transposes(0, 0, 16)
            x_transposes(1, 1, 16)
            gate_up(0, 0, 0, 0)

            def step(b, p, landed, w0, w1):
                h_transposes(b - 1, 1 - p)
                x_transposes(b + 1, 1 - p, landed)
                gate_up(b, p, w1 & 1, w1 & 63)
                down(b - 1, w0 & 1, w0 & 63)

            step(1, 1, 32, word(0), word(1))
            rest = pe.value_load(pairs_rest[0:1, 0:1], min_val=NE // 2 - 1, max_val=MAXB // 2 - 1)
            with pe.Fori(0, rest) as i:
                w0, w1 = word(2 * i + 1), word(2 * i + 2)
                step(2 * i + 2, 0, 16 * i + 32, w0, w1)
                w2 = word(2 * i + 3)
                step(2 * i + 3, 1, 16 * i + 48, w1, w2)
            h_transposes(2 * rest + 1, 1)
            w0 = word(2 * rest + 1)
            down(2 * rest + 1, w0 & 1, w0 & 63)

        @block.vector
        def _(dve):
            n = {"c": 0}

            def link(ins):
                n["c"] += 1
                ins.then_inc(S("dve_step"), 1)
                dve.wait_ge(S("dve_step"), n["c"])

            tt, ts, stt = dve.tensor_tensor, dve.tensor_scalar, dve.scalar_tensor_tensor

            def moments(x, o, done):
                dve.bn_stats(stats[:, 0:6], x[:, 0:512])
                link(dve.bn_stats(stats[:, 6:12], x[:, 512:1024]))
                dve.bn_aggr(o, stats[:, :]).then_inc(S(done), 1)

            def norm(t):
                dve.wait_ge(S(f"x_in{XG[t]}"), 16 * XG.count(XG[t]))
                moments(xin[t], mv[:, 2 * t:2 * t + 2], "mv_ready")
                dve.wait_ge(S("rstd_ready"), t + 1)
                ts(xin[t], xin[t], mv[:, 2 * t:2 * t + 1], rstd[:, t:t + 1], ALU.subtract, ALU.mult).then_inc(S("xn_ready"), 1)

            def modulation(i, m):
                dve.wait_ge(S("ada_done" if i < 2 else "piece_used"), 2 if i < 2 else 4)
                o = modc[:, 16 * i:16 * i + 16].rearrange("p (k w) -> p k w", k=8)
                link(tt(o, bank(7)[:, 16 * i:16 * i + 16].rearrange("p (k w) -> p k w", k=8),
                        bada[:, 8 * m:8 * m + 8].unsqueeze(2).to_broadcast([P, 8, 2]), ALU.add))
                if i % 2:
                    o = modc[:, 16 * i:16 * i + 16]
                    link(ts(o, o, 1.0, None, ALU.add))
                dve.sem_inc(S("mod_ready"), 1)

            def u_evac(g):
                t0, nt = GROUPS[g]
                w = 0 if g else 1
                for k in range(1, 8, 2):
                    dve.wait_ge(S("tr_done"), 8 * g + k + 1)
                    ts(uT[:, k, P * t0:P * (t0 + nt)], bank((8 * g + k) % 4)[:, 0:P * nt], modc[:, 16 + 2 * k + w:17 + 2 * k + w],
                       modc[:, 2 * k + w:2 * k + w + 1], ALU.mult, ALU.add).then_inc(S("uT_dve"), 1)

            norm(0)
            norm(1)
            dve.wait_ge(S("const_in"), 32)
            modulation(0, 0)
            modulation(1, 1)
            u_evac(0)
            for t in range(2, NT):
                norm(t)
            u_evac(1)
            u_evac(2)
            modulation(2, 3)
            modulation(3, 4)
            for q, (idx, j, cp) in enumerate(ABJOBS):
                if idx % 2 == 1:
                    dve.wait_ge(S("ab_done"), q + 1)
                    dve.wait_ge(S("ab_act"), 2 * (idx // 2) + cp + 1)
                    lo, hi = EO[:, j - 4, 2 * cp:2 * cp + 2, :], EO[:, j, 2 * cp:2 * cp + 2, :]
                    pp = bank(1 + q % 3).rearrange("p (c n) -> p c n", c=2)
                    tt(hi, lo, pp, ALU.add)
                    tt(lo, lo, pp, ALU.subtract).then_inc(S("ab_dve"), 1)
            for c in range(4):
                bk = 0 if c % 2 else 4
                m = mixT[:, 4 + c, :]
                dve.wait_ge(S("qtmp_ready"), 2 * c + 1)
                tt(m[:, 0:513:2], bank(bk)[:, 0:NEV], qtmp[:, 0, 0:NEV], ALU.subtract)
                tt(m[:, 1022:512:-2], bank(bk)[:, 1:NEV - 1], qtmp[:, 0, 1:NEV - 1], ALU.add).then_inc(S("qtmp_used"), 1)
                dve.wait_ge(S("qtmp_ready"), 2 * c + 2)
                tt(m[:, 1:512:2], bank(bk + 2)[:, 0:NOD], qtmp[:, 1, 0:NOD], ALU.subtract)
                tt(m[:, 1023:512:-2], bank(bk + 2)[:, 0:NOD], qtmp[:, 1, 0:NOD], ALU.add).then_inc(S("qtmp_used"), 1)
            nq = 0
            for c in range(8):
                nq += 2 + (c >= 4)
                dve.wait_ge(S("cv_evac"), nq)
                if c >= 1:
                    dve.wait_ge(S("silu_done"), c)
                for tap in range(9):
                    src = cbuf[c % 2][:, tap // 3:tap // 3 + 16, tap % 3:tap % 3 + 64]
                    w = convw[:, 9 * c + tap:9 * c + tap + 1]
                    ins = ts(cacc, src, w, None, ALU.mult) if tap == 0 else stt(cacc, src, w, cacc, ALU.mult, ALU.add)
                    if tap < 8 or c >= 4:
                        link(ins)
                if c >= 4:
                    if c >= 5:
                        dve.wait_ge(S("siluc_done"), c - 4)
                    for tap in range(3):
                        src = cbufc[:, tap:tap + 256]
                        w = convw[:, 9 * c + 3 + tap:9 * c + 4 + tap]
                        ins = ts(caccc, src, w, None, ALU.mult) if tap == 0 else stt(caccc, src, w, caccc, ALU.mult, ALU.add)
                        if tap < 2:
                            link(ins)
                ins.then_inc(S("conv_done"), 1)
            link(dve.memset(G[:, :], 0.0))
            for t in range(NT):
                dve.wait_ge(S("g_done"), t + 1)
                src = bank(6 + t % 2)[:, 0:16].rearrange("p (d g h) -> p d g h", d=2, g=2)
                for d in range(2):
                    o = G[:, 32 * t + 16 * d:32 * t + 16 * d + 16].rearrange("p (g x) -> p g x", g=2)[:, :, 4 * d:4 * d + 4]
                    ins = dve.tensor_copy(o, src[:, d])
                ins.then_inc(S("g_evac"), 1)
            dve.wait_ge(S("silu_done"), 8)
            dve.wait_ge(S("siluc_done"), 4)
            for r, (s0, ns) in enumerate(((0, 4), (4, 4), (8, 2))):
                for gate in range(2):
                    q = 2 * r + gate
                    dve.wait_ge(S("rows_mm"), q + 1)
                    ts((Rf if gate else Ra)[:, P * s0:P * (s0 + ns)], bank(q % 4)[0:8, 0:P * ns], gateb[0:8, gate:gate + 1], None, ALU.add).then_inc(S("rows_evac"), 1)
            dve.wait_ge(S("rows_evac"), 6)
            link(dve.memset(mprev[0:8, 0:1], 0.0))
            link(dve.memset(zrow[0:8, :], 0.0))
            dve.wait_ge(S("rl_step"), 3)
            link(stt(Rl, Rf, 0.0, Rl, ALU.min, ALU.subtract))
            for s in range(NT):
                ins = dve.tensor_tensor_scan(Rb[:, P * s:P * s + P], Rl[:, P * s:P * s + P], zrow[0:8, :], 0.0, ALU.add, ALU.add)
            link(ins)
            link(tt(Ra, Ra, Rb, ALU.subtract))
            for s in range(NT):
                sl_ = slice(P * s, P * s + P)
                link(dve.tensor_tensor_scan(Rm[:, sl_], Ra[:, sl_], Ra[:, sl_], mprev[0:8, s:s + 1], ALU.max, ALU.max))
                link(tt(mprev[0:8, s + 1:s + 2], Rb[:, P * s + P - 1:P * s + P], Rm[:, P * s + P - 1:P * s + P], ALU.add))

            def v3(r):
                return r.rearrange("p (s n) -> p s n", s=NT)

            dve.wait_ge(S("v_done"), NT)
            dve.wait_ge(S("o_done"), NTX)
            tt(v3(Rw), v3(Ra), v3(Rm)[:, :, P - 1:P].to_broadcast([8, NT, P]), ALU.subtract).then_inc(S("wargs_ready"), 1)
            stt(Re, Rb, -1.0, Rm, ALU.mult, ALU.subtract).then_inc(S("wargs_ready"), 1)
            tt(v3(Ri), mprev[0:8, 0:NT].unsqueeze(2).to_broadcast([8, NT, P]), v3(Rm), ALU.subtract).then_inc(S("wargs_ready"), 1)
            dve.wait_ge(S("wargs_ready"), 3)
            link(ts(Rm, Rm, -1.0, None, ALU.mult))
            dve.wait_ge(S("rows_exp"), 3)
            tt(dgl[0:8, :].rearrange("p (s r) -> p s r", s=NT), cst[0:8, C_ID:C_ID + 8].unsqueeze(1).to_broadcast([8, NT, 8]),
               v3(Ri)[:, :, P - 1:P].to_broadcast([8, NT, 8]), ALU.mult).then_inc(S("rows_rev"), 1)
            dve.wait_ge(S("cols_mm"), 1)
            link(dve.tensor_copy(COL[:, :], bank(2)[:, 0:NT * 48]))
            link(dve.memset(Cst.rearrange("p b h n -> p (b h n)"), 0.0))
            dve.tensor_copy(DEC[:, :], bank(3)[:, 0:NT * 8]).then_inc(S("cols_ready"), 1)
            dve.wait_ge(S("cols_ready"), 1)
            for q, (s, d, t) in enumerate(JOBS):
                x = q - FIRSTX
                if x >= 0:
                    c = t - NTC
                    dve.wait_ge(S("I_done"), x + 1)
                    if x >= 2:
                        dve.wait_ge(S("N_done"), x - 1)
                    tt(qI[:, x % 2].rearrange("p (h n) -> p h n", h=4), qkT[:, 0:4, P * c:P * c + P],
                       bank(6).rearrange("p (h n) -> p h n", h=4), ALU.mult).then_inc(S("qI_ready"), 1)
                    dve.wait_ge(S("D_ready"), x + 1)
                    stt(Dt[:, x % 2], bank(x % 2), KSCALE, Dt[:, x % 2], ALU.mult, ALU.mult).then_inc(S("P_ready"), 1)
                    dve.wait_ge(S("N_done"), x + 1)
                    num = psN.rearrange("p (b i n) -> p b i n", b=2, i=2)
                    den4 = den[:, :].rearrange("p (b i) -> p b i", b=2)
                    c0 = s * 48 + 32 + 12 * d
                    e4 = COL[:, c0:c0 + 4].rearrange("p (b i) -> p b i", b=2)
                    link(stt(den4, num[:, :, :, DH], -1.0, e4, ALU.mult, ALU.max))
                    link(tt(den4, num[:, :, :, DH], den4, ALU.max))
                    link(dve.reciprocal(rec[:, :], den[:, :]))
                    r4 = rec[:, :].rearrange("p (b i) -> p b i", b=2).unsqueeze(3).to_broadcast([P, 2, 2, DH])
                    tgt = H[:, c] if s - NTC < 4 else htmp
                    ins = tt(tgt.rearrange("p (b i n) -> p b i n", b=2, i=2), num[:, :, :, 0:DH], r4, ALU.mult)
                    ins.then_inc(S("h_read"), 1)
                    if s - NTC >= 4:
                        dve.wait_ge(S("h_read"), x + 1)
                        link(tt(H[:, c], H[:, c], htmp, ALU.add))
                for half in range(2):
                    dve.wait_ge(S("U_half"), 2 * q + half + 1)
                    for i in range(2):
                        h = 2 * half + i
                        dc = DEC[:, 8 * s + 4 * d + h:8 * s + 4 * d + h + 1]
                        ins = stt(Cst[:, d, h], Cst[:, d, h], dc, bank(6 if half else 7)[:, 256 * i:256 * i + VW], ALU.mult, ALU.add)
                    ins.then_inc(S("C_half"), 1)
            dve.wait_ge(S("C_half"), 2 * NJ)
            dve.sem_inc(S("h_done"), 16)
            dve.wait_ge(S("wout_in"), 32)
            link(ts(hgB, hgB, 0.5, None, ALU.mult))
            for j in range(NTX):
                for h in range(4):
                    ins = dve.bn_stats(hst[:, 6 * h:6 * h + 6], H[:, j, P * h:P * h + P])
                link(ins)
                for h in range(4):
                    ins = dve.bn_aggr(hmv[:, j % 2, h], hst[:, 6 * h:6 * h + 6])
                ins.then_inc(S("hmv_ready"), 1)
                link(stt(og, O[:, j], 1.0, hgB, ALU.add, ALU.mult))
                dve.wait_ge(S("hrstd_ready"), j + 1)
                for h in range(4):
                    hh = H[:, j, P * h:P * h + P]
                    ins = ts(hh, hh, hmv[:, j % 2, h, 0:1], hrstd[:, j % 2, h:h + 1], ALU.subtract, ALU.mult)
                link(ins)
                tt(H[:, j], H[:, j], og, ALU.mult).then_inc(S("mix_ready"), 1)
            dve.wait_ge(S("rows1_in"), 64)
            dve.wait_ge(S("mixt_done"), NTX)
            link(tt(g1B, g1B, ytmp[:, 0], ALU.add))
            for j in range(NTX + 1):
                if j < NTX:
                    y = ytmp[:, j % 2]
                    dve.wait_ge(S("proj_done"), j + 1)
                    tt(y, psN if j % 2 == 0 else psY, g1B, ALU.mult).then_inc(S("y_read"), 1)
                    dve.wait_ge(S("y_read"), j + 1)
                    dve.wait_ge(S(f"xres_in{j % 2}"), 16 * (j // 2 + 1))
                    stt(y, xres[:, j % 2], ALPHA, y, ALU.mult, ALU.add).then_inc(S("res_used"), 1)
                    dve.wait_ge(S("res_used"), j + 1)
                    moments(y, mvj[:, j % 2], "y_mv")
                    dve.wait_ge(S("y_rstd"), j + 1)
                    ts(y, y, mvj[:, j % 2, 0:1], rstd[:, j % 2:j % 2 + 1], ALU.subtract, ALU.mult).then_inc(S("y_norm"), 1)
                if j >= 1:
                    i = j - 1
                    dve.wait_ge(S("y_gain"), i + 1)
                    link(tt(x1[:, i], ytmp[:, i % 2], lb1, ALU.add))
                    moments(x1[:, i], mvk[:, i % 2], "x1_mv")
                    dve.wait_ge(S("x1_rstd"), i + 1)
                    if i >= 2:
                        dve.wait_ge(S(f"t_out{i % 2}"), 16 * (i // 2))
                        dve.wait_ge(S("tt_done"), i - 1)
                    if i == 0:
                        dve.wait_ge(S("rows_evac2"), 1)
                    link(stt(lnt[:, i % 2], x1[:, i], mvk[:, i % 2, 0:1], sc2B, ALU.subtract, ALU.mult))
                    stt(lnt[:, i % 2], lnt[:, i % 2], rstd[:, 2 + i % 2:3 + i % 2], sh2B, ALU.mult, ALU.add).then_inc(S("ln_ready"), 1)
            def t3(x):
                return x.rearrange("p (j e) -> p j e", j=8)

            def shared(j):
                dve.wait_ge(S("s_sg"), j + 1)
                tt(hxL[:, j % 2], sgL[:, j % 2], bank(3 + j % 2)[:, DE:2 * DE], ALU.mult).then_inc(S("s_hx"), 1)

            def shared_y(j):
                dve.wait_ge(S("sdown_done"), j + 1)
                if j >= 2:
                    dve.wait_ge(S(f"acc_out{j % 2}"), 16 * (j // 2))
                dve.tensor_copy(yB[:, j % 2, 512:1024], bank(6)).then_inc(S("sy_dve"), 1)

            dve.wait_ge(S("sc_ready"), 1)
            dve.wait_ge(S("wr_in"), 32)
            link(dve.memset(zr, 0.0))
            link(tt(t3(bs), t3(sc), rbB.unsqueeze(1).to_broadcast([P, 8, NE]), ALU.add))
            for j in range(8):
                link(dve.max(m8[:, 8 * j:8 * j + 8], bs[:, NE * j:NE * j + NE]))
                link(dve.match_replace(rp[:, NE * j:NE * j + NE], m8[:, 8 * j:8 * j + 8], bs[:, NE * j:NE * j + NE], -BIG))
            ts(mk, rp, -BIG, None, ALU.is_equal).then_inc(S("mask_ready"), 1)
            dve.wait_ge(S("mask_ready"), 1)
            shared(0)
            link(tt(wt, sc, mk, ALU.mult))
            link(dve.tensor_reduce(ssum, t3(wt), AX, ALU.add))
            link(dve.reciprocal(ssum, ssum))
            link(ts(ssum, ssum, ROUTED, None, ALU.mult))
            tt(t3(wt), t3(wt), ssum.unsqueeze(2).to_broadcast([P, 8, NE]), ALU.mult).then_inc(S("wt_ready"), 1)
            shared_y(0)
            dve.wait_ge(S("pos_done"), 1)
            link(ts(cnti, bank(1)[:, 0:NE], float(P - 1), None, ALU.add))
            link(ts(cnti, cnti, 7, None, ALU.arith_shift_right))
            link(dve.tensor_copy(nbf, cnti))
            link(ts(nbf, nbf, 1.0, None, ALU.max))
            link(dve.tensor_tensor_scan(bend, nbf, zr, 0.0, ALU.add, ALU.add))
            link(tt(bbase, bend, nbf, ALU.subtract))
            link(ts(bbase, bbase, float(P), 1.0, ALU.mult, ALU.add))
            link(ts(n2, bend, cst[:, C_P:C_P + 1], None, ALU.is_le))
            link(dve.tensor_reduce(ebc, n2, AX, ALU.add))
            ts(ebc, ebc, float(NE - 1), None, ALU.min).then_inc(S("eb_ready"), 1)
            link(tt(t3(sl), t3(bank(0)), bbase.unsqueeze(1).to_broadcast([P, 8, NE]), ALU.add))
            link(tt(sl, sl, mk, ALU.mult))
            shared(1)
            for j in range(8):
                ins = dve.max(m8[:, 8 * j:8 * j + 8], sl[:, NE * j:NE * j + NE])
            link(ins)
            link(ts(s8i, m8, -1.0, None, ALU.add))
            link(ts(b8i, s8i, 7, None, ALU.arith_shift_right))
            link(ts(s8i, s8i, P - 1, None, ALU.bitwise_and))
            link(dve.tensor_copy(p8, s8i))
            link(dve.tensor_copy(b8, b8i))
            shared_y(1)
            shared(2)
            shared_y(2)
            link(ts(pairs_rest[:, :], bend[0:1, NE - 1:NE], 1.0, None, ALU.add))
            link(ts(pairs_rest[:, :], pairs_rest[:, :], 1, None, ALU.arith_shift_right))
            link(ts(pairs_rest[:, :], pairs_rest[:, :], -1.0, None, ALU.add))
            dve.wait_ge(S("eb_mm"), 1)

            def trow(r):
                return tbl[:, r:r + P]

            link(dve.tensor_copy(trow(T_E), bank(1)[0:1, 0:P]))

            link(tt(trow(T_NEW)[:, 1:P], trow(T_E)[:, 1:P], trow(T_E)[:, 0:P - 1], ALU.not_equal))
            link(dve.memset(trow(T_NEW)[:, 0:1], 1))
            link(ts(tblf[:, :], trow(T_E), float(NE - 1), None, ALU.is_lt))
            link(tt(trow(T_NEW), trow(T_NEW), tblf[:, :], ALU.mult))
            link(stt(trow(T_WORD), trow(T_NEW), 64.0, trow(T_E), ALU.mult, ALU.add))
            link(dve.memset(tbl[:, P:P + 2], 0))
            for q in range(64):
                j, k = q // 8, q % 8
                if q >= 2:
                    dve.wait_ge(S("onehot_used"), q - 1)
                ts(oneP[:, q % 2], iota, p8[:, q:q + 1], None, ALU.is_equal)
                ts(oneB[:, q % 2], iota, b8[:, q:q + 1], cst[:, C_TOK + j:C_TOK + j + 1], ALU.is_equal, ALU.mult).then_inc(S("onehot_ready"), 1)
            dve.wait_ge(S("onehot_used"), 64)
            pad = cst[:, C_PADROW:C_PADROW + 1]
            link(ts(Ttmp[:, 0], bank(2)[:, 0:P], 0.0, pad, ALU.is_equal, ALU.mult))
            link(tt(Ttmp[:, 1], bank(2)[:, 0:P], Ttmp[:, 0], ALU.add))
            link(ts(idxT[:, 0:P], Ttmp[:, 1], -1.0, None, ALU.add))
            ts(idxT[:, P:P + 2], cst[:, C_PADROW:C_PADROW + 1].to_broadcast([P, 2]), -1.0, None, ALU.add).then_inc(S("idx_ready"), 1)
            dve.wait_ge(S("idx_ready"), 1)
            dve.sem_inc(S("table_ready"), 1)
            for j in range(3, NTX):
                shared(j)
                shared_y(j)
            def word(b):
                return word_of(dve, b)

            def x_low(b, p, w):
                dve.wait_ge(S("m_xh"), b + 1)
                dve.tensor_copy(gcol[:, p:p + 1], xg[:, p, D:XW][:, bass.ds(w & 63, 1)])
                tt(xTl[p], psum[:, 0:1024], xTh[p].bitcast(F32), ALU.subtract).then_inc(S("m_xb"), 1)

            def h_low(b):
                dve.wait_ge(S("m_hh"), b + 1)
                tt(hTl, bank(7)[:, 0:2 * P], hTh.bitcast(F32), ALU.subtract).then_inc(S("m_hT"), 1)

            def w_low(e, par, chunks):
                for c in chunks:
                    dve.wait_ge(S("hi_split"), 6 * e + (c + 1))
                    high = cols(wsplit, par * (2 * WE) + 1024 * c, 1024).bitcast(F32)
                    tt(cols(wsplit, par * (2 * WE) + (WE + 1024 * c), 1024), cols(raw, par * WE + 1024 * c, 1024), high,
                       ALU.subtract).then_inc(S("lo_split"), 1)

            def h_rows(b, p):
                dve.wait_ge(S("m_xb"), b + 1)
                dve.wait_ge(S("m_sg"), b + 1)
                stt(hx[:, p], bank(3 + p)[:, DE:2 * DE], gcol[:, p:p + 1], sg[:, p], ALU.mult, ALU.mult).then_inc(S("m_hx"), 1)

            w_low(0, 0, range(6))
            x_low(0, 0, word(0))
            x_low(1, 1, word(1))
            w_low(1, 1, range(4))
            h_rows(0, 0)

            def step(b, p, w0, w1, w2):
                h_low(b - 1)
                x_low(b + 1, 1 - p, w2)
                if w0 is None:
                    w_low(1, 1, range(4, 6))
                else:
                    with dve.If_ne(dve.to_reg((w0 >> 6) & 1), 0):
                        w_low((w0 & 63) + 1, 1 - (w0 & 1), range(4, 6))
                first, e1, par1 = (w1 >> 6) & 1, (w1 & 63) + 1, 1 - (w1 & 1)
                with dve.If_ne(dve.to_reg(first), 0):
                    w_low(e1, par1, range(2))
                h_rows(b, p)
                with dve.If_ne(dve.to_reg(first), 0):
                    w_low(e1, par1, range(2, 4))

            step(1, 1, None, word(1), word(2))
            rest = dve.value_load(pairs_rest[0:1, 0:1], min_val=NE // 2 - 1, max_val=MAXB // 2 - 1)
            with dve.Fori(0, rest) as i:
                w0, w1, w2 = word(2 * i + 1), word(2 * i + 2), word(2 * i + 3)
                step(2 * i + 2, 0, w0, w1, w2)
                w3 = word(2 * i + 4)
                step(2 * i + 3, 1, w1, w2, w3)
            h_low(2 * rest + 1)
            dve.wait_ge(S("rows2_in"), 64 + 16 * NTX)
            link(tt(g2B, g2B, acc_tmp, ALU.add))
            for j in range(NTX + 1):
                if j < NTX:
                    y = acc_in[j]
                    dve.wait_ge(S(f"accin{j // 4}"), 64)
                    link(tt(y, y, g2B, ALU.mult))
                    link(stt(y, x1_in[j], ALPHA, y, ALU.mult, ALU.add))
                    moments(y, mvj[:, j % 2], "y_mv")
                    dve.wait_ge(S("y_rstd"), NTX + j + 1)
                    ts(y, y, mvj[:, j % 2, 0:1], rstd[:, j % 2:j % 2 + 1], ALU.subtract, ALU.mult).then_inc(S("y_norm"), 1)
                if j >= 1:
                    dve.wait_ge(S("y_gain"), NTX + j)
                    tt(acc_in[j - 1], acc_in[j - 1], lb2, ALU.add).then_inc(S("out_ready"), 1)


def kernel(**inputs):
    import concourse.bacc as bacc
    from concourse.bass_utils import run_bass_kernel_spmd

    def flat(name):
        return np.asarray(inputs[name])

    const, dft = constant_tiles()
    w_in = flat("w_in")[0]
    cc = np.stack([flat("c")[0], flat("c_ctx")], axis=-1).reshape(P, 16)
    gate_b = flat("gate_b")[0]
    arrays = {
        "toks": np.concatenate([flat("ctx")[0], flat("x")[0]], axis=0),
        "cc": cc,
        "const": const,
        "dft": dft,
        "w_ada": flat("w_ada")[0],
        "b_ada": flat("b_ada"),
        "w_qk": w_in[:, 0:2 * DM],
        "w_vog": w_in[:, 2 * DM:4 * DM + 16],
        "w_f": w_in[:, 4 * DM + 16:],
        "conv_wt": flat("conv_w")[0].reshape(9, 8, P).transpose(2, 1, 0).reshape(P, 72),
        "conv_bt": flat("conv_b")[0].reshape(8, P).T,
        "gate_bt": gate_b.transpose(0, 2, 1).reshape(8, 2),
        "head_g": flat("head_g"),
        "w_out": flat("w_out")[0],
        "ln1_g": flat("ln1_g"), "ln1_b": flat("ln1_b"), "ln2_g": flat("ln2_g"), "ln2_b": flat("ln2_b"),
        "w_router": flat("w_router")[0],
        "router_bias": flat("router_bias"),
        "w_gu": flat("w_expert_gu")[0].reshape(NE * P, 8 * 2 * DE),
        "w_dn": flat("w_expert_down")[0].reshape(NE * P, 2 * D),
        "w_shared_gu": flat("w_shared_gu")[0],
        "w_shared_down": flat("w_shared_down")[0],
    }
    nc = bacc.Bacc("TRN2", target_bir_lowering=False, num_devices=1)
    feed, aps = {}, {}
    for name, v in arrays.items():
        v = np.ascontiguousarray(v)
        feed[f"in_{name}"] = v
        aps[name] = nc.dram_tensor(f"in_{name}", v.shape, F32, kind="ExternalInput").ap()
    out = nc.dram_tensor("out_0", (SEQ, D), F32, kind="ExternalOutput").ap()
    build(nc, aps, out)
    r = run_bass_kernel_spmd(nc, [feed], core_ids=[0])
    return r.results[0]["out_0"].reshape(1, SEQ, D)
```

```python
from contextlib import ExitStack

import numpy as np

import concourse.bass as bass
from concourse import mybir

P = 128
D = 1024
KT = D // P
SEQ = 1024
CTX = 256
NTC = CTX // P
NTX = SEQ // P
NT = NTC + NTX
HEADS = 4
DH = 128
DM = HEADS * DH
DF = 512
VW = DH + 1
NE = 64
TOPK = 8
DE = 256
ROWS_OUT = SEQ + P
XW = D + NE
MAXB = P
NBUF = 2
WE = KT * 2 * DE + (DE // P) * D
ALPHA = 2.0 ** 0.25
EPS = 1e-5
KSCALE = DH ** -0.5
ROUTED = 2.5
BIG = 1e30
NEV = SEQ // 4 + 1
NOD = SEQ // 4
GW = 66
GH = 18

ALU = mybir.AluOpType
ACT = mybir.ActivationFunctionType
AX = mybir.AxisListType.X
F32 = mybir.dt.float32
I32 = mybir.dt.int32
U32 = mybir.dt.uint32
F32R = mybir.dt.float32r

C_ID, C_REV, C_MF, C_MB, C_ONE, C_LT, C_IOTA, C_SEL = (i * P for i in range(8))
C_HALF = C_SEL + 8 * P
C_PADROW = C_HALF + 16
C_TOK = C_PADROW + 1
C_P = C_TOK + 8
C_CD = C_P + 7
C_END = C_CD + 256
ARENA = 48192


def constant_tiles():
    p = np.arange(P)
    c = np.zeros((P, C_END), np.float32)
    c[p, C_ID + p] = 1
    c[p, C_REV + P - 1 - p] = 1
    c[:, C_MF:C_MF + P] = np.where(p[:, None] <= p[None, :], 0, -BIG)
    c[:, C_MB:C_MB + P] = np.where(p[:, None] >= p[None, :], 0, -BIG)
    c[:, C_ONE:C_ONE + P] = 1
    c[:, C_LT:C_LT + P] = p[:, None] < p[None, :]
    c[:, C_IOTA:C_IOTA + P] = p[None, :]
    for r in range(8):
        c[r, C_SEL + r * P:C_SEL + (r + 1) * P] = 1
    c[:, C_HALF:C_HALF + 16] = -0.5
    c[:, C_PADROW] = SEQ + p + 1
    c[:, C_TOK:C_TOK + 8] = p[:, None] + P * np.arange(8)[None, :] + 1
    c[:, C_P] = p
    g = 64
    m = np.arange(g)
    ang = 2 * np.pi * (np.outer(m, m) % g) / g
    scale = 1.0 / np.sqrt(SEQ * g)
    for b in range(2):
        s = slice(b * g, (b + 1) * g)
        c[s, C_CD + b * g:C_CD + (b + 1) * g] = np.cos(ang) * scale
        c[s, C_CD + P + b * g:C_CD + P + (b + 1) * g] = np.sin(ang) * scale
    n = np.arange(SEQ // 2)
    ev = 2 * np.pi * (np.outer(n, 2 * np.arange(NEV)) % SEQ) / SEQ
    od = 2 * np.pi * (np.outer(n, 2 * np.arange(NOD) + 1) % SEQ) / SEQ
    dft = np.concatenate([np.cos(ev), np.sin(ev), np.cos(od), np.sin(od)], axis=1).astype(np.float32)
    return c, np.ascontiguousarray(dft)


def build(nc, a, out):
    ctx = ExitStack()
    with ctx:
        def sb(name, cols, dt=F32, parts=P):
            return ctx.enter_context(nc.sbuf_tensor(name, [parts, cols], dt))

        sems = {}

        def sem(name):
            if name not in sems:
                sems[name] = ctx.enter_context(nc.semaphore(name))
            return sems[name]

        cst = sb("cst", C_END)
        A0, B0, C0, D0 = 0, 10240, 19496, 40000
        arena_base = (nc.sbuf_base + 31) // 32 * 32
        arena = sb("arena", ARENA)

        def at(o, n):
            return arena[:, o:o + n]

        ident = cst[:, C_ID:C_ID + P]
        rev = cst[:, C_REV:C_REV + P]
        ones = cst[:, C_ONE:C_ONE + P]
        iota = cst[:, C_IOTA:C_IOTA + P]

        ccol = sb("ccol", 16)
        silc = sb("silc", 16)
        modc = sb("modc", 2 * 16)
        convw = sb("convw", 8 * 9)
        convb = sb("convb", 8)
        gateb = sb("gateb", 2)
        stats = sb("stats", 12)
        mv = sb("mv", 2 * NT)
        veps = sb("veps", NT)
        rstd = sb("rstd", NT)
        G = sb("G", NT * 32)
        mprev = sb("mprev", NT + 1)
        COL = sb("COL", NT * 48)
        dgl = sb("dgl", NT * 8)
        DEC = sb("DEC", NT * 8)
        den = sb("den", 4)
        rec = sb("rec", 4)
        idxg = sb("idxg", 2, U32)
        idxs = sb("idxs", 2, U32)
        zrow = sb("zrow", P, parts=8)
        hst = sb("hst", 24)
        hmv = sb("hmv", 16)[:, :].rearrange("p (b h n) -> p b h n", b=2, h=4)
        hveps = sb("hveps", 8)[:, :].rearrange("p (b h) -> p b h", b=2)
        hrstd = sb("hrstd", 8)[:, :].rearrange("p (b h) -> p b h", b=2)
        hbias = sb("hbias", 8)[:, :].rearrange("p (b h) -> p b h", b=2)
        mvj = sb("mvj", 4)[:, :].rearrange("p (b n) -> p b n", b=2)
        mvk = sb("mvk", 4)[:, :].rearrange("p (b n) -> p b n", b=2)

        def overlay(name, o, cols, dt):
            return nc.alloc_sbuf_tensor_at(name, [P, cols], dt, offset=arena_base + 4 * o)

        psum = ctx.enter_context(nc.psum_tensor("psum", [P, 8 * 512], F32))
        psN = psum[:, 3 * 512:5 * 512]
        psY = psum[:, 5 * 512:7 * 512]

        def bank(i):
            return psum[:, 512 * i:512 * i + 512]

        ada = [at(C0, 8192).rearrange("p (k n) -> p k n", k=8), at(C0 + 8192, 8192).rearrange("p (k n) -> p k n", k=8)]
        piece = [at(D0, 4096).rearrange("p (k n) -> p k n", k=4), at(D0 + 4096, 4096).rearrange("p (k n) -> p k n", k=4)]
        xin = [at(B0 + 1024 * t, 1024) for t in range(9)] + [at(C0, 1024)]
        rows01 = [arena[0:2, A0 + 1024 * v:A0 + 1024 * (v + 1)] for v in range(2)]
        mrow = arena[0:1, B0 + 8192:B0 + 9216]
        uT = at(A0, 10240).rearrange("p (k n) -> p k n", k=8)
        wf = at(C0 + 16396, 4096).rearrange("p (k n) -> p k n", k=8)
        fT = at(C0, 4096).rearrange("p (c n) -> p c n", c=4)
        EO = at(C0 + 4096, 8192).rearrange("p (s c n) -> p s c n", s=8, c=4)
        CSW = 2 * NEV + 2 * NOD
        CS = at(C0 + 12288, 4 * CSW).rearrange("p (j n) -> p j n", j=4)
        qtmp = at(C0 + 16400, 2 * 260).rearrange("p (b n) -> p b n", b=2)
        mixT = at(D0, 8192).rearrange("p (k n) -> p k n", k=8)
        wqk = at(B0, 8192).rearrange("p (k n) -> p k n", k=8)
        cbuf = [at(D0 + 1188 * i, 1188).rearrange("p (r c) -> p r c", r=GH) for i in range(2)]
        cacc = at(D0 + 2376, 1024).rearrange("p (r c) -> p r c", r=16)
        cbufc = at(D0 + 3400, 258)
        caccc = at(D0 + 3658, 256)
        qkT = at(C0, 8192).rearrange("p (c n) -> p c n", c=8)
        kTc = at(C0 + 8192, 1024).rearrange("p (c n) -> p c n", c=4)
        wvog = at(C0 + 9216, 8320).rearrange("p (k n) -> p k n", k=8)
        V = at(B0, NT * 4 * VW).rearrange("p (t h n) -> p t h n", t=NT, h=4)
        O = at(B0 + NT * 4 * VW, 4096).rearrange("p (t n) -> p t n", t=NTX)
        NR = NT * P

        def row(o):
            return arena[0:8, o:o + NR]

        Ra, Rf, Rl = row(D0), row(D0 + NR), row(D0 + 2 * NR)
        Ri, Rw, Re = (row(C0 + 9216 + i * NR) for i in range(3))
        Rb, Rm = (row(C0 + 17536 + i * NR) for i in range(2))
        stack = at(C0 + 9216 + 3 * NR, 2 * NR).rearrange("p (d n) -> p d n", d=2)
        kM = at(A0, 5120).rearrange("p (t n) -> p t n", t=NT)
        H = at(A0 + 5120, 4096).rearrange("p (t n) -> p t n", t=NTX)
        qI = at(A0 + 9216, 1024).rearrange("p (b n) -> p b n", b=2)
        HB = C0 + 9216 + 3 * NR
        Dt = at(HB, 1024).rearrange("p (b n) -> p b n", b=2)
        vw = at(HB + 1024, 1032).rearrange("p (b h n) -> p b h n", b=2, h=4)
        Cst = at(HB + 2056, 1032).rearrange("p (b h n) -> p b h n", b=2, h=4)
        htmp = at(HB + 3088, 512)
        maskr = overlay("maskr", HB + 3600, 3 * P, F32R)
        hgB = at(C0 + 8192, 512)
        wout = at(C0, 8192).rearrange("p (k n) -> p k n", k=8)
        x1 = at(A0, 2048).rearrange("p (b n) -> p b n", b=2)
        g1B, lg1, lb1 = (at(B0 + i * 1024, 1024) for i in range(3))
        sc2B, sh2B = (at(B0 + 7168 + i * 1024, 1024) for i in range(2))
        xres = at(B0 + 3072, 2048).rearrange("p (b n) -> p b n", b=2)
        ytmp = at(B0 + 5120, 2048).rearrange("p (b n) -> p b n", b=2)
        tT = at(C0 + 8192, 8192).rearrange("p (k n) -> p k n", k=8)
        lnt = at(C0 + 16384, 2 * 1024).rearrange("p (b n) -> p b n", b=2)
        wr = at(C0 + 18432, 512).rearrange("p (k n) -> p k n", k=8)
        rbB = at(C0 + 18432 + 512, 64)
        KB = 2 * WE + 1024
        sc, bs, rp, wt, sl = (at(KB + i * 512, 512) for i in range(5))
        KC = KB + 8 * 512
        m8 = at(KC, 64)
        s8 = at(KC + 64, 64)
        ssum = at(KC + 128, 8)
        cnt, nbf, bend, bbase, zr, n2 = (at(KC + 136 + 64 * i, 64) for i in range(6))
        cnti = arena[:, KC + 520:KC + 584].bitcast(I32)
        p8 = at(KC + 584, 64)
        b8 = at(KC + 648, 64)
        s8i = arena[:, KC + 712:KC + 776].bitcast(I32)
        b8i = arena[:, KC + 776:KC + 840].bitcast(I32)
        ebc = at(KC + 840, 1)
        zpad = at(KC + 848, XW)
        NOH = 4
        onehot = overlay("onehot", C0 + 16384, 2 * NOH * P + 2 * P, F32R)
        oneP = onehot[:, 0:NOH * P].rearrange("p (b n) -> p b n", b=NOH)
        oneB = onehot[:, NOH * P:2 * NOH * P].rearrange("p (b n) -> p b n", b=NOH)
        lt_r, ones_r = (onehot[:, (2 * NOH + i) * P:(2 * NOH + i + 1) * P] for i in range(2))
        mask_r = overlay("mask", C0 + 16384 + 2 * NOH * P + 2 * P, 512, F32R)
        Ttmp = at(C0 + 16384, 256).rearrange("p (b n) -> p b n", b=2)
        idxT = sb("idxT", P + 2, U32)
        tbl = sb("tbl", 3 * P + 2, I32, parts=1)
        T_WORD, T_E, T_NEW = 0, P + 2, 2 * P + 2
        tblf = sb("tblf", P, parts=1)
        pairs_rest = sb("pairs_rest", 1, I32, parts=1)
        sgL, hxL, hTL = (at(A0 + 8192 + 512 * i, 512).rearrange("p (b n) -> p b n", b=2) for i in range(3))
        hTL = hTL.rearrange("p b (k n) -> p b k n", k=2)
        wsgu = at(A0 + 2048, 4096).rearrange("p (k n) -> p k n", k=8)
        wsd = at(A0 + 6144, 2048).rearrange("p (k n) -> p k n", k=2)
        wsplit = overlay("split_weights", A0, 4 * WE, F32R)
        xg = at(4 * WE, 2 * XW).rearrange("p (b n) -> p b n", b=2)
        MX = 4 * WE + 2 * XW
        xh = overlay("split_rows", MX, 4 * 1024 + 4 * P, F32R)
        xTh = [xh[:, 2048 * i:2048 * i + 1024] for i in range(2)]
        xTl = [xh[:, 2048 * i + 1024:2048 * i + 2048] for i in range(2)]
        hTh, hTl = xh[:, 4096:4096 + 2 * P], xh[:, 4096 + 2 * P:4096 + 4 * P]
        sg, hx = (at(MX + 4096 + 4 * P + 512 * i, 512).rearrange("p (b n) -> p b n", b=2) for i in range(2))
        raw = overlay("raw_weights", D0 - WE, 2 * WE, F32)
        assert MX + 4096 + 4 * P + 1024 <= D0 - WE
        yB = at(D0 + 6144, 2048).rearrange("p (b n) -> p b n", b=2)
        gcol = sb("gcol", 2)
        g2B, lg2, lb2 = (at(D0 - WE + i * 1024, 1024) for i in range(3))
        acc_in = [at(A0 + 1024 * i, 1024) for i in range(8)]
        x1_in = [at(D0 - WE + 4096 + 1024 * i, 1024) for i in range(8)]

        x1_dram = nc.dram_tensor("x1_rows", [SEQ, D], F32, kind="Internal").ap()
        t_dram = nc.dram_tensor("t_rows", [ROWS_OUT, XW], F32, kind="Internal").ap()
        acc = nc.dram_tensor("moe_sum", [ROWS_OUT, D], F32, kind="Internal").ap()
        grow = nc.dram_tensor("modulation_rows", [4, D], F32, kind="Internal").ap()

        def cols(t, o, n):
            return t[:, o:o + n] if isinstance(o, int) else t[:, bass.ds(o, n)]

        def word_of(engine, b):
            return engine.value_load(cols(tbl, b, 1), min_val=0, max_val=127)

        def drows(w, n0, n1):
            return w.rearrange("(p k) n -> p k n", k=8)[:, :, n0:n1]

        def tiles_of(s):
            return (s, NTC - 1 - s) if s < NTC else (s, NTC + NT - 1 - s)

        ABJOBS = [(i, j, cp) for i, j in enumerate((0, 4, 1, 5, 2, 6, 3, 7)) for cp in range(2)]
        QKJOBS = [(c, part) for c in range(8) for part in range(3 if c >= 4 else 2)]
        JOBS = [(s, d, tiles_of(s)[d]) for s in range(NT) for d in range(2)]
        NJ = len(JOBS)
        POOL_GAINS = (3, 5, 7)
        FIRSTX = 2 * NTC
        HTILES = [t - NTC for s, d, t in JOBS[FIRSTX + NTX:]]
        PIECES = [(m, h) for m in (2, 3, 4, 5) for h in range(2)]
        ROWBANKS = {2: (6, 0), 3: (7, 1), 4: (6, 0), 5: (7, 1)}
        XG = [0] * 2 + [1] * 4 + [2] * 4
        GROUPS = [(0, 2), (2, 4), (6, 4)]

        block = ctx.enter_context(nc.Block())
        S = sem

        @block.sync
        def _(sp):
            sp.dma_start(ccol[:, :], a["cc"]).then_inc(S("c_in"), 16)
            for m in range(2):
                sp.dma_start(rows01[m], a["b_ada"][0:1, m * D:(m + 1) * D].to_broadcast([2, D])).then_inc(S("b_in"), 16)

            def load_x(tiles):
                for t in tiles:
                    sp.dma_start(xin[t], a["toks"][P * t:P * t + P, :]).then_inc(S(f"x_in{XG[t]}"), 16)

            def load_ada(m, h):
                sp.dma_start(ada[m][:, 4 * h:4 * h + 4, :], drows(a["w_ada"], m * D, (m + 1) * D)[:, 4 * h:4 * h + 4, :]).then_inc(S(f"ada_in{2 * m + h}"), 16)

            load_ada(0, 0)
            load_x(range(2))
            load_ada(0, 1)
            sp.dma_start(cst[:, :], a["const"]).then_inc(S("const_in"), 16)
            load_x(range(2, 6))
            load_ada(1, 0)
            load_x(range(6, 9))
            sp.wait_ge(S("ada_done"), 1)
            load_x((9,))
            load_ada(1, 1)
            sp.dma_start(wf, drows(a["w_f"], 0, DF)).then_inc(S("wf_in"), 16)
            sp.dma_start(convw[:, :], a["conv_wt"]).then_inc(S("small_in"), 16)
            sp.dma_start(convb[:, :], a["conv_bt"]).then_inc(S("small_in"), 16)
            sp.dma_start(gateb[0:8, :], a["gate_bt"]).then_inc(S("small_in"), 16)
            for i, (m, h) in enumerate(PIECES):
                if i >= 2:
                    sp.wait_ge(S("piece_used"), i - 1)
                sp.dma_start(piece[i % 2], drows(a["w_ada"], m * D, (m + 1) * D)[:, 4 * h:4 * h + 4, :]).then_inc(S(f"piece_in{i % 2}"), 16)
                if i == 2:
                    sp.wait_ge(S("ada_done"), 2)
                    sp.dma_start(CS, a["dft"].rearrange("(j p) n -> p j n", p=P)).then_inc(S("cs_in"), 16)
                if i == 3:
                    sp.wait_ge(S("tr_done"), 24)
                    sp.dma_start(wqk, drows(a["w_qk"], 0, D)).then_inc(S("wqk_in"), 16)
            sp.wait_ge(S("fourier_mm"), 16)
            sp.wait_ge(S("qtmp_used"), 8)
            sp.dma_start(wvog, drows(a["w_vog"], 0, 1040)).then_inc(S("wvog_in"), 16)
            sp.wait_ge(S("kM_evac"), NT)
            sp.dma_start(hgB, a["head_g"].to_broadcast([P, DM])).then_inc(S("hg_in"), 16)
            sp.wait_ge(S("SD_done"), 16)
            sp.dma_start(wout[:, 4:8], a["w_out"].rearrange("(k p) n -> p k n", p=P)[:, 4:8]).then_inc(S("woutf_in"), 16)
            sp.wait_ge(S("qI_ready"), 16)
            sp.dma_start(wout[:, 0:4], a["w_out"].rearrange("(k p) n -> p k n", p=P)[:, 0:4]).then_inc(S("wout_in"), 16)
            sp.wait_ge(S("mix_ready"), NTX)
            sp.wait_ge(S("mrow_out"), 64)
            sp.dma_start(g1B, grow[0:1, :].to_broadcast([P, D])).then_inc(S("rows1_in"), 16)
            sp.dma_start(lg1, a["ln1_g"].to_broadcast([P, D])).then_inc(S("rows1_in"), 16)
            sp.dma_start(lb1, a["ln1_b"].to_broadcast([P, D])).then_inc(S("rows1_in"), 16)
            sp.dma_start(sh2B, grow[1:2, :].to_broadcast([P, D])).then_inc(S("rows1_in"), 16)
            sp.dma_start(sc2B, grow[2:3, :].to_broadcast([P, D])).then_inc(S("rows1_in"), 16)
            for j in range(NTX):
                if j >= 2:
                    sp.wait_ge(S("res_used"), j - 1)
                sp.dma_start(xres[:, j % 2, :], a["toks"][P * (NTC + j):P * (NTC + j + 1), :]).then_inc(S(f"xres_in{j % 2}"), 16)
                if j == 4:
                    sp.wait_ge(S("mixt_done"), NTX)
                    sp.dma_start(wr, drows(a["w_router"], 0, NE)).then_inc(S("ws_in"), 16)
                    sp.dma_start(rbB, a["router_bias"].to_broadcast([P, NE])).then_inc(S("ws_in"), 16)
                    sp.dma_start(wsgu, drows(a["w_shared_gu"], 0, 2 * DE)).then_inc(S("ws_in"), 16)
                if j == 6:
                    sp.dma_start(wsd, a["w_shared_down"].rearrange("(p k) n -> p k n", k=2)).then_inc(S("ws_in"), 16)
                if j >= 1:
                    sp.wait_ge(S("ln_ready"), j)
                    sp.dma_start(t_dram[P * (j - 1):P * j, 0:D], lnt[:, (j - 1) % 2, :]).then_inc(S(f"t_out{(j - 1) % 2}"), 16)
                    sp.dma_start(x1_dram[P * (j - 1):P * j, :], x1[:, (j - 1) % 2]).then_inc(S(f"x1_out{(j - 1) % 2}"), 16)
            sp.wait_ge(S("ln_ready"), NTX)
            sp.dma_start(t_dram[P * (NTX - 1):P * NTX, 0:D], lnt[:, (NTX - 1) % 2, :]).then_inc(S(f"t_out{(NTX - 1) % 2}"), 16)
            sp.dma_start(x1_dram[P * (NTX - 1):P * NTX, :], x1[:, (NTX - 1) % 2]).then_inc(S(f"x1_out{(NTX - 1) % 2}"), 16)

            def load_expert(e, i):
                w = raw[:, WE * (1 - i):WE * (1 - i) + WE]
                rows = slice(e * P, e * P + P) if isinstance(e, int) else bass.ds(e * P, P)
                if not isinstance(e, int):
                    sp.wait_ge(S("lo_split"), 6 * e - 8)
                sp.dma_start(w[:, 0:4096], a["w_gu"][rows, :]).then_inc(S(f"w_in{i}"), 16)
                if not isinstance(e, int):
                    sp.wait_ge(S("lo_split"), 6 * e - 6)
                sp.dma_start(w[:, 4096:WE], a["w_dn"][rows, :]).then_inc(S(f"w_in{i}"), 16)

            sp.wait_ge(S("proj_done"), NTX)
            load_expert(0, 0)
            sp.wait_ge(S("wt_ready"), 1)
            sp.dma_start(t_dram[0:SEQ, D:XW].rearrange("(t p) n -> p t n", p=P), wt.rearrange("p (t n) -> p t n", t=8)).then_inc(S("pad_out"), 16)
            sp.wait_ge(S("zpad_ready"), 1)
            sp.dma_start(t_dram[SEQ:ROWS_OUT, :], zpad).then_inc(S("pad_out"), 16)
            for j in range(NTX):
                if j == 3:
                    sp.wait_ge(S("w_in0"), 32)
                    sp.sem_inc(S("weights_ready"), 1)
                if j == 6:
                    sp.wait_ge(S("sgu_done"), NTX)
                    sp.wait_ge(S("table_ready"), 1)
                    load_expert(1, 1)
                sp.wait_ge(S("sy_act"), j + 1)
                sp.dma_start(acc[P * j:P * j + P, :], yB[:, j % 2, :]).then_inc(S(f"acc_out{j % 2}"), 16)
            for i in range(2):
                sp.wait_ge(S(f"acc_out{i}"), 16 * 4)
                sp.wait_ge(S(f"x1_out{i}"), 16 * 4)
            sp.wait_ge(S("pad_out"), 32)
            sp.wait_ge(S("scattered"), 16)
            with sp.Fori(1, NE // NBUF) as g:
                for i in range(NBUF):
                    load_expert(g * NBUF + i, i)
                    sp.wait_ge(S(f"w_in{1 - i}"), 32 * (g + i))
                    sp.sem_inc(S("weights_ready"), 1)
            sp.wait_ge(S("w_in1"), 32 * (NE // NBUF))
            sp.sem_inc(S("weights_ready"), 1)
            sp.wait_ge(S("lo_split"), 6 * NE)
            sp.dma_start(g2B, grow[3:4, :].to_broadcast([P, D])).then_inc(S("rows2_in"), 16)
            sp.dma_start(lg2, a["ln2_g"].to_broadcast([P, D])).then_inc(S("rows2_in"), 16)
            sp.dma_start(lb2, a["ln2_b"].to_broadcast([P, D])).then_inc(S("rows2_in"), 16)
            for j in range(NTX):
                sp.dma_start(x1_in[j], x1_dram[P * j:P * j + P, :]).then_inc(S("rows2_in"), 16)
            sp.wait_ge(S("experts_done"), 1)
            for j in range(NTX):
                sp.dma_start(acc_in[j], acc[P * j:P * j + P, :]).then_inc(S(f"accin{j // 4}"), 16)
            for j in range(NTX):
                sp.wait_ge(S("out_ready"), j + 1)
                sp.dma_start(out[P * j:P * j + P, :], acc_in[j]).then_inc(S("out_done"), 16)
            sp.wait_ge(S("out_done"), 16 * NTX)

        @block.gpsimd
        def _(pool):
            def rstd_of(var_ready, v, col, done):
                pool.wait_ge(*var_ready)
                pool.tensor_scalar(veps[:, col:col + 1], v, EPS, None, ALU.add).then_inc(S("pool_step"), 1)
                n["p"] += 1
                pool.wait_ge(S("pool_step"), n["p"])
                pool.tensor_tensor(rstd[:, col:col + 1], veps[:, col:col + 1], cst[:, C_HALF:C_HALF + 1], ALU.pow).then_inc(S(done), 1)

            n = {"p": 0}
            pool.wait_ge(S("const_in"), 16)
            for t in range(NT):
                rstd_of((S("mv_ready"), t + 1), mv[:, 2 * t + 1:2 * t + 2], t, "rstd_ready")
            pool.wait_ge(S("piece_used"), 8)
            pool.memset(at(D0, 2376), 0.0).then_inc(S("cbuf_zero"), 1)
            pool.memset(cbufc, 0.0).then_inc(S("cbuf_zero"), 1)
            pool.wait_ge(S("qk_done"), 20)
            pool.memset(V[:, :, :, DH:VW], 1.0).then_inc(S("v_ones"), 1)
            pool.wait_ge(S("v_evac"), NT)
            pool.wait_ge(S("v_ones"), 1)
            pool.wait_ge(S("cols_ready"), 1)
            def head_rstd(n_):
                b = n_ % 2
                pool.wait_ge(S("hmv_ready"), n_ + 1)
                if n_ >= 2:
                    pool.wait_ge(S("h_normed"), n_ - 1)
                for op in (lambda: pool.tensor_scalar(hveps[:, b], hmv[:, b, :, 1], EPS, None, ALU.add),
                           lambda: pool.tensor_tensor(hrstd[:, b], hveps[:, b], cst[:, C_HALF:C_HALF + 4], ALU.pow),
                           lambda: pool.tensor_tensor(hbias[:, b], hmv[:, b, :, 0], hrstd[:, b], ALU.mult)):
                    op().then_inc(S("pool_step"), 1)
                    n["p"] += 1
                    pool.wait_ge(S("pool_step"), n["p"])
                pool.tensor_scalar(hbias[:, b], hbias[:, b], -1.0, None, ALU.mult).then_inc(S("hrstd_ready"), 1)

            for q, (s, d, t) in enumerate(JOBS):
                if q >= 2:
                    pool.wait_ge(S("U_half"), 2 * (q - 1))
                c0 = s * 48 + 16 + 12 * d
                pool.tensor_tensor(vw[:, q % 2], V[:, t], COL[:, c0:c0 + 4].unsqueeze(2).to_broadcast([P, 4, VW]), ALU.mult).then_inc(S("vw_ready"), 1)
                if 4 <= q < 4 + NTX:
                    o = O[:, q - 4]
                    pool.wait_ge(S("o_evac"), NTX)
                    pool.wait_ge(S("hg_in"), 16)
                    pool.tensor_scalar(o, o, 1.0, 0.5, ALU.add, ALU.mult).then_inc(S("pool_step"), 1)
                    n["p"] += 1
                    pool.wait_ge(S("pool_step"), n["p"])
                    pool.tensor_tensor(o, o, hgB, ALU.mult).then_inc(S("og_ready"), 1)
                if q >= FIRSTX + NTX + 2:
                    head_rstd(q - (FIRSTX + NTX + 2))
            for n_ in range(NJ - (FIRSTX + NTX + 2), NTX):
                head_rstd(n_)
            for j in range(NTX + 1):
                if j < NTX:
                    rstd_of((S("y_mv"), j + 1), mvj[:, j % 2, 1:2], j % 2, "y_rstd")
                    pool.wait_ge(S("y_norm"), j + 1)
                    pool.wait_ge(S("rows1_in"), 80)
                    pool.tensor_tensor(ytmp[:, j % 2], ytmp[:, j % 2], lg1, ALU.mult).then_inc(S("y_gain"), 1)
                if j >= 1:
                    rstd_of((S("x1_mv"), j), mvk[:, (j - 1) % 2, 1:2], 2 + (j - 1) % 2, "x1_rstd")
            pool.wait_ge(S("ln_ready"), NTX)
            pool.memset(zpad, 0.0).then_inc(S("zpad_ready"), 1)
            pool.wait_ge(S("zpad_ready"), 1)
            pool.dma_start(acc[SEQ:ROWS_OUT, :], zpad[:, 0:D]).then_inc(S("scattered"), 16)
            pool.wait_ge(S("slots_ready"), 1)
            for q in range(64):
                if q >= NOH:
                    pool.wait_ge(S("onehot_used"), q - NOH + 1)
                pool.tensor_scalar(oneP[:, q % NOH], iota, p8[:, q:q + 1], None, ALU.is_equal).then_inc(S("onehotp_ready"), 1)
            pool.wait_ge(S("idx_ready"), 1)
            pool.wait_ge(S("table_ready"), 1)
            for i in range(2):
                pool.wait_ge(S(f"t_out{i}"), 64)
            pool.wait_ge(S("pad_out"), 32)
            pool.sem_inc(S("y_free"), 1)

            def gather(col, p, nth):
                pool.tensor_copy(idxg[:, p:p + 1], idxT[:, col]).then_inc(S("idx_copied"), 1)
                pool.wait_ge(S("idx_copied"), nth)
                pool.sem_inc(S("pool_pass"), 1)
                pool.indirect_dma_start(out=xg[:, p], out_offset=None, in_=t_dram[:, :],
                                        in_offset=bass.IndirectOffsetOnAxis(ap=idxg[:, p:p + 1], axis=0)).then_inc(S(f"gathered{p}"), 16)

            def scatter(b, p, nth):
                pool.wait_ge(S("scattered"), 16 * b + 16)
                pool.sem_inc(S("y_free"), 1)
                pool.tensor_copy(idxs[:, p:p + 1], idxT[:, b:b + 1] if isinstance(b, int) else idxT[:, bass.ds(b, 1)]).then_inc(S("idx_copied"), 1)
                pool.wait_ge(S("idx_copied"), nth)
                pool.wait_ge(S("m_y"), b + 2)
                pool.sem_inc(S("pool_pass"), 1)
                pool.indirect_dma_start(out=acc[:, :], out_offset=bass.IndirectOffsetOnAxis(ap=idxs[:, p:p + 1], axis=0),
                                        in_=yB[:, p], in_offset=None, compute_op=ALU.add).then_inc(S("scattered"), 16)

            gather(slice(0, 1), 0, 1)
            gather(slice(1, 2), 1, 2)
            for i in range(2):
                pool.wait_ge(S(f"acc_out{i}"), 64)
            pool.wait_ge(S("m_xb"), 1)
            gather(slice(2, 3), 0, 3)
            pool.wait_ge(S("m_xb"), 2)
            gather(slice(3, 4), 1, 4)
            rest = pool.value_load(pairs_rest[0:1, 0:1], min_val=NE // 2 - 1, max_val=MAXB // 2 - 1)
            with pool.Fori(0, rest) as i:
                for p in range(2):
                    pool.wait_ge(S("m_xb"), 2 * i + (p + 3))
                    gather(bass.ds(2 * i + (p + 4), 1), p, 4 * i + (2 * p + 5))
                    scatter(2 * i + p, p, 4 * i + (2 * p + 6))
            scatter(2 * rest, 0, 4 * rest + 5)
            scatter(2 * rest + 1, 1, 4 * rest + 6)
            pool.wait_ge(S("scattered"), 32 * rest + 48)
            for p in range(2):
                pool.wait_ge(S(f"gathered{p}"), 16 * rest + 32)
            pool.sem_inc(S("experts_done"), 1)
            def final_rstd(j):
                rstd_of((S("y_mv"), NTX + j + 1), mv[:, 2 * j + 1:2 * j + 2], j, "y_rstd")
                pool.wait_ge(S("y_rstd"), NTX + j + 1)
                pool.tensor_scalar(hst[:, j:j + 1], mv[:, 2 * j:2 * j + 1], rstd[:, j:j + 1], -1.0, ALU.mult, ALU.mult).then_inc(S("hrstd_ready"), 1)

            def final_gate(j):
                pool.wait_ge(S(f"accin{j // 4}"), 64)
                pool.tensor_tensor(acc_in[j], acc_in[j], g2B, ALU.mult).then_inc(S("og_ready"), 1)

            pool.wait_ge(S("rows2_in"), 48 + 16 * NTX)
            final_gate(POOL_GAINS[0])
            final_rstd(0)
            for j in range(NTX):
                if j in (1, 3):
                    final_gate(j + 4)
                if j + 1 < NTX:
                    final_rstd(j + 1)
                pool.wait_ge(S("y_norm"), NTX + j + 1)
                pool.tensor_tensor(acc_in[j], acc_in[j], lg2, ALU.mult).then_inc(S("y_gain"), 1)

        @block.scalar
        def _(act):
            def copy(o, i):
                return act.activation(o, i, ACT.Copy)

            act.wait_ge(S("c_in"), 16)
            act.activation(silc[:, :], ccol[:, :], ACT.Silu).then_inc(S("sil_ready"), 1)
            act.wait_ge(S("mod_ready"), 1)
            for g, (t0, nt) in enumerate(GROUPS):
                for k in range(0, 8, 2):
                    q = 8 * g + k
                    w = 0 if g else 1
                    act.wait_ge(S("tr_done"), q + 1)
                    act.activation(uT[:, k, P * t0:P * (t0 + nt)], bank(q % 4)[:, 0:P * nt], ACT.Identity,
                                   scale=modc[:, 16 + 2 * k + w:17 + 2 * k + w], bias=modc[:, 2 * k + w:2 * k + w + 1]).then_inc(S("uT_act"), 1)
            act.wait_ge(S("tr_done"), 24)
            act.dma_start(mrow, a["b_ada"][0:1, 2 * D:3 * D]).then_inc(S("b_in"), 16)
            for i in range(8):
                act.wait_ge(S("f_done"), i + 1)
                c, h = i // 2, i % 2
                copy(fT[:, c, 512 * h:512 * h + 512], bank(4 + i % 2)).then_inc(S("f_evac"), 1)
                if h == 1:
                    act.wait_ge(S("mrow_ready"), c + 1)
                    act.dma_start(grow[c:c + 1, :], mrow).then_inc(S("mrow_out"), 16)
                    if c < 3:
                        act.wait_ge(S("mrow_out"), 16 * (c + 1))
                        act.dma_start(mrow, a["b_ada"][0:1, (c + 3) * D:(c + 4) * D]).then_inc(S("b_in"), 16)
            for q, (idx, j, cp) in enumerate(ABJOBS):
                if idx % 2 == 0:
                    act.wait_ge(S("ab_done"), q + 1)
                    copy(EO[:, j, 2 * cp:2 * cp + 2, :], bank(1 + q % 3).rearrange("p (c n) -> p c n", c=2)).then_inc(S("ab_act"), 1)
            for c in range(4):
                for g, w in ((0, NEV), (1, NOD)):
                    act.wait_ge(S("fourier_mm"), 4 * c + 2 * g + 2)
                    if c:
                        act.wait_ge(S("qtmp_used"), 2 * (c - 1) + g + 1)
                    copy(qtmp[:, g, 0:w], bank((0 if c % 2 else 4) + 2 * g + 1)[:, 0:w]).then_inc(S("qtmp_ready"), 1)
            act.wait_ge(S("cbuf_zero"), 2)
            act.wait_ge(S("small_in"), 48)
            for c in range(9):
                if c < 8:
                    for q, (cc, part) in enumerate(QKJOBS):
                        if cc != c:
                            continue
                        act.wait_ge(S("qk_done"), q + 1)
                        if part == 0 and c >= 2:
                            act.wait_ge(S("conv_done"), c - 1)
                        if part == 2 and c >= 5:
                            act.wait_ge(S("conv_done"), c)
                        if part < 2:
                            copy(cbuf[c % 2][:, 1 + 8 * part:9 + 8 * part, 1:65], bank(q % 4).rearrange("p (r c) -> p r c", r=8)).then_inc(S("cv_evac"), 1)
                        else:
                            copy(cbufc[:, 1:257], bank(q % 4)[:, 0:256]).then_inc(S("cv_evac"), 1)
                if c >= 1:
                    act.wait_ge(S("conv_done"), c)
                    x = c - 1
                    act.activation(qkT[:, x, :], cacc.rearrange("p r c -> p (r c)"), ACT.Silu, bias=convb[:, x:x + 1]).then_inc(S("silu_done"), 1)
                    if x >= 4:
                        act.activation(kTc[:, x - 4, :], caccc, ACT.Silu, bias=convb[:, x:x + 1]).then_inc(S("siluc_done"), 1)
            def values(t):
                act.wait_ge(S("v_done"), t + 1)
                copy(V[:, t, :, 0:DH], bank(4 + t % 2).rearrange("p (h n) -> p h n", h=4)).then_inc(S("v_evac"), 1)

            act.wait_ge(S("mrow_out"), 64)
            for t in range(NTC):
                values(t)
            act.wait_ge(S("rows_evac"), 6)
            act.activation(Rl, Rf, ACT.Abs).then_inc(S("rl_step"), 1)
            act.wait_ge(S("rl_step"), 1)
            act.activation(Rl, Rl, ACT.Exp, scale=-1.0).then_inc(S("rl_step"), 1)
            act.wait_ge(S("rl_step"), 2)
            act.activation(Rl, Rl, ACT.Ln, bias=1.0).then_inc(S("rl_step"), 1)
            for t in range(NTC, NT):
                values(t)
                if t >= NTC:
                    act.wait_ge(S("o_done"), t - NTC + 1)
                    act.activation(O[:, t - NTC], bank(6), ACT.Tanh, scale=0.5).then_inc(S("o_evac"), 1)
            for t in range(NT):
                act.wait_ge(S("kM_done"), t + 1)
                act.mul(kM[:, t], bank(t % 2), KSCALE).then_inc(S("kM_evac"), 1)
                if t in (4, 6):
                    r, v = (Rw, 1) if t == 4 else (Re, 2)
                    act.wait_ge(S("wargs_ready"), v + 1)
                    for d in range(2):
                        src = r.rearrange("p (s n) -> p s n", s=NT)
                        act.activation(stack[32 * v:32 * v + 8, d].rearrange("p (s n) -> p s n", s=NT), src[:, :, ::-1] if d else src,
                                       ACT.Exp).then_inc(S("rows_exp"), 1)
                if t == 8:
                    act.wait_ge(S("wargs_ready"), 4)
                    act.activation(Ri, Ri, ACT.Exp).then_inc(S("rows_exp"), 1)
            act.wait_ge(S("cols_ready"), 1)
            def head_norm(n_):
                j, b = HTILES[n_], n_ % 2
                act.wait_ge(S("hrstd_ready"), n_ + 1)
                for h in range(4):
                    hh = H[:, j, P * h:P * h + P]
                    ins = act.activation(hh, hh, ACT.Identity, scale=hrstd[:, b, h:h + 1], bias=hbias[:, b, h:h + 1])
                ins.then_inc(S("h_normed"), 1)

            for x in range(16):
                s, d, t = JOBS[x + FIRSTX]
                act.wait_ge(S("SD_done"), x + 1)
                if x >= 2:
                    act.wait_ge(S("N_done"), x - 1)
                for h in range(4):
                    c0 = s * 48 + 12 * d + h
                    ins = act.activation(Dt[:, x % 2, P * h:P * h + P], bank(2 if x % 2 == 0 else 5)[:, P * h:P * h + P], ACT.Exp, bias=COL[:, c0:c0 + 1])
                ins.then_inc(S("D_ready"), 1)
                if x >= NTX + 2:
                    head_norm(x - NTX - 2)
            for n_ in range(16 - NTX - 2, NTX):
                head_norm(n_)
            for n_, j in enumerate(HTILES):
                act.wait_ge(S("mixt_done"), n_ + 1)
                copy(mixT[:, 0:4, P * j:P * j + P], bank(n_ % 2).rearrange("p (h n) -> p h n", h=4)).then_inc(S("mixt_evac"), 1)
            def t_evac(j):
                act.wait_ge(S("tt_done"), j + 1)
                for h in range(2):
                    ins = copy(tT[:, 4 * h:4 * h + 4, P * j:P * j + P], bank(h).rearrange("p (k n) -> p k n", k=4))
                ins.then_inc(S("tT_evac"), 1)

            def shared_silu(j):
                act.wait_ge(S("sgu_done"), j + 1)
                act.activation(sgL[:, j % 2], bank(3 + j % 2)[:, 0:DE], ACT.Silu).then_inc(S("s_sg"), 1)

            def shared_hT(j):
                act.wait_ge(S("sht_done"), j + 1)
                copy(hTL[:, j % 2], bank(7)[:, 0:2 * P].rearrange("p (k n) -> p k n", k=2)).then_inc(S("s_hT"), 1)

            def shared_y(j):
                act.wait_ge(S("sdown_done"), j + 1)
                if j >= 2:
                    act.wait_ge(S(f"acc_out{j % 2}"), 16 * (j // 2))
                copy(yB[:, j % 2], psY).then_inc(S("sy_act"), 1)

            def shared_out(j):
                shared_hT(j)
                shared_y(j)

            def w_high(par, chunks):
                for c in chunks:
                    copy(cols(wsplit, (1 - par) * (2 * WE) + 1024 * c, 1024), cols(raw, (1 - par) * WE + 1024 * c, 1024)).then_inc(S("hi_split"), 1)

            for j in range(NTX - 2):
                t_evac(j)
            shared_silu(0)
            shared_silu(1)
            t_evac(NTX - 2)
            t_evac(NTX - 1)
            act.wait_ge(S("router_done"), 1)
            act.activation(sc, bank(2), ACT.Sigmoid).then_inc(S("sc_ready"), 1)
            shared_out(0)
            for j in range(2, NTX):
                shared_silu(j)
                shared_out(j - 1)
            shared_hT(NTX - 1)
            act.wait_ge(S("table_ready"), 1)
            act.wait_ge(S("pad_out"), 32)
            act.wait_ge(S("scattered"), 16)
            act.wait_ge(S("weights_ready"), 1)
            w_high(0, range(4))
            shared_y(NTX - 1)
            w_high(0, range(4, 6))
            def x_high(b, p):
                act.wait_ge(S("m_xt"), b + 1)
                copy(xTh[p], psum[:, 0:1024]).then_inc(S("m_xh"), 1)

            def h_high(b):
                act.wait_ge(S("m_ht"), b + 1)
                copy(hTh, bank(7)[:, 0:2 * P]).then_inc(S("m_hh"), 1)

            def y_evac(b, p):
                act.wait_ge(S("block_done"), b + 2)
                act.wait_ge(S("y_free"), b + 1)
                copy(yB[:, p], psY).then_inc(S("m_y"), 1)

            def silu(b, p):
                act.wait_ge(S("m_gu"), b + 1)
                act.activation(sg[:, p], bank(3 + p)[:, 0:DE], ACT.Silu).then_inc(S("m_sg"), 1)

            act.sem_inc(S("m_y"), 1)
            x_high(0, 0)
            x_high(1, 1)
            act.wait_ge(S("weights_ready"), 2)
            w_high(1, range(4))
            silu(0, 0)

            def step(b, p, w0, w1):
                h_high(b - 1)
                if w0 is not None:
                    y_evac(b - 2, p)
                x_high(b + 1, 1 - p)
                if w0 is None:
                    w_high(1, range(4, 6))
                else:
                    with act.If_ne(act.to_reg((w0 >> 6) & 1), 0):
                        w_high(1 - (w0 & 1), range(4, 6))
                first, par1 = (w1 >> 6) & 1, 1 - (w1 & 1)
                with act.If_ne(act.to_reg(first), 0):
                    act.wait_ge(S("weights_ready"), (w1 & 63) + 2)
                    act.sem_inc(S("act_pass"), 1)
                    w_high(par1, range(2))
                silu(b, p)
                with act.If_ne(act.to_reg(first), 0):
                    w_high(par1, range(2, 4))

            def word(b):
                return word_of(act, b)

            step(1, 1, None, word(1))
            rest = act.value_load(pairs_rest[0:1, 0:1], min_val=NE // 2 - 1, max_val=MAXB // 2 - 1)
            with act.Fori(0, rest) as i:
                w0, w1 = word(2 * i + 1), word(2 * i + 2)
                step(2 * i + 2, 0, w0, w1)
                w2 = word(2 * i + 3)
                step(2 * i + 3, 1, w1, w2)
            h_high(2 * rest + 1)
            y_evac(2 * rest, 0)
            y_evac(2 * rest + 1, 1)
            for j in range(NTX):
                act.wait_ge(S("hrstd_ready"), NTX + j + 1)
                act.activation(acc_in[j], acc_in[j], ACT.Identity, scale=rstd[:, j:j + 1], bias=hst[:, j:j + 1]).then_inc(S("y_norm"), 1)

        @block.tensor
        def _(pe):
            mm = pe.matmul

            pe.wait_ge(S("sil_ready"), 1)
            for m in range(2):
                for kc in range(8):
                    if kc % 4 == 0:
                        pe.wait_ge(S(f"ada_in{2 * m + kc // 4}"), 16)
                    for h in range(2):
                        ins = mm(bank(4 + 2 * m + h)[0:2, :], silc[:, 2 * kc:2 * kc + 2], ada[m][:, kc, 512 * h:512 * h + 512], start=(kc == 0), stop=(kc == 7))
                ins.then_inc(S("ada_done"), 1)

            def modulation_columns():
                pe.wait_ge(S("rows01_ready"), 2)
                for v in range(2):
                    for k in range(8):
                        o = 16 * v + 2 * k
                        ins = mm(bank(4)[:, o:o + 2], rows01[v][:, k::8], cst[0:2, C_ID:C_ID + 2], start=True, stop=True)
                ins.then_inc(S("modc_mm"), 1)

            pe.wait_ge(S("const_in"), 16)
            for g, (t0, nt) in enumerate(GROUPS):
                pe.wait_ge(S("xn_ready"), t0 + nt)
                for k in range(8):
                    q = 8 * g + k
                    if q == 4:
                        modulation_columns()
                    if q >= 4:
                        pe.wait_ge(S("uT_act") if q % 2 == 0 else S("uT_dve"), (q - 4) // 2 + 1)
                    for i in range(nt):
                        ins = pe.transpose(bank(q % 4)[:, P * i:P * i + P], xin[t0 + i][:, k::8], ident)
                    ins.then_inc(S("tr_done"), 1)
            pe.wait_ge(S("uT_act"), 12)
            pe.wait_ge(S("uT_dve"), 12)
            pe.wait_ge(S("wf_in"), 16)
            pe.wait_ge(S("mod_ready"), 1)
            for i in range(8):
                c, h = i // 2, i % 2
                if i >= 2:
                    pe.wait_ge(S("f_evac"), i - 1)
                for k in range(8):
                    ins = mm(bank(4 + i % 2), wf[:, k, P * c:P * c + P], uT[:, k, CTX + 512 * h:CTX + 512 * h + 512], start=(k == 0), stop=(k == 7))
                ins.then_inc(S("f_done"), 1)
                m, ph = PIECES[i]
                pe.wait_ge(S(f"piece_in{i % 2}"), 16 * (i // 2 + 1))
                if i == 4:
                    pe.wait_ge(S("mrow_ready"), 1)
                if i == 6:
                    pe.wait_ge(S("mrow_ready"), 2)
                for kc in range(4 * ph, 4 * ph + 4):
                    for h2 in range(2):
                        ins = mm(bank(ROWBANKS[m][h2])[0:1, :], silc[:, 2 * kc:2 * kc + 1], piece[i % 2][:, kc % 4, 512 * h2:512 * h2 + 512],
                                 start=(kc == 0), stop=(kc == 7))
                ins.then_inc(S("piece_used"), 1)
            pe.wait_ge(S("f_evac"), 8)
            pe.wait_ge(S("mrow_ready"), 4)
            for q, (idx, j, cp) in enumerate(ABJOBS):
                if q >= 3:
                    i3, _, c3 = ABJOBS[q - 3]
                    pe.wait_ge(S("ab_act") if i3 % 2 == 0 else S("ab_dve"), 2 * (i3 // 2) + c3 + 1)
                for c in range(2):
                    ins = mm(bank(1 + q % 3)[:, 256 * c:256 * c + 256], fT[:, 2 * cp + c, P * j:P * j + P], cst[:, C_CD:C_CD + 256], start=True, stop=True)
                ins.then_inc(S("ab_done"), 1)
            pe.wait_ge(S("ab_act"), 8)
            pe.wait_ge(S("ab_dve"), 8)
            pe.wait_ge(S("cs_in"), 16)
            for c in range(4):
                if c >= 2:
                    pe.wait_ge(S("qtmp_used"), 2 * (c - 1))
                for g in range(4):
                    odd, sin = g // 2, g % 2
                    w = NOD if odd else NEV
                    o = (2 * NEV if odd else 0) + sin * w
                    for j in range(4):
                        ins = mm(bank((0 if c % 2 else 4) + g)[:, 0:w], EO[:, j if odd else 4 + j, c, P * sin:P * sin + P], CS[:, j, o:o + w], start=(j == 0), stop=(j == 3))
                    ins.then_inc(S("fourier_mm"), 1)
            pe.wait_ge(S("qtmp_used"), 8)
            pe.wait_ge(S("wqk_in"), 16)
            for q, (c, part) in enumerate(QKJOBS):
                if q >= 4:
                    pe.wait_ge(S("cv_evac"), q - 3)
                n, o = (512, CTX + 512 * part) if part < 2 else (CTX, 0)
                for k in range(8):
                    ins = mm(bank(q % 4)[:, 0:n], wqk[:, k, P * c:P * c + P], uT[:, k, o:o + n], start=(k == 0), stop=(k == 7))
                ins.then_inc(S("qk_done"), 1)
            pe.wait_ge(S("wvog_in"), 16)

            def values(t):
                if t >= 2:
                    pe.wait_ge(S("v_evac"), t - 1)
                for k in range(8):
                    ins = mm(bank(4 + t % 2), uT[:, k, P * t:P * t + P], wvog[:, k, 0:512], start=(k == 0), stop=(k == 7))
                ins.then_inc(S("v_done"), 1)

            values(0)
            values(1)
            for t in range(NT):
                if t >= 2:
                    pe.wait_ge(S("g_evac"), t - 1)
                for k in range(8):
                    ins = mm(bank(6 + t % 2)[:, 0:16], uT[:, k, P * t:P * t + P], wvog[:, k, 1024:1040], start=(k == 0), stop=(k == 7))
                ins.then_inc(S("g_done"), 1)
            pe.wait_ge(S("g_evac"), NT)
            pe.wait_ge(S("cv_evac"), 20)
            for r, (s0, ns) in enumerate(((0, 4), (4, 4), (8, 2))):
                for gate in range(2):
                    q = 2 * r + gate
                    if q >= 4:
                        pe.wait_ge(S("rows_evac"), q - 3)
                    for i in range(ns):
                        tf, tb = tiles_of(s0 + i)
                        o = bank(q % 4)[0:8, P * i:P * i + P]
                        mm(o, G[:, 32 * tf + 8 * gate:32 * tf + 8 * gate + 8], ident, start=True, stop=False)
                        ins = mm(o, G[:, 32 * tb + 16 + 8 * gate:32 * tb + 24 + 8 * gate], rev, start=False, stop=True)
                    ins.then_inc(S("rows_mm"), 1)
            for t in range(NTC, NT):
                values(t)
                if t >= NTC:
                    if t > NTC:
                        pe.wait_ge(S("o_evac"), t - NTC)
                    for k in range(8):
                        ins = mm(bank(6), uT[:, k, P * t:P * t + P], wvog[:, k, 512:1024], start=(k == 0), stop=(k == 7))
                    ins.then_inc(S("o_done"), 1)
            pe.wait_ge(S("silu_done"), 8)
            pe.wait_ge(S("siluc_done"), 4)
            pe.wait_ge(S("rows_evac"), 6)
            for t in range(NT):
                if t >= 2:
                    pe.wait_ge(S("kM_evac"), t - 1)
                for h in range(4):
                    src = kTc[:, h, P * t:P * t + P] if t < NTC else qkT[:, 4 + h, P * (t - NTC):P * (t - NTC) + P]
                    ins = pe.transpose(bank(t % 2)[:, P * h:P * h + P], src, ident)
                ins.then_inc(S("kM_done"), 1)
            pe.wait_ge(S("rows_exp"), 4)
            pe.wait_ge(S("rows_rev"), 2)
            first = True
            for s in range(NT):
                for d in range(2):
                    o = bank(2)[:, 48 * s:48 * s + 48].rearrange("p (v d r) -> p v d r", v=3, d=2)[:, :, d]
                    mm(o, stack[0:72, d, P * s:P * s + P], cst[0:72, C_ID:C_ID + 96].rearrange("p (v r) -> p v r", v=3)[:, :, 0:8],
                       start=first, stop=False, skip_group_check=True)
                    first = False
            pe.wait_ge(S("rows_rev"), 3)
            mm(bank(3)[:, 0:NT * 8], cst[0:8, C_ONE:C_ONE + P], dgl[0:8, :], start=True, stop=True).then_inc(S("cols_mm"), 1)
            pe.wait_ge(S("cols_ready"), 1)
            pe.wait_ge(S("kM_evac"), NT)
            pe.wait_ge(S("v_evac"), NT)
            pe.wait_ge(S("v_ones"), 1)

            def rows_of(r, s, d, n=P):
                src = r[:, P * s:P * s + P]
                return src[:, ::-1] if d else src

            def scores(x):
                s, d, t = JOBS[x + FIRSTX]
                c = t - NTC
                if x >= 2:
                    pe.wait_ge(S("P_ready"), x - 1)
                for h in range(4):
                    mm(bank(x % 2)[:, P * h:P * h + P], qkT[:, 4 + h, P * c:P * c + P], qkT[:, h, P * c:P * c + P], start=True, stop=True)

            def masks(x):
                s, d, t = JOBS[x + FIRSTX]
                db = bank(2 if x % 2 == 0 else 5)
                mm(db.rearrange("p (h n) -> p h n", h=4), maskr[:, 0:P], maskr[:, P * (1 + d):P * (2 + d)].unsqueeze(1).to_broadcast([P, 4, P]), start=True, stop=False, skip_group_check=True)
                for h in range(4):
                    r = 4 * d + h
                    ins = mm(db[:, P * h:P * h + P], cst[0:8, C_SEL + P * r:C_SEL + P * r + P], rows_of(Rm, s, d), start=False, stop=(h == 3), skip_group_check=True)
                ins.then_inc(S("SD_done"), 1)

            def update(q, half, b):
                s, d, t = JOBS[q]
                for i in range(2):
                    h = 2 * half + i
                    ins = mm(bank(b)[:, 256 * i:256 * i + VW], kM[:, t, P * h:P * h + P], vw[:, q % 2, h], start=True, stop=True)
                ins.then_inc(S("U_half"), 1)
                return ins

            for q, (s, d, t) in enumerate(JOBS):
                x = q - FIRSTX
                if 0 <= x + 1 < 16:
                    scores(x + 1)
                if x >= 0:
                    pe.wait_ge(S("C_half"), 2 * q - 1)
                    for h in range(4):
                        r = 4 * d + h
                        ins = mm(bank(6)[:, P * h:P * h + P], cst[0:8, C_SEL + P * r:C_SEL + P * r + P], rows_of(Ri, s, d), start=True, stop=True)
                    ins.then_inc(S("I_done"), 1)
                if 0 <= x + 1 < 16:
                    masks(x + 1)
                pe.wait_ge(S("vw_ready"), q + 1)
                if q >= 1:
                    pe.wait_ge(S("C_half"), 2 * q)
                update(q, 0, 7)
                if x >= 0:
                    pe.wait_ge(S("qI_ready"), x + 1)
                update(q, 1, 6)
                if x >= 0:
                    pe.wait_ge(S("P_ready"), x + 1)
                    if x >= 1:
                        pe.wait_ge(S("h_read"), x)
                    for h in range(4):
                        o = psN[:, 512 * (h // 2) + 256 * (h % 2):512 * (h // 2) + 256 * (h % 2) + VW]
                        mm(o, Dt[:, x % 2, P * h:P * h + P], V[:, t, h], start=True, stop=False)
                        ins = mm(o, qI[:, x % 2, P * h:P * h + P], Cst[:, d, h], start=False, stop=True)
                    ins.then_inc(S("N_done"), 1)
            def project(j, ks):
                for h in range(2):
                    o = (psN if j % 2 == 0 else psY)[:, 512 * h:512 * h + 512]
                    for k in ks:
                        ins = mm(o, mixT[:, k, P * j:P * j + P], wout[:, k, 512 * h:512 * h + 512], start=(k == 4), stop=(k == 3))
                return ins

            pe.wait_ge(S("woutf_in"), 16)
            pe.wait_ge(S("C_half"), 2 * len(JOBS))
            project(1, range(4, 8))
            pe.wait_ge(S("h_read"), 16)
            project(0, range(4, 8))
            for n_, j in enumerate(HTILES):
                pe.wait_ge(S("mix_ready"), n_ + 1)
                if n_ >= 2:
                    pe.wait_ge(S("mixt_evac"), n_ - 1)
                for h in range(4):
                    ins = pe.transpose(bank(n_ % 2)[:, P * h:P * h + P], H[:, j, P * h:P * h + P], ident)
                ins.then_inc(S("mixt_done"), 1)
            pe.wait_ge(S("mixt_evac"), NTX)
            pe.wait_ge(S("wout_in"), 16)
            def t_transposes(i):
                pe.wait_ge(S("ln_ready"), i + 1)
                if i >= 1:
                    pe.wait_ge(S("tT_evac"), i)
                for k in range(8):
                    ins = pe.transpose(bank(k // 4)[:, P * (k % 4):P * (k % 4) + P], lnt[:, i % 2, k::8], ident)
                ins.then_inc(S("tt_done"), 1)

            for j in range(NTX):
                if j >= 2:
                    pe.wait_ge(S("y_read"), j - 1)
                    project(j, range(4, 8))
                project(j, range(4)).then_inc(S("proj_done"), 1)
                if j >= 2:
                    t_transposes(j - 2)

            def shared_gu(j, slots=False):
                pe.wait_ge(S("tT_evac"), j + 1)
                if j < 2:
                    pe.wait_ge(S("y_read"), NTX - 1)
                for k in range(8):
                    ins = mm(bank(3 + j % 2), tT[:, k, P * j:P * j + P], wsgu[:, k, :], start=(k == 0), stop=(k == 7))
                    if k == 7:
                        ins.then_inc(S("sgu_done"), 1)
                    if slots:
                        onehots(2)

            def shared_down(j, slots=False):
                pe.wait_ge(S("s_hx"), j + 1)
                for k in range(2):
                    ins = pe.transpose(bank(7)[:, P * k:P * k + P], hxL[:, j % 2, k::2], ident)
                ins.then_inc(S("sht_done"), 1)
                pe.wait_ge(S("s_hT"), j + 1)
                if j >= 1:
                    pe.wait_ge(S("sy_act"), j)
                else:
                    pe.wait_ge(S("y_read"), NTX)
                for h in range(2):
                    for k in range(2):
                        ins = mm(bank(5 + h), hTL[:, j % 2, k], wsd[:, k, 512 * h:512 * h + 512], start=(k == 0), stop=(k == 1))
                        if h == 1 and k == 1:
                            ins.then_inc(S("sdown_done"), 1)
                        if slots:
                            onehots(2)

            made = [0]

            def onehots(count):
                for q in range(made[0], made[0] + count):
                    pe.wait_ge(S("onehot_ready"), q + 1)
                    pe.wait_ge(S("onehotp_ready"), q + 1)
                    mm(bank(2)[:, 0:P], oneP[:, q % NOH], oneB[:, q % NOH], start=(q == 0), stop=(q == 63), skip_group_check=True).then_inc(S("onehot_used"), 1)
                made[0] += count

            pe.wait_ge(S("ws_in"), 64)
            shared_gu(0)
            shared_gu(1)
            pe.wait_ge(S("ws_in"), 64)
            for j in range(NTX):
                if j == NTX - 2:
                    t_transposes(NTX - 2)
                    t_transposes(NTX - 1)
                pe.wait_ge(S("tT_evac"), j + 1)
                for k in range(8):
                    ins = mm(bank(2)[:, NE * j:NE * j + NE], tT[:, k, P * j:P * j + P], wr[:, k, :], start=(k == 0), stop=(k == 7))
            ins.then_inc(S("router_done"), 1)
            shared_down(0)
            shared_gu(2)
            shared_down(1)
            shared_gu(3)
            shared_down(2)
            pe.wait_ge(S("mask_ready"), 1)
            mkv = mask_r[:, :].rearrange("p (j e) -> p j e", j=8)
            for j in range(NTX):
                for i in range(j + 1):
                    mm(bank(0)[:, NE * j:NE * j + NE], lt_r if i == j else ones_r, mkv[:, i, :], start=(i == 0), stop=(i == j))
            for i in range(NTX):
                ins = mm(bank(1)[:, 0:NE], ones_r, mkv[:, i, :], start=(i == 0), stop=(i == NTX - 1))
            ins.then_inc(S("pos_done"), 1)
            shared_gu(4)
            shared_down(3)
            pe.wait_ge(S("eb_ready"), 1)
            mm(bank(1)[0:1, 0:P], ebc, ident, start=True, stop=True).then_inc(S("eb_mm"), 1)
            shared_gu(5, slots=True)
            shared_down(4, slots=True)
            shared_gu(6, slots=True)
            shared_down(5, slots=True)
            shared_gu(7, slots=True)
            shared_down(6)
            shared_down(7)
            def x_transposes(b, p, landed):
                pe.wait_ge(S(f"gathered{p}"), landed)
                if not isinstance(b, int) or b > 0:
                    pe.wait_ge(S("m_xb"), b)
                for k in range(8):
                    ins = pe.transpose(bank(k // 4)[:, P * (k % 4):P * (k % 4) + P], xg[:, p, 0:D][:, k::8], ident)
                ins.then_inc(S("m_xt"), 1)

            def part(par, low, o):
                return cols(wsplit, (1 - par) * (2 * WE) + (WE * low + o), 512)

            def gate_up(b, p, par, e):
                pe.wait_ge(S("m_xb"), b + 1)
                for k in range(8):
                    if k % 2 == 0:
                        pe.wait_ge(S("lo_split"), 6 * e + (k // 2 + 1))
                    xk, xl = (x[:, P * k:P * k + P] for x in (xTh[p], xTl[p]))
                    mm(bank(3 + p), xk, part(par, 0, 512 * k), start=(k == 0), stop=False)
                    mm(bank(3 + p), xk, part(par, 1, 512 * k), start=False, stop=False)
                    ins = mm(bank(3 + p), xl, part(par, 0, 512 * k), start=False, stop=(k == 7))
                ins.then_inc(S("m_gu"), 1)

            def h_transposes(b, p):
                pe.wait_ge(S("m_hx"), b + 1)
                for k in range(2):
                    ins = pe.transpose(bank(7)[:, P * k:P * k + P], hx[:, p, k::2], ident)
                ins.then_inc(S("m_ht"), 1)

            def down(b, par, e):
                pe.wait_ge(S("m_hT"), b + 1)
                pe.wait_ge(S("m_y"), b + 1)
                pe.wait_ge(S("lo_split"), 6 * e + 6)
                for h in range(2):
                    for k in range(2):
                        hk, hl = (x[:, P * k:P * k + P] for x in (hTh, hTl))
                        o = 4096 + 1024 * k + 512 * h
                        mm(bank(5 + h), hk, part(par, 0, o), start=(k == 0), stop=False)
                        mm(bank(5 + h), hk, part(par, 1, o), start=False, stop=False)
                        ins = mm(bank(5 + h), hl, part(par, 0, o), start=False, stop=(k == 1))
                ins.then_inc(S("block_done"), 1)

            def word(b):
                return word_of(pe, b)

            pe.wait_ge(S("table_ready"), 1)
            pe.sem_inc(S("block_done"), 1)
            x_transposes(0, 0, 16)
            x_transposes(1, 1, 16)
            gate_up(0, 0, 0, 0)
            pe.wait_ge(S("sy_act"), NTX)

            def step(b, p, landed, w0, w1):
                h_transposes(b - 1, 1 - p)
                x_transposes(b + 1, 1 - p, landed)
                gate_up(b, p, w1 & 1, w1 & 63)
                down(b - 1, w0 & 1, w0 & 63)

            step(1, 1, 32, word(0), word(1))
            rest = pe.value_load(pairs_rest[0:1, 0:1], min_val=NE // 2 - 1, max_val=MAXB // 2 - 1)
            with pe.Fori(0, rest) as i:
                w0, w1 = word(2 * i + 1), word(2 * i + 2)
                step(2 * i + 2, 0, 16 * i + 32, w0, w1)
                w2 = word(2 * i + 3)
                step(2 * i + 3, 1, 16 * i + 48, w1, w2)
            h_transposes(2 * rest + 1, 1)
            w0 = word(2 * rest + 1)
            down(2 * rest + 1, w0 & 1, w0 & 63)

        @block.vector
        def _(dve):
            n = {"c": 0}

            def link(ins):
                n["c"] += 1
                ins.then_inc(S("dve_step"), 1)
                dve.wait_ge(S("dve_step"), n["c"])

            tt, ts, stt = dve.tensor_tensor, dve.tensor_scalar, dve.scalar_tensor_tensor

            def moments(x, o, done, st=stats):
                dve.bn_stats(st[:, 0:6], x[:, 0:512])
                link(dve.bn_stats(st[:, 6:12], x[:, 512:1024]))
                dve.bn_aggr(o, st[:, 0:12]).then_inc(S(done), 1)

            def norm(t):
                dve.wait_ge(S("rstd_ready"), t + 1)
                ts(xin[t], xin[t], mv[:, 2 * t:2 * t + 1], rstd[:, t:t + 1], ALU.subtract, ALU.mult).then_inc(S("xn_ready"), 1)

            def u_evac(g):
                t0, nt = GROUPS[g]
                w = 0 if g else 1
                for k in range(1, 8, 2):
                    dve.wait_ge(S("tr_done"), 8 * g + k + 1)
                    ts(uT[:, k, P * t0:P * (t0 + nt)], bank((8 * g + k) % 4)[:, 0:P * nt], modc[:, 16 + 2 * k + w:17 + 2 * k + w],
                       modc[:, 2 * k + w:2 * k + w + 1], ALU.mult, ALU.add).then_inc(S("uT_dve"), 1)

            for t in range(NT):
                dve.wait_ge(S(f"x_in{XG[t]}"), 16 * XG.count(XG[t]))
                moments(xin[t], mv[:, 2 * t:2 * t + 2], "mv_ready", hst if t % 2 else stats)
                if t >= 1:
                    norm(t - 1)
            norm(NT - 1)
            dve.wait_ge(S("b_in"), 32)
            for v in range(2):
                dve.wait_ge(S("ada_done"), v + 1)
                for h in range(2):
                    r01 = rows01[v][:, 512 * h:512 * h + 512]
                    ins = stt(r01, r01, float(v), bank(4 + 2 * v + h)[0:2, :], ALU.add, ALU.add)
                ins.then_inc(S("rows01_ready"), 1)
            dve.wait_ge(S("modc_mm"), 1)
            dve.tensor_copy(modc[:, :], bank(4)[:, 0:32]).then_inc(S("mod_ready"), 1)
            dve.wait_ge(S("mod_ready"), 1)
            for g in range(3):
                u_evac(g)
            for g in range(4):
                dve.wait_ge(S("b_in"), 48 + 16 * g)
                dve.wait_ge(S("piece_used"), 2 * g + 2)
                for h in range(2):
                    o = mrow[:, 512 * h:512 * h + 512]
                    ins = stt(o, o, 1.0 if g == 2 else 0.0, bank(ROWBANKS[g + 2][h])[0:1, :], ALU.add, ALU.add)
                ins.then_inc(S("mrow_ready"), 1)
            for q, (idx, j, cp) in enumerate(ABJOBS):
                if idx % 2 == 1:
                    dve.wait_ge(S("ab_done"), q + 1)
                    dve.wait_ge(S("ab_act"), 2 * (idx // 2) + cp + 1)
                    lo, hi = EO[:, j - 4, 2 * cp:2 * cp + 2, :], EO[:, j, 2 * cp:2 * cp + 2, :]
                    pp = bank(1 + q % 3).rearrange("p (c n) -> p c n", c=2)
                    tt(hi, lo, pp, ALU.add)
                    tt(lo, lo, pp, ALU.subtract).then_inc(S("ab_dve"), 1)
            for c in range(4):
                bk = 0 if c % 2 else 4
                m = mixT[:, 4 + c, :]
                dve.wait_ge(S("qtmp_ready"), 2 * c + 1)
                tt(m[:, 0:513:2], bank(bk)[:, 0:NEV], qtmp[:, 0, 0:NEV], ALU.subtract)
                tt(m[:, 1022:512:-2], bank(bk)[:, 1:NEV - 1], qtmp[:, 0, 1:NEV - 1], ALU.add).then_inc(S("qtmp_used"), 1)
                dve.wait_ge(S("qtmp_ready"), 2 * c + 2)
                tt(m[:, 1:512:2], bank(bk + 2)[:, 0:NOD], qtmp[:, 1, 0:NOD], ALU.subtract)
                tt(m[:, 1023:512:-2], bank(bk + 2)[:, 0:NOD], qtmp[:, 1, 0:NOD], ALU.add).then_inc(S("qtmp_used"), 1)
            nq = 0
            for c in range(8):
                nq += 2 + (c >= 4)
                dve.wait_ge(S("cv_evac"), nq)
                if c >= 1:
                    dve.wait_ge(S("silu_done"), c)
                for tap in range(9):
                    src = cbuf[c % 2][:, tap // 3:tap // 3 + 16, tap % 3:tap % 3 + 64]
                    w = convw[:, 9 * c + tap:9 * c + tap + 1]
                    ins = ts(cacc, src, w, None, ALU.mult) if tap == 0 else stt(cacc, src, w, cacc, ALU.mult, ALU.add)
                    if tap < 8 or c >= 4:
                        link(ins)
                if c >= 4:
                    if c >= 5:
                        dve.wait_ge(S("siluc_done"), c - 4)
                    for tap in range(3):
                        src = cbufc[:, tap:tap + 256]
                        w = convw[:, 9 * c + 3 + tap:9 * c + 4 + tap]
                        ins = ts(caccc, src, w, None, ALU.mult) if tap == 0 else stt(caccc, src, w, caccc, ALU.mult, ALU.add)
                        if tap < 2:
                            link(ins)
                ins.then_inc(S("conv_done"), 1)
            link(dve.memset(G[:, :], 0.0))
            for t in range(NT):
                dve.wait_ge(S("g_done"), t + 1)
                src = bank(6 + t % 2)[:, 0:16].rearrange("p (d g h) -> p d g h", d=2, g=2)
                for d in range(2):
                    o = G[:, 32 * t + 16 * d:32 * t + 16 * d + 16].rearrange("p (g x) -> p g x", g=2)[:, :, 4 * d:4 * d + 4]
                    ins = dve.tensor_copy(o, src[:, d])
                ins.then_inc(S("g_evac"), 1)
            dve.wait_ge(S("silu_done"), 8)
            dve.wait_ge(S("siluc_done"), 4)
            for r, (s0, ns) in enumerate(((0, 4), (4, 4), (8, 2))):
                for gate in range(2):
                    q = 2 * r + gate
                    dve.wait_ge(S("rows_mm"), q + 1)
                    ts((Rf if gate else Ra)[:, P * s0:P * (s0 + ns)], bank(q % 4)[0:8, 0:P * ns], gateb[0:8, gate:gate + 1], None, ALU.add).then_inc(S("rows_evac"), 1)
            dve.wait_ge(S("rows_evac"), 6)
            link(dve.memset(mprev[0:8, 0:1], 0.0))
            link(dve.memset(zrow[0:8, :], 0.0))
            dve.wait_ge(S("rl_step"), 3)
            link(stt(Rl, Rf, 0.0, Rl, ALU.min, ALU.subtract))
            for s in range(NT):
                ins = dve.tensor_tensor_scan(Rb[:, P * s:P * s + P], Rl[:, P * s:P * s + P], zrow[0:8, :], 0.0, ALU.add, ALU.add)
            link(ins)
            link(tt(Ra, Ra, Rb, ALU.subtract))
            for s in range(NT):
                sl_ = slice(P * s, P * s + P)
                link(dve.tensor_tensor_scan(Rm[:, sl_], Ra[:, sl_], Ra[:, sl_], mprev[0:8, s:s + 1], ALU.max, ALU.max))
                link(tt(mprev[0:8, s + 1:s + 2], Rb[:, P * s + P - 1:P * s + P], Rm[:, P * s + P - 1:P * s + P], ALU.add))

            def v3(r):
                return r.rearrange("p (s n) -> p s n", s=NT)

            dve.wait_ge(S("v_done"), NT)
            dve.wait_ge(S("o_done"), NTX)
            dve.memset(stack[0:72].rearrange("p d n -> p (d n)"), 0.0).then_inc(S("wargs_ready"), 1)
            tt(v3(Rw), v3(Ra), v3(Rm)[:, :, P - 1:P].to_broadcast([8, NT, P]), ALU.subtract).then_inc(S("wargs_ready"), 1)
            stt(Re, Rb, -1.0, Rm, ALU.mult, ALU.subtract).then_inc(S("wargs_ready"), 1)
            tt(v3(Ri), mprev[0:8, 0:NT].unsqueeze(2).to_broadcast([8, NT, P]), v3(Rm), ALU.subtract).then_inc(S("wargs_ready"), 1)
            for i, c0 in enumerate((C_ID, C_MF, C_MB)):
                dve.tensor_copy(maskr[:, P * i:P * i + P], cst[:, c0:c0 + P])
            dve.wait_ge(S("wargs_ready"), 4)
            for d in range(2):
                dve.tensor_copy(v3(stack[0:8, d]), v3(Ra)[:, :, ::-1] if d else v3(Ra)).then_inc(S("rows_rev"), 1)
            link(ts(Rm, Rm, -1.0, None, ALU.mult))
            dve.wait_ge(S("rows_exp"), 5)
            tt(dgl[0:8, :].rearrange("p (s r) -> p s r", s=NT), cst[0:8, C_ID:C_ID + 8].unsqueeze(1).to_broadcast([8, NT, 8]),
               v3(Ri)[:, :, P - 1:P].to_broadcast([8, NT, 8]), ALU.mult).then_inc(S("rows_rev"), 1)
            dve.wait_ge(S("cols_mm"), 1)
            link(dve.tensor_copy(COL[:, :], bank(2)[:, 0:NT * 48]))
            link(dve.memset(Cst.rearrange("p b h n -> p (b h n)"), 0.0))
            dve.tensor_copy(DEC[:, :], bank(3)[:, 0:NT * 8]).then_inc(S("cols_ready"), 1)
            dve.wait_ge(S("cols_ready"), 1)

            def weigh(x):
                dve.wait_ge(S("D_ready"), x + 1)
                stt(Dt[:, x % 2], bank(x % 2), KSCALE, Dt[:, x % 2], ALU.mult, ALU.mult).then_inc(S("P_ready"), 1)

            def head_stats(n_):
                j, b = HTILES[n_], n_ % 2
                for h in range(4):
                    ins = dve.bn_stats(hst[:, 6 * h:6 * h + 6], H[:, j, P * h:P * h + P])
                link(ins)
                if n_ >= 2:
                    dve.wait_ge(S("hrstd_ready"), n_ - 1)
                for h in range(4):
                    ins = dve.bn_aggr(hmv[:, b, h], hst[:, 6 * h:6 * h + 6])
                ins.then_inc(S("hmv_ready"), 1)

            def gate(n_):
                j = HTILES[n_]
                dve.wait_ge(S("h_normed"), n_ + 1)
                dve.wait_ge(S("og_ready"), j + 1)
                tt(H[:, j], H[:, j], O[:, j], ALU.mult).then_inc(S("mix_ready"), 1)

            for q, (s, d, t) in enumerate(JOBS):
                x = q - FIRSTX
                if x >= 0:
                    c = t - NTC
                    dve.wait_ge(S("I_done"), x + 1)
                    if x >= 2:
                        dve.wait_ge(S("N_done"), x - 1)
                    tt(qI[:, x % 2].rearrange("p (h n) -> p h n", h=4), qkT[:, 0:4, P * c:P * c + P],
                       bank(6).rearrange("p (h n) -> p h n", h=4), ALU.mult).then_inc(S("qI_ready"), 1)
                if 0 <= x + 1 < 16:
                    weigh(x + 1)
                if x >= NTX + 1:
                    head_stats(x - NTX - 1)
                if x >= NTX + 3:
                    gate(x - NTX - 3)
                if x >= 0:
                    dve.wait_ge(S("N_done"), x + 1)
                dve.wait_ge(S("U_half"), 2 * q + 2)
                for half in (1, 0):
                    for i in range(2):
                        h = 2 * half + i
                        dc = DEC[:, 8 * s + 4 * d + h:8 * s + 4 * d + h + 1]
                        ins = stt(Cst[:, d, h], Cst[:, d, h], dc, bank(6 if half else 7)[:, 256 * i:256 * i + VW], ALU.mult, ALU.add)
                    ins.then_inc(S("C_half"), 1)
                if x >= 0:
                    num = psN.rearrange("p (b i n) -> p b i n", b=2, i=2)
                    den4 = den[:, :].rearrange("p (b i) -> p b i", b=2)
                    c0 = s * 48 + 32 + 12 * d
                    e4 = COL[:, c0:c0 + 4].rearrange("p (b i) -> p b i", b=2)
                    link(stt(den4, num[:, :, :, DH], -1.0, e4, ALU.mult, ALU.max))
                    link(tt(den4, num[:, :, :, DH], den4, ALU.max))
                    link(dve.reciprocal(rec[:, :], den[:, :]))
                    r4 = rec[:, :].rearrange("p (b i) -> p b i", b=2).unsqueeze(3).to_broadcast([P, 2, 2, DH])
                    tgt = H[:, c] if s - NTC < 4 else htmp
                    ins = tt(tgt.rearrange("p (b i n) -> p b i n", b=2, i=2), num[:, :, :, 0:DH], r4, ALU.mult)
                    ins.then_inc(S("h_read"), 1)
                    if s - NTC >= 4:
                        dve.wait_ge(S("h_read"), x + 1)
                        link(tt(H[:, c], H[:, c], htmp, ALU.add))
            head_stats(NTX - 1)
            for n_ in range(16 - NTX - 3, NTX):
                gate(n_)
            dve.wait_ge(S("rows1_in"), 80)
            dve.wait_ge(S("mixt_done"), NTX)
            for j in range(NTX + 1):
                if j < NTX:
                    y = ytmp[:, j % 2]
                    dve.wait_ge(S("proj_done"), j + 1)
                    tt(y, psN if j % 2 == 0 else psY, g1B, ALU.mult).then_inc(S("y_read"), 1)
                    dve.wait_ge(S("y_read"), j + 1)
                    dve.wait_ge(S(f"xres_in{j % 2}"), 16 * (j // 2 + 1))
                    stt(y, xres[:, j % 2], ALPHA, y, ALU.mult, ALU.add).then_inc(S("res_used"), 1)
                    dve.wait_ge(S("res_used"), j + 1)
                    moments(y, mvj[:, j % 2], "y_mv")
                    dve.wait_ge(S("y_rstd"), j + 1)
                    ts(y, y, mvj[:, j % 2, 0:1], rstd[:, j % 2:j % 2 + 1], ALU.subtract, ALU.mult).then_inc(S("y_norm"), 1)
                if j >= 1:
                    i = j - 1
                    dve.wait_ge(S("y_gain"), i + 1)
                    if i >= 2:
                        dve.wait_ge(S(f"x1_out{i % 2}"), 16 * (i // 2))
                    link(tt(x1[:, i % 2], ytmp[:, i % 2], lb1, ALU.add))
                    moments(x1[:, i % 2], mvk[:, i % 2], "x1_mv")
                    dve.wait_ge(S("x1_rstd"), i + 1)
                    if i >= 2:
                        dve.wait_ge(S(f"t_out{i % 2}"), 16 * (i // 2))
                        dve.wait_ge(S("tt_done"), i - 1)
                    link(stt(lnt[:, i % 2], x1[:, i % 2], mvk[:, i % 2, 0:1], sc2B, ALU.subtract, ALU.mult))
                    stt(lnt[:, i % 2], lnt[:, i % 2], rstd[:, 2 + i % 2:3 + i % 2], sh2B, ALU.mult, ALU.add).then_inc(S("ln_ready"), 1)
            def t3(x):
                return x.rearrange("p (j e) -> p j e", j=8)

            def shared(j):
                dve.wait_ge(S("s_sg"), j + 1)
                tt(hxL[:, j % 2], sgL[:, j % 2], bank(3 + j % 2)[:, DE:2 * DE], ALU.mult).then_inc(S("s_hx"), 1)

            shared(0)
            shared(1)
            dve.wait_ge(S("sc_ready"), 1)
            dve.wait_ge(S("ws_in"), 64)
            link(dve.memset(zr, 0.0))
            link(tt(t3(bs), t3(sc), rbB.unsqueeze(1).to_broadcast([P, 8, NE]), ALU.add))
            for j in range(8):
                link(dve.max(m8[:, 8 * j:8 * j + 8], bs[:, NE * j:NE * j + NE]))
                link(dve.match_replace(rp[:, NE * j:NE * j + NE], m8[:, 8 * j:8 * j + 8], bs[:, NE * j:NE * j + NE], -BIG))
                if j == 5:
                    shared(2)
            dve.wait_ge(S("tt_done"), NTX)
            for i in range(2):
                dve.wait_ge(S(f"t_out{i}"), 64)
            dve.tensor_copy(lt_r, cst[:, C_LT:C_LT + P])
            dve.tensor_copy(ones_r, ones)
            ts(mask_r[:, :], rp, -BIG, None, ALU.is_equal).then_inc(S("mask_ready"), 1)
            dve.wait_ge(S("mask_ready"), 1)
            link(tt(wt, sc, mask_r[:, :].bitcast(F32), ALU.mult))
            link(dve.tensor_reduce(ssum, t3(wt), AX, ALU.add))
            link(dve.reciprocal(ssum, ssum))
            link(ts(ssum, ssum, ROUTED, None, ALU.mult))
            tt(t3(wt), t3(wt), ssum.unsqueeze(2).to_broadcast([P, 8, NE]), ALU.mult).then_inc(S("wt_ready"), 1)
            shared(3)
            dve.wait_ge(S("pos_done"), 1)
            link(ts(cnti, bank(1)[:, 0:NE], float(P - 1), None, ALU.add))
            link(ts(cnti, cnti, 7, None, ALU.arith_shift_right))
            link(dve.tensor_copy(nbf, cnti))
            link(ts(nbf, nbf, 1.0, None, ALU.max))
            link(dve.tensor_tensor_scan(bend, nbf, zr, 0.0, ALU.add, ALU.add))
            link(tt(bbase, bend, nbf, ALU.subtract))
            link(ts(bbase, bbase, float(P), 1.0, ALU.mult, ALU.add))
            link(ts(n2, bend, cst[:, C_P:C_P + 1], None, ALU.is_le))
            link(dve.tensor_reduce(ebc, n2, AX, ALU.add))
            ts(ebc, ebc, float(NE - 1), None, ALU.min).then_inc(S("eb_ready"), 1)
            link(tt(t3(sl), t3(bank(0)), bbase.unsqueeze(1).to_broadcast([P, 8, NE]), ALU.add))
            link(tt(sl, sl, mask_r[:, :].bitcast(F32), ALU.mult))
            for j in range(8):
                ins = dve.max(m8[:, 8 * j:8 * j + 8], sl[:, NE * j:NE * j + NE])
            link(ins)
            link(ts(s8i, m8, -1.0, None, ALU.add))
            link(ts(b8i, s8i, 7, None, ALU.arith_shift_right))
            link(ts(s8i, s8i, P - 1, None, ALU.bitwise_and))
            link(dve.tensor_copy(b8, b8i))
            dve.tensor_copy(p8, s8i).then_inc(S("slots_ready"), 1)
            shared(4)
            for q in range(64):
                j, k = q // 8, q % 8
                if q in (16, 40):
                    shared(5 if q == 16 else 6)
                if q >= NOH:
                    dve.wait_ge(S("onehot_used"), q - NOH + 1)
                ts(oneB[:, q % NOH], iota, b8[:, q:q + 1], cst[:, C_TOK + j:C_TOK + j + 1], ALU.is_equal, ALU.mult).then_inc(S("onehot_ready"), 1)
            shared(7)
            link(ts(pairs_rest[:, :], bend[0:1, NE - 1:NE], 1.0, None, ALU.add))
            link(ts(pairs_rest[:, :], pairs_rest[:, :], 1, None, ALU.arith_shift_right))
            link(ts(pairs_rest[:, :], pairs_rest[:, :], -1.0, None, ALU.add))
            dve.wait_ge(S("eb_mm"), 1)

            def trow(r):
                return tbl[:, r:r + P]

            link(dve.tensor_copy(trow(T_E), bank(1)[0:1, 0:P]))

            link(tt(trow(T_NEW)[:, 1:P], trow(T_E)[:, 1:P], trow(T_E)[:, 0:P - 1], ALU.not_equal))
            link(dve.memset(trow(T_NEW)[:, 0:1], 1))
            link(ts(tblf[:, :], trow(T_E), float(NE - 1), None, ALU.is_lt))
            link(tt(trow(T_NEW), trow(T_NEW), tblf[:, :], ALU.mult))
            link(stt(trow(T_WORD), trow(T_NEW), 64.0, trow(T_E), ALU.mult, ALU.add))
            link(dve.memset(tbl[:, P:P + 2], 0))
            dve.wait_ge(S("onehot_used"), 64)
            pad = cst[:, C_PADROW:C_PADROW + 1]
            link(ts(Ttmp[:, 0], bank(2)[:, 0:P], 0.0, pad, ALU.is_equal, ALU.mult))
            link(tt(Ttmp[:, 1], bank(2)[:, 0:P], Ttmp[:, 0], ALU.add))
            link(ts(idxT[:, 0:P], Ttmp[:, 1], -1.0, None, ALU.add))
            ts(idxT[:, P:P + 2], cst[:, C_PADROW:C_PADROW + 1].to_broadcast([P, 2]), -1.0, None, ALU.add).then_inc(S("idx_ready"), 1)
            dve.wait_ge(S("idx_ready"), 1)
            dve.sem_inc(S("table_ready"), 1)
            def word(b):
                return word_of(dve, b)

            def x_low(b, p, w):
                dve.wait_ge(S("m_xh"), b + 1)
                dve.tensor_copy(gcol[:, p:p + 1], xg[:, p, D:XW][:, bass.ds(w & 63, 1)])
                tt(xTl[p], psum[:, 0:1024], xTh[p].bitcast(F32), ALU.subtract).then_inc(S("m_xb"), 1)

            def h_low(b):
                dve.wait_ge(S("m_hh"), b + 1)
                tt(hTl, bank(7)[:, 0:2 * P], hTh.bitcast(F32), ALU.subtract).then_inc(S("m_hT"), 1)

            def w_low(e, par, chunks):
                for c in chunks:
                    dve.wait_ge(S("hi_split"), 6 * e + (c + 1))
                    high = cols(wsplit, (1 - par) * (2 * WE) + 1024 * c, 1024).bitcast(F32)
                    tt(cols(wsplit, (1 - par) * (2 * WE) + (WE + 1024 * c), 1024), cols(raw, (1 - par) * WE + 1024 * c, 1024), high,
                       ALU.subtract).then_inc(S("lo_split"), 1)

            def h_rows(b, p):
                dve.wait_ge(S("m_xb"), b + 1)
                dve.wait_ge(S("m_sg"), b + 1)
                stt(hx[:, p], bank(3 + p)[:, DE:2 * DE], gcol[:, p:p + 1], sg[:, p], ALU.mult, ALU.mult).then_inc(S("m_hx"), 1)

            w_low(0, 0, range(6))
            x_low(0, 0, word(0))
            x_low(1, 1, word(1))
            w_low(1, 1, range(4))
            h_rows(0, 0)

            def step(b, p, w0, w1, w2):
                h_low(b - 1)
                x_low(b + 1, 1 - p, w2)
                if w0 is None:
                    w_low(1, 1, range(4, 6))
                else:
                    with dve.If_ne(dve.to_reg((w0 >> 6) & 1), 0):
                        w_low((w0 & 63) + 1, 1 - (w0 & 1), range(4, 6))
                first, e1, par1 = (w1 >> 6) & 1, (w1 & 63) + 1, 1 - (w1 & 1)
                with dve.If_ne(dve.to_reg(first), 0):
                    w_low(e1, par1, range(2))
                h_rows(b, p)
                with dve.If_ne(dve.to_reg(first), 0):
                    w_low(e1, par1, range(2, 4))

            step(1, 1, None, word(1), word(2))
            rest = dve.value_load(pairs_rest[0:1, 0:1], min_val=NE // 2 - 1, max_val=MAXB // 2 - 1)
            with dve.Fori(0, rest) as i:
                w0, w1, w2 = word(2 * i + 1), word(2 * i + 2), word(2 * i + 3)
                step(2 * i + 2, 0, w0, w1, w2)
                w3 = word(2 * i + 4)
                step(2 * i + 3, 1, w1, w2, w3)
            h_low(2 * rest + 1)
            dve.wait_ge(S("rows2_in"), 48 + 16 * NTX)
            for j in range(NTX + 2):
                if j < NTX:
                    y = acc_in[j]
                    dve.wait_ge(S(f"accin{j // 4}"), 64)
                    if j in POOL_GAINS:
                        dve.wait_ge(S("og_ready"), NTX + POOL_GAINS.index(j) + 1)
                    else:
                        link(tt(y, y, g2B, ALU.mult))
                    link(stt(y, x1_in[j], ALPHA, y, ALU.mult, ALU.add))
                    moments(y, mv[:, 2 * j:2 * j + 2], "y_mv", hst[:, 8:20] if j % 2 else stats)
                if j >= 2:
                    dve.wait_ge(S("y_gain"), NTX + j - 1)
                    tt(acc_in[j - 2], acc_in[j - 2], lb2, ALU.add).then_inc(S("out_ready"), 1)


def kernel(**inputs):
    import concourse.bacc as bacc
    from concourse.bass_utils import run_bass_kernel_spmd

    def flat(name):
        return np.asarray(inputs[name])

    const, dft = constant_tiles()
    w_in = flat("w_in")[0]
    cc = np.stack([flat("c")[0], flat("c_ctx")], axis=-1).reshape(P, 16)
    gate_b = flat("gate_b")[0]
    arrays = {
        "toks": np.concatenate([flat("ctx")[0], flat("x")[0]], axis=0),
        "cc": cc,
        "const": const,
        "dft": dft,
        "w_ada": flat("w_ada")[0],
        "b_ada": flat("b_ada"),
        "w_qk": w_in[:, 0:2 * DM],
        "w_vog": w_in[:, 2 * DM:4 * DM + 16],
        "w_f": w_in[:, 4 * DM + 16:],
        "conv_wt": flat("conv_w")[0].reshape(9, 8, P).transpose(2, 1, 0).reshape(P, 72),
        "conv_bt": flat("conv_b")[0].reshape(8, P).T,
        "gate_bt": gate_b.transpose(0, 2, 1).reshape(8, 2),
        "head_g": flat("head_g"),
        "w_out": flat("w_out")[0],
        "ln1_g": flat("ln1_g"), "ln1_b": flat("ln1_b"), "ln2_g": flat("ln2_g"), "ln2_b": flat("ln2_b"),
        "w_router": flat("w_router")[0],
        "router_bias": flat("router_bias"),
        "w_gu": flat("w_expert_gu")[0].reshape(NE * P, 8 * 2 * DE),
        "w_dn": flat("w_expert_down")[0].reshape(NE * P, 2 * D),
        "w_shared_gu": flat("w_shared_gu")[0],
        "w_shared_down": flat("w_shared_down")[0],
    }
    nc = bacc.Bacc("TRN2", target_bir_lowering=False, num_devices=1)
    feed, aps = {}, {}
    for name, v in arrays.items():
        v = np.ascontiguousarray(v)
        feed[f"in_{name}"] = v
        aps[name] = nc.dram_tensor(f"in_{name}", v.shape, F32, kind="ExternalInput").ap()
    out = nc.dram_tensor("out_0", (SEQ, D), F32, kind="ExternalOutput").ap()
    build(nc, aps, out)
    r = run_bass_kernel_spmd(nc, [feed], core_ids=[0])
    return r.results[0]["out_0"].reshape(1, SEQ, D)
```
